# Optimizing a Trainium2 kernel written in Bass

```python
import math
import jax, jax.numpy as jnp
from jax import lax
import numpy as np
import jax
import jax.numpy as jnp

D_MODEL = 2048
BATCH = 1
SEQ = 256
DEPTH = 2

N_MIXERS = 2
N_LAYERS_A = (DEPTH + 1) // 2
N_LAYERS_B = DEPTH // 2

DSA_PATTERNS = ((128, 1), (512, 4), (2048, 16))
DSA_GROUPS = len(DSA_PATTERNS)
DSA_HEADS = 16
DSA_HEAD_DIM = 128
DSA_WIDTH = DSA_HEADS * DSA_HEAD_DIM
DSA_BLOCK = 128
DSA_IN = 3 * DSA_GROUPS * DSA_WIDTH + DSA_WIDTH

MLA_HEADS = 16
MLA_Q_RANK = 512
MLA_KV_RANK = 512
MLA_NOPE = 128
MLA_ROPE = 64
MLA_V = 128
MLA_WIDTH = MLA_HEADS * MLA_V
MLA_IN = MLA_Q_RANK + MLA_KV_RANK + MLA_ROPE + MLA_WIDTH
MLA_QBLOCK = 128

ROPE_THETA = 10000.0
RMS_EPS = 1e-6
LN_EPS = 1e-5
DEEPNORM_ALPHA = (2 * DEPTH) ** 0.25
DEEPNORM_BETA = (8 * DEPTH) ** -0.25


def rope_tables(positions, dim):
    inv = 1.0 / (ROPE_THETA ** (jnp.arange(0, dim, 2, dtype=jnp.float32) / dim))
    ang = positions.astype(jnp.float32)[..., None] * inv
    return jnp.cos(ang), jnp.sin(ang)

def apply_rope(x, cos, sin):
    xf = x.astype(jnp.float32)
    x1, x2 = jnp.split(xf, 2, axis=-1)
    c = cos[:, :, None, :]
    s = sin[:, :, None, :]
    return jnp.concatenate([x1 * c - x2 * s, x2 * c + x1 * s], axis=-1).astype(x.dtype)

def rms_norm(x, g):
    xf = x.astype(jnp.float32)
    y = xf * lax.rsqrt(jnp.mean(xf * xf, axis=-1, keepdims=True) + RMS_EPS)
    return (y * g.astype(jnp.float32)).astype(x.dtype)

def layer_norm(x, g, b):
    xf = x.astype(jnp.float32)
    mu = jnp.mean(xf, axis=-1, keepdims=True)
    xc = xf - mu
    var = jnp.mean(xc * xc, axis=-1, keepdims=True)
    y = xc * lax.rsqrt(var + LN_EPS) * g.astype(jnp.float32) + b.astype(jnp.float32)
    return y.astype(x.dtype)

def dilated_window_attention(q, k, v, window, dilation):
    B, S, H, Dh = q.shape
    span = window // dilation
    assert span <= DSA_BLOCK
    L = S // dilation
    nb = -(-L // DSA_BLOCK)
    Lp = nb * DSA_BLOCK
    N = B * dilation

    def to_sub(t):
        t = t.reshape(B, L, dilation, H, Dh).transpose(0, 2, 1, 3, 4).reshape(N, L, H, Dh)
        t = jnp.pad(t, ((0, 0), (0, Lp - L), (0, 0), (0, 0)))
        return t.reshape(N, nb, DSA_BLOCK, H, Dh)

    def with_prev(t):
        prev = jnp.pad(t, ((0, 0), (1, 0), (0, 0), (0, 0), (0, 0)))[:, :-1]
        return jnp.concatenate([prev, t], axis=2)

    qb = to_sub(q)
    kk = with_prev(to_sub(k))
    vv = with_prev(to_sub(v))
    scores = jnp.einsum('nbqhd,nbkhd->nbhqk', qb, kk).astype(jnp.float32) * (Dh ** -0.5)
    qi = jnp.arange(nb)[:, None, None] * DSA_BLOCK + jnp.arange(DSA_BLOCK)[None, :, None]
    kj = (jnp.arange(nb)[:, None, None] - 1) * DSA_BLOCK + jnp.arange(2 * DSA_BLOCK)[None, None, :]
    dist = qi - kj
    mask = (dist >= 0) & (dist <= span) & (kj >= 0)
    scores = jnp.where(mask[None, :, None], scores, -jnp.inf)
    lse = jax.nn.logsumexp(scores, axis=-1)
    p = jnp.exp(scores - lse[..., None])
    out = jnp.einsum('nbhqk,nbkhd->nbqhd', p.astype(v.dtype), vv)
    out = out.reshape(B, dilation, Lp, H, Dh)[:, :, :L].transpose(0, 2, 1, 3, 4).reshape(B, S, H, Dh)
    lse = lse.transpose(0, 1, 3, 2).reshape(B, dilation, Lp, H)[:, :, :L]
    lse = lse.transpose(0, 2, 1, 3).reshape(B, S, H)
    return out, lse

def dilated_mixer(x, w_in, w_out, cos, sin):
    B, S, _ = x.shape
    h = x @ w_in
    qkv = h[..., :3 * DSA_GROUPS * DSA_WIDTH].reshape(B, S, DSA_GROUPS, 3, DSA_HEADS, DSA_HEAD_DIM)
    z = h[..., 3 * DSA_GROUPS * DSA_WIDTH:]
    outs = []
    lses = []
    for g, (window, dilation) in enumerate(DSA_PATTERNS):
        q = apply_rope(qkv[:, :, g, 0], cos, sin)
        k = apply_rope(qkv[:, :, g, 1], cos, sin)
        o, l = dilated_window_attention(q, k, qkv[:, :, g, 2], window, dilation)
        outs.append(o)
        lses.append(l)
    wts = jax.nn.softmax(jnp.stack(lses, axis=0), axis=0)
    o = jnp.einsum('gbsh,gbshd->bshd', wts, jnp.stack(outs, axis=0).astype(jnp.float32))
    y = o.reshape(B, S, DSA_WIDTH).astype(x.dtype) * jax.nn.silu(z)
    return y @ w_out

def causal_mla_attention(q_nope, q_pe, k_nope, k_pe, v):
    B, S, H, _ = q_nope.shape
    nq = S // MLA_QBLOCK
    scale = (MLA_NOPE + MLA_ROPE) ** -0.5
    qn = q_nope.reshape(B, nq, MLA_QBLOCK, H, MLA_NOPE).transpose(1, 0, 2, 3, 4)
    qp = q_pe.reshape(B, nq, MLA_QBLOCK, H, MLA_ROPE).transpose(1, 0, 2, 3, 4)
    kpos = jnp.arange(S)

    def one_block(args):
        i, qn_i, qp_i = args
        s = (jnp.einsum('bqhd,bkhd->bhqk', qn_i, k_nope).astype(jnp.float32)
             + jnp.einsum('bqhr,bkr->bhqk', qp_i, k_pe).astype(jnp.float32)) * scale
        qpos = i * MLA_QBLOCK + jnp.arange(MLA_QBLOCK)
        s = jnp.where(kpos[None, :] <= qpos[:, None], s, -jnp.inf)
        p = jax.nn.softmax(s, axis=-1)
        return jnp.einsum('bhqk,bkhd->bqhd', p.astype(v.dtype), v)

    o = lax.map(one_block, (jnp.arange(nq), qn, qp))
    return o.transpose(1, 0, 2, 3, 4).reshape(B, S, H, MLA_V)

def mla_mixer(x, w_in, q_norm, w_uq, kv_norm, w_ukv, w_out, cos, sin):
    B, S, _ = x.shape
    h = x @ w_in
    o1 = MLA_Q_RANK
    o2 = o1 + MLA_KV_RANK
    o3 = o2 + MLA_ROPE
    c_q = h[..., :o1]
    c_kv = h[..., o1:o2]
    k_pe = h[..., o2:o3]
    z = h[..., o3:]
    q = (rms_norm(c_q, q_norm) @ w_uq).reshape(B, S, MLA_HEADS, MLA_NOPE + MLA_ROPE)
    q_nope = q[..., :MLA_NOPE]
    q_pe = apply_rope(q[..., MLA_NOPE:], cos, sin)
    k_pe = apply_rope(k_pe[:, :, None, :], cos, sin)[:, :, 0]
    kv = (rms_norm(c_kv, kv_norm) @ w_ukv).reshape(B, S, MLA_HEADS, MLA_NOPE + MLA_V)
    k_nope = kv[..., :MLA_NOPE]
    v = kv[..., MLA_NOPE:]
    o = causal_mla_attention(q_nope, q_pe, k_nope, k_pe, v)
    y = o.reshape(B, S, MLA_WIDTH) * jax.nn.silu(z)
    return y @ w_out

def first_inputs(seed: int = 0) -> dict:
    key = jax.random.key(seed)
    ks = jax.random.split(key, 12)
    f32 = jnp.float32
    x = jax.random.normal(ks[0], (BATCH, SEQ, D_MODEL), f32)
    start = jax.random.randint(ks[1], (BATCH, 1), 0, 4096, dtype=jnp.int32)
    positions = (start + jnp.arange(SEQ, dtype=jnp.int32)[None, :]).astype(jnp.int32)
    dsa_w_in = jax.random.normal(ks[2], (N_LAYERS_A, D_MODEL, DSA_IN), f32) * D_MODEL ** -0.5
    dsa_w_out = jax.random.normal(ks[3], (N_LAYERS_A, DSA_WIDTH, D_MODEL), f32) * (DSA_WIDTH ** -0.5 * DEEPNORM_BETA)
    mla_w_in = jax.random.normal(ks[4], (N_LAYERS_B, D_MODEL, MLA_IN), f32) * D_MODEL ** -0.5
    mla_q_norm = 1.0 + 0.01 * jax.random.normal(ks[5], (N_LAYERS_B, MLA_Q_RANK), f32)
    mla_w_uq = jax.random.normal(ks[6], (N_LAYERS_B, MLA_Q_RANK, MLA_HEADS * (MLA_NOPE + MLA_ROPE)), f32) * MLA_Q_RANK ** -0.5
    mla_kv_norm = 1.0 + 0.01 * jax.random.normal(ks[7], (N_LAYERS_B, MLA_KV_RANK), f32)
    mla_w_ukv = jax.random.normal(ks[8], (N_LAYERS_B, MLA_KV_RANK, MLA_HEADS * (MLA_NOPE + MLA_V)), f32) * MLA_KV_RANK ** -0.5
    mla_w_out = jax.random.normal(ks[9], (N_LAYERS_B, MLA_WIDTH, D_MODEL), f32) * (MLA_WIDTH ** -0.5 * DEEPNORM_BETA)
    ln_g = 1.0 + 0.01 * jax.random.normal(ks[10], (DEPTH, D_MODEL), f32)
    ln_b = 0.01 * jax.random.normal(ks[11], (DEPTH, D_MODEL), f32)
    return {"x": x, "positions": positions, "dsa_w_in": dsa_w_in, "dsa_w_out": dsa_w_out,
            "mla_w_in": mla_w_in, "mla_q_norm": mla_q_norm, "mla_w_uq": mla_w_uq,
            "mla_kv_norm": mla_kv_norm, "mla_w_ukv": mla_w_ukv, "mla_w_out": mla_w_out,
            "ln_g": ln_g, "ln_b": ln_b}

def first_block(x, positions, dsa_w_in, dsa_w_out, mla_w_in, mla_q_norm, mla_w_uq,
              mla_kv_norm, mla_w_ukv, mla_w_out, ln_g, ln_b):
    cos_a, sin_a = rope_tables(positions, DSA_HEAD_DIM)
    cos_b, sin_b = rope_tables(positions, MLA_ROPE)
    for layer in range(DEPTH):
        j = layer // N_MIXERS
        if layer % N_MIXERS == 0:
            y = dilated_mixer(x, dsa_w_in[j], dsa_w_out[j], cos_a, sin_a)
        else:
            y = mla_mixer(x, mla_w_in[j], mla_q_norm[j], mla_w_uq[j], mla_kv_norm[j],
                          mla_w_ukv[j], mla_w_out[j], cos_b, sin_b)
        x = layer_norm(DEEPNORM_ALPHA * x + y, ln_g[layer], ln_b[layer])
    return x


CHUNK = 64
EPS = 1e-6
NEG = -1e30
CONV_K = 4

HD_A = 128
W_A = D_MODEL // 2
H_A = W_A // HD_A
LOOKBACK = 8
BAND = (LOOKBACK + 1) * CHUNK
REL_MAX = 256
H_B = 4
W_B = D_MODEL // 2
HD_B = W_B // H_B
FORGET_BIAS = 3.0
W_C = D_MODEL // 2
N_BLK_C = 8
BLK_C = W_C // N_BLK_C
C_RG = 8.0
HD_D = 128
W_D = D_MODEL // 2
H_D = W_D // HD_D

EV_SIZES = (W_A, W_A, W_A, W_A, W_B, W_B, W_B, W_B, W_B, 2 * H_B)
OD_SIZES = (W_C, W_C, W_D, W_D, W_D, W_D, H_D, H_D)
EV_IN = sum(EV_SIZES)
OD_IN = sum(OD_SIZES)
W_EV = W_A + W_B
W_OD = W_C + W_D
N_EVEN = (DEPTH + 1) // 2
N_ODD = DEPTH // 2


def split_cols(t, sizes):
    offs = np.cumsum(sizes)[:-1].tolist()
    return jnp.split(t, offs, axis=-1)

def rmsnorm(x, g):
    xf = x.astype(jnp.float32)
    y = xf * lax.rsqrt(jnp.mean(xf * xf, axis=-1, keepdims=True) + EPS)
    return (y * g.astype(jnp.float32)).astype(x.dtype)

def l2norm(x):
    return x * lax.rsqrt(jnp.sum(x * x, axis=-1, keepdims=True) + EPS)

def causal_dwconv(x, w):
    s = x.shape[1]
    xp = jnp.pad(x, ((0, 0), (CONV_K - 1, 0), (0, 0)))
    return sum(xp[:, j:j + s] * w[j] for j in range(CONV_K))

def to_chunks(t):
    b, s, h = t.shape[:3]
    t = t.reshape(b, s // CHUNK, CHUNK, h, *t.shape[3:])
    return jnp.moveaxis(t, (1, 3), (0, 2))

def from_chunks(t):
    nc, b, h, l, d = t.shape
    return jnp.moveaxis(t, (0, 2), (1, 3)).reshape(b, nc * l, h * d)

def chunk_rel_attention(q, k, v, qn_g, kn_g, rel_bias):
    b, s, h, d = q.shape
    nc = s // CHUNK
    q = rmsnorm(q, qn_g).astype(jnp.float32) * (d ** -0.5)
    k = rmsnorm(k, kn_g).astype(jnp.float32)
    v = v.astype(jnp.float32)
    qc = q.reshape(b, nc, CHUNK, h, d)
    pad = ((0, 0), (LOOKBACK, 0), (0, 0), (0, 0), (0, 0))
    kp = jnp.pad(k.reshape(b, nc, CHUNK, h, d), pad)
    vp = jnp.pad(v.reshape(b, nc, CHUNK, h, d), pad)
    idx = jnp.arange(nc)[:, None] + jnp.arange(LOOKBACK + 1)[None, :]
    kb = kp[:, idx].reshape(b, nc, BAND, h, d)
    vb = vp[:, idx].reshape(b, nc, BAND, h, d)
    sc = jnp.einsum('bnqhd,bnkhd->bhnqk', qc, kb)
    qpos = LOOKBACK * CHUNK + jnp.arange(CHUNK)
    kpos = jnp.arange(BAND)
    rel = jnp.clip(qpos[:, None] - kpos[None, :], -REL_MAX, REL_MAX) + REL_MAX
    sc = sc + rel_bias.astype(jnp.float32)[:, rel][None, :, None]
    valid = (idx - LOOKBACK) >= 0
    valid = jnp.repeat(valid, CHUNK, axis=1)
    sc = jnp.where(valid[None, None, :, None, :], sc, NEG)
    p = jax.nn.softmax(sc, axis=-1)
    o = jnp.einsum('bhnqk,bnkhd->bnqhd', p, vb)
    return o.reshape(b, s, h * d)

def mlstm_chunkwise(q, k, v, li, lf):
    b, s, h, d = q.shape
    q = q * (d ** -0.5)
    qc, kc, vc = to_chunks(q), to_chunks(k), to_chunks(v)
    lic, lfc = to_chunks(li), to_chunks(lf)
    tril = jnp.tril(jnp.ones((CHUNK, CHUNK), dtype=bool))

    def step(carry, inp):
        cm, nm, m = carry
        qn, kn, vn, lin, lfn = inp
        bcum = jnp.cumsum(lfn, axis=-1)
        dmat = bcum[..., :, None] - bcum[..., None, :] + lin[..., None, :]
        dmat = jnp.where(tril, dmat, NEG)
        m_t = jnp.maximum(bcum + m[..., None], jnp.max(dmat, axis=-1))
        w_inter = jnp.exp(bcum + m[..., None] - m_t)
        p = jnp.exp(dmat - m_t[..., None]) * jnp.einsum('bhtd,bhsd->bhts', qn, kn)
        num = w_inter[..., None] * jnp.einsum('bhtk,bhkv->bhtv', qn, cm) + jnp.einsum('bhts,bhsv->bhtv', p, vn)
        den = w_inter * jnp.einsum('bhtk,bhk->bht', qn, nm) + jnp.sum(p, axis=-1)
        hout = num / jnp.maximum(jnp.abs(den), jnp.exp(-m_t))[..., None]
        b_last = bcum[..., -1]
        gs = b_last[..., None] - bcum + lin
        m_new = jnp.maximum(b_last + m, jnp.max(gs, axis=-1))
        w_c = jnp.exp(b_last + m - m_new)
        ws = jnp.exp(gs - m_new[..., None])
        cm = w_c[..., None, None] * cm + jnp.einsum('bhs,bhsk,bhsv->bhkv', ws, kn, vn)
        nm = w_c[..., None] * nm + jnp.einsum('bhs,bhsk->bhk', ws, kn)
        return (cm, nm, m_new), hout

    init = (jnp.zeros((b, h, d, d), jnp.float32), jnp.zeros((b, h, d), jnp.float32), jnp.zeros((b, h), jnp.float32))
    _, hs = lax.scan(step, init, (qc, kc, vc, lic, lfc))
    return from_chunks(hs)

def gated_delta_chunkwise(q, k, v, beta, g):
    b, s, h, d = q.shape
    qc = to_chunks(q) * (d ** -0.5)
    kc, vc = to_chunks(k), to_chunks(v)
    bc, gc = to_chunks(beta), to_chunks(g)
    tril = jnp.tril(jnp.ones((CHUNK, CHUNK), dtype=bool))
    strict = jnp.tril(jnp.ones((CHUNK, CHUNK), dtype=bool), k=-1)
    decay = jnp.cumsum(gc, axis=-1)
    gam = jnp.exp(jnp.where(tril, decay[..., :, None] - decay[..., None, :], NEG))
    kbeta = kc * bc[..., None]
    a_mat = jnp.where(strict, jnp.einsum('nbhtd,nbhsd->nbhts', kbeta, kc) * gam, 0.0)
    eye = jnp.eye(CHUNK, dtype=jnp.float32)
    t_inv = lax.linalg.triangular_solve(eye + a_mat, jnp.broadcast_to(eye, a_mat.shape), left_side=True, lower=True, unit_diagonal=True)
    u = jnp.einsum('nbhts,nbhsv->nbhtv', t_inv, vc * bc[..., None])
    w = jnp.einsum('nbhts,nbhsk->nbhtk', t_inv, kbeta * jnp.exp(decay)[..., None])
    qd = qc * jnp.exp(decay)[..., None]
    qk = jnp.einsum('nbhtd,nbhsd->nbhts', qc, kc) * gam
    kd = kc * jnp.exp(decay[..., -1:] - decay)[..., None]
    d_last = jnp.exp(decay[..., -1])

    def step(st, inp):
        un, wn, qdn, qkn, kdn, dln = inp
        v_new = un - jnp.einsum('bhtk,bhkv->bhtv', wn, st)
        o = jnp.einsum('bhtk,bhkv->bhtv', qdn, st) + jnp.einsum('bhts,bhsv->bhtv', qkn, v_new)
        st = dln[..., None, None] * st + jnp.einsum('bhsk,bhsv->bhkv', kdn, v_new)
        return st, o

    init = jnp.zeros((b, h, d, d), jnp.float32)
    _, os_ = lax.scan(step, init, (u, w, qd, qk, kd, d_last))
    return jnp.moveaxis(os_, (0, 2), (1, 3)).reshape(b, s, h, d)

def rg_lru(xconv, gate_w, gate_b, lam):
    b, s, _ = xconv.shape
    gates = jnp.einsum('bsnc,ncd->bsnd', xconv.reshape(b, s, N_BLK_C, BLK_C), gate_w.astype(jnp.float32))
    gb = gate_b.astype(jnp.float32)
    r = jax.nn.sigmoid(gates[..., :BLK_C].reshape(b, s, W_C) + gb[:W_C])
    i = jax.nn.sigmoid(gates[..., BLK_C:].reshape(b, s, W_C) + gb[W_C:])
    log_a = -C_RG * r * jax.nn.softplus(-lam.astype(jnp.float32))
    a = jnp.exp(log_a)
    inp = jnp.sqrt(-jnp.expm1(2.0 * log_a)) * (i * xconv)

    def combine(e1, e2):
        a1, b1 = e1
        a2, b2 = e2
        return a1 * a2, a2 * b1 + b2

    _, hs = lax.associative_scan(combine, (a, inp), axis=1)
    return hs

def even_layer(x, norm_g, w_in, if_bias, qn_g, kn_g, rel_bias, w_out):
    b, s, _ = x.shape
    proj = rmsnorm(x, norm_g) @ w_in
    qa, ka, va, za, qb, kb, vb, ob, zb, gif = split_cols(proj, EV_SIZES)
    ya = chunk_rel_attention(qa.reshape(b, s, H_A, HD_A), ka.reshape(b, s, H_A, HD_A), va.reshape(b, s, H_A, HD_A), qn_g, kn_g, rel_bias)
    ya = ya * jax.nn.silu(za.astype(jnp.float32))
    gif = gif.astype(jnp.float32) + if_bias.astype(jnp.float32)
    li = gif[..., :H_B]
    lf = jax.nn.log_sigmoid(gif[..., H_B:])
    f32 = jnp.float32
    hb = mlstm_chunkwise(qb.astype(f32).reshape(b, s, H_B, HD_B), kb.astype(f32).reshape(b, s, H_B, HD_B), vb.astype(f32).reshape(b, s, H_B, HD_B), li, lf)
    yb = jax.nn.sigmoid(ob.astype(f32)) * hb * jax.nn.silu(zb.astype(f32))
    y = jnp.concatenate([ya, yb], axis=-1).astype(x.dtype)
    return y @ w_out

def odd_layer(x, norm_g, w_in, conv_c_w, conv_c_b, gate_w, gate_b, lam, conv_d_w, a_log, dt_bias, onorm_g, w_out):
    b, s, _ = x.shape
    f32 = jnp.float32
    proj = rmsnorm(x, norm_g) @ w_in
    xc, zc, qd, kd, vd, zd, a_pre, b_pre = split_cols(proj, OD_SIZES)
    xconv = causal_dwconv(xc.astype(f32), conv_c_w.astype(f32)) + conv_c_b.astype(f32)
    yc = rg_lru(xconv, gate_w, gate_b, lam) * jax.nn.silu(zc.astype(f32))
    qkv = jax.nn.silu(causal_dwconv(jnp.concatenate([qd, kd, vd], axis=-1).astype(f32), conv_d_w.astype(f32)))
    q, k, v = jnp.split(qkv, 3, axis=-1)
    q = l2norm(q.reshape(b, s, H_D, HD_D))
    k = l2norm(k.reshape(b, s, H_D, HD_D))
    v = v.reshape(b, s, H_D, HD_D)
    beta = jax.nn.sigmoid(b_pre.astype(f32))
    g = -jnp.exp(a_log.astype(f32)) * jax.nn.softplus(a_pre.astype(f32) + dt_bias.astype(f32))
    od = gated_delta_chunkwise(q, k, v, beta, g)
    yd = rmsnorm(od, onorm_g).reshape(b, s, W_D) * jax.nn.silu(zd.astype(f32))
    y = jnp.concatenate([yc, yd], axis=-1).astype(x.dtype)
    return y @ w_out

def second_inputs(seed: int = 0) -> dict:
    key = jax.random.key(seed)
    ks = jax.random.split(key, 24)
    f32 = jnp.float32
    ne, no = N_EVEN, N_ODD

    def nrm(k, shape, scale):
        return scale * jax.random.normal(k, shape, f32)

    x = nrm(ks[0], (BATCH, SEQ, D_MODEL), 1.0)
    ev_norm = 1.0 + nrm(ks[1], (ne, D_MODEL), 0.05)
    ev_w_in = nrm(ks[2], (ne, D_MODEL, EV_IN), D_MODEL ** -0.5)
    ev_if_bias = jnp.concatenate([nrm(ks[3], (ne, H_B), 0.1), FORGET_BIAS + nrm(ks[4], (ne, H_B), 0.5)], axis=-1)
    ev_qn_gain = 1.0 + nrm(ks[5], (ne, HD_A), 0.05)
    ev_kn_gain = 1.0 + nrm(ks[6], (ne, HD_A), 0.05)
    ev_rel_bias = nrm(ks[7], (ne, H_A, 2 * REL_MAX + 1), 0.2)
    ev_w_out = nrm(ks[8], (ne, W_EV, D_MODEL), W_EV ** -0.5)
    od_norm = 1.0 + nrm(ks[9], (no, D_MODEL), 0.05)
    od_w_in = nrm(ks[10], (no, D_MODEL, OD_IN), D_MODEL ** -0.5)
    od_conv_c_w = nrm(ks[11], (no, CONV_K, W_C), CONV_K ** -0.5)
    od_conv_c_b = nrm(ks[12], (no, W_C), 0.01)
    od_gate_w = nrm(ks[13], (no, N_BLK_C, BLK_C, 2 * BLK_C), BLK_C ** -0.5)
    od_gate_b = nrm(ks[14], (no, 2 * W_C), 0.1)
    a0 = jax.random.uniform(ks[15], (no, W_C), f32, minval=0.9, maxval=0.999)
    sig = a0 ** (1.0 / C_RG)
    od_lambda = jnp.log(sig) - jnp.log1p(-sig)
    od_conv_d_w = nrm(ks[16], (no, CONV_K, 3 * W_D), CONV_K ** -0.5)
    od_a_log = jnp.log(jax.random.uniform(ks[17], (no, H_D), f32, minval=1.0, maxval=16.0))
    u = jax.random.uniform(ks[18], (no, H_D), f32)
    dt = jnp.exp(np.log(0.001) + u * (np.log(0.1) - np.log(0.001)))
    od_dt_bias = dt + jnp.log(-jnp.expm1(-dt))
    od_onorm = 1.0 + nrm(ks[19], (no, HD_D), 0.05)
    od_w_out = nrm(ks[20], (no, W_OD, D_MODEL), W_OD ** -0.5)
    return {"x": x, "ev_norm": ev_norm, "ev_w_in": ev_w_in, "ev_if_bias": ev_if_bias, "ev_qn_gain": ev_qn_gain, "ev_kn_gain": ev_kn_gain, "ev_rel_bias": ev_rel_bias, "ev_w_out": ev_w_out, "od_norm": od_norm, "od_w_in": od_w_in, "od_conv_c_w": od_conv_c_w, "od_conv_c_b": od_conv_c_b, "od_gate_w": od_gate_w, "od_gate_b": od_gate_b, "od_lambda": od_lambda, "od_conv_d_w": od_conv_d_w, "od_a_log": od_a_log, "od_dt_bias": od_dt_bias, "od_onorm": od_onorm, "od_w_out": od_w_out}

def second_block(x, ev_norm, ev_w_in, ev_if_bias, ev_qn_gain, ev_kn_gain, ev_rel_bias, ev_w_out, od_norm, od_w_in, od_conv_c_w, od_conv_c_b, od_gate_w, od_gate_b, od_lambda, od_conv_d_w, od_a_log, od_dt_bias, od_onorm, od_w_out):
    for layer in range(DEPTH):
        j = layer // 2
        if layer % 2 == 0:
            x = x + even_layer(x, ev_norm[j], ev_w_in[j], ev_if_bias[j], ev_qn_gain[j], ev_kn_gain[j], ev_rel_bias[j], ev_w_out[j])
        else:
            x = x + odd_layer(x, od_norm[j], od_w_in[j], od_conv_c_w[j], od_conv_c_b[j], od_gate_w[j], od_gate_b[j], od_lambda[j], od_conv_d_w[j], od_a_log[j], od_dt_bias[j], od_onorm[j], od_w_out[j])
    return x


def setup_inputs(seed=0):
    out = dict(first_inputs(seed))
    for name, value in second_inputs(seed + 1).items():
        if name != "x":
            out[name + "_2"] = value
    return out


def reference(
    x, positions, dsa_w_in, dsa_w_out, mla_w_in, mla_q_norm, mla_w_uq, mla_kv_norm, mla_w_ukv,
    mla_w_out, ln_g, ln_b, ev_norm_2, ev_w_in_2, ev_if_bias_2, ev_qn_gain_2, ev_kn_gain_2,
    ev_rel_bias_2, ev_w_out_2, od_norm_2, od_w_in_2, od_conv_c_w_2, od_conv_c_b_2, od_gate_w_2,
    od_gate_b_2, od_lambda_2, od_conv_d_w_2, od_a_log_2, od_dt_bias_2, od_onorm_2, od_w_out_2,
):
    x = first_block(
        x, positions, dsa_w_in, dsa_w_out, mla_w_in, mla_q_norm, mla_w_uq, mla_kv_norm,
        mla_w_ukv, mla_w_out, ln_g, ln_b,
    )
    return second_block(
        x, ev_norm_2, ev_w_in_2, ev_if_bias_2, ev_qn_gain_2, ev_kn_gain_2, ev_rel_bias_2,
        ev_w_out_2, od_norm_2, od_w_in_2, od_conv_c_w_2, od_conv_c_b_2, od_gate_w_2,
        od_gate_b_2, od_lambda_2, od_conv_d_w_2, od_a_log_2, od_dt_bias_2, od_onorm_2,
        od_w_out_2,
    )


_drawn_inputs = setup_inputs


def setup_inputs(seed=0):
    import zlib

    import numpy as np

    out = dict(_drawn_inputs(seed))
    spreads = {}
    factors = {'mla_q_norm': 8.0,
     'mla_kv_norm': 8.0,
     'ev_qn_gain_2': 8.0,
     'ev_kn_gain_2': 8.0,
     'ev_rel_bias_2': 4.734,
     'od_conv_c_b_2': 4.293,
     'od_gate_b_2': 6.961,
     'od_onorm_2': 3.558}
    for name, (base, spread) in spreads.items():
        noise = np.random.default_rng([zlib.crc32(name.encode()), seed]).standard_normal(out[name].shape)
        drawn = base * np.exp(spread * noise) if base else spread * noise
        out[name] = jnp.asarray(drawn.astype(out[name].dtype))
    for name, factor in factors.items():
        out[name] = (out[name] * factor).astype(out[name].dtype)
    return out
```

```python
from contextlib import ExitStack, contextmanager
import math

import numpy as np
import concourse.bass as bass
import concourse.mybir as mybir

F32 = mybir.dt.float32
F32R = mybir.dt.float32r
I32 = mybir.dt.int32
ALU = mybir.AluOpType
ACT = mybir.ActivationFunctionType
AX = mybir.AxisListType
ds = bass.ds

P = 128
D = 2048
S = 256
TB = S // P
KT = D // P
N = 512
HALF = N // 2
NEG = -1e30
LOWEST = -3e38
DEPTH = 2
ALPHA = (2 * DEPTH) ** 0.25
LN_EPS = 1e-5
EPS = 1e-6
THETA = 10000.0
ENGINES = ("pe", "act", "dve", "pool", "sp")


class Loop:
    reg = None


class Index:
    def __init__(self, b, loop=None, a=0):
        self.loop, self.a, self.b = loop, a, b

    @property
    def v(self):
        return self.b if self.loop is None else self.loop.reg * self.a + self.b

    def __add__(self, k):
        return Index(self.b + k, self.loop, self.a)

    def __mul__(self, k):
        return Index(self.b * k, self.loop, self.a * k)


def index(i):
    return i if isinstance(i, Index) else Index(i)


class Program:
    def __init__(self, nc, ctx):
        self.nc, self.ctx = nc, ctx
        self.items = {e: [] for e in ENGINES}
        self.tracks = []

    @contextmanager
    def loop(self, lo, hi):
        lp = Loop()
        outer = self.items
        self.items = {e: [] for e in ENGINES}
        yield Index(0, lp, 1)
        inner, self.items = self.items, outer
        for e in ENGINES:
            if inner[e]:
                self.items[e].append(("loop", lp, lo, hi, inner[e]))

    def track(self, name):
        t = Track(self, name)
        self.tracks.append(t)
        return t

    def emit(self, name, eng):
        for t in self.tracks:
            t.close()
            for key, owner in t.owner.items():
                if t.repeats and owner == name:
                    eng.sem_inc(t.sem(key), t.per[key])
        self._emit(eng, self.items[name], {})

    def _emit(self, eng, items, seen):
        for it in items:
            if it[0] == "loop":
                _, lp, lo, hi, inner = it
                with eng.Fori(lo, hi) as i:
                    lp.reg = i
                    self._emit(eng, inner, {})
                lp.reg = None
                continue
            _, after, fn, sem, inc, by_itself = it
            looped = False
            for t in after:
                sem_, val = t.resolve()
                if val.loop is None:
                    key, b = (sem_, None), val.b
                    if b <= 0:
                        continue
                else:
                    key, b = (sem_, val.loop, val.a), val.b
                if seen.get(key, -1 << 30) >= b:
                    continue
                seen[key] = b
                eng.wait_ge(t.track.sem(sem_[1]), val.v)
                looped = val.loop is not None
            if by_itself and looped:
                by_itself()
            r = fn()
            if inc:
                r.then_inc(sem[0].sem(sem[1]), inc)


def flat(after):
    for t in after:
        if t is None:
            continue
        if isinstance(t, (list, tuple)):
            yield from flat(t)
        else:
            yield t


class Tok:
    def __init__(self, track, key, step, n):
        self.track, self.key, self.step, self.n = track, key, step, n

    def resolve(self):
        key, n = (self.key, self.n) if self.key else self.track.names[self.n]
        per = self.track.per[key]
        st = self.step
        return (self.track.name, key), Index(st.b * per + n, st.loop if st.a else None, st.a * per)


class Track:
    def __init__(self, prog, name):
        self.prog, self.name = prog, name
        self.sems, self.per, self.names, self.count, self.owner = {}, {}, {}, {}, {}
        self.step, self.repeats, self.fixed, self.started = Index(0), False, False, False

    def sem(self, key):
        return self.sems[key]

    def close(self):
        if self.count and not self.fixed:
            assert not self.per or self.per == self.count, (self.name, self.per, self.count)
            self.per = dict(self.count)
        self.count = {}

    def fix(self, per):
        self.fixed, self.repeats, self.per = True, True, per

    def begin(self, step):
        self.close()
        self.step, self.repeats = index(step), True
        return self

    def do(self, eng, fn, *after, sem=None, inc=1, name=None, by_itself=None):
        key = sem or eng
        if key not in self.sems:
            self.sems[key] = self.prog.ctx.enter_context(self.prog.nc.semaphore(f"{self.name}_{key}"))
            self.owner[key] = eng
        self.count[key] = self.count.get(key, 0) + inc
        tok = Tok(self, key, self.step, self.count[key])
        if name:
            self.names[name] = (key, self.count[key])
        self.prog.items[eng].append(("op", list(flat(after)), fn, (self, key), inc, by_itself))
        return tok

    def at(self, step, name):
        return Tok(self, None, index(step), name)


def quiet(side):
    for _ in side:
        pass


def build_program(nc, a, out, layers=(0, 1, 2, 3)):
    pe, act, dve, pool = nc.tensor, nc.scalar, nc.vector, nc.gpsimd
    ctx = ExitStack()
    with ctx:
        pr = Program(nc, ctx)

        def sb(name, shape, dt=F32):
            return ctx.enter_context(nc.sbuf_tensor(name, shape, dt))

        raw = sb("raw", [P, 4, 4, N])
        whi = sb("whi", [P, 4, 2, N], F32R)
        wlo = sb("wlo", [P, 4, 2, N], F32R)
        xh = sb("xh", [P, KT, S], F32R)
        xl = sb("xl", [P, KT, S], F32R)
        x = sb("x", [P, TB, D])
        y = sb("y", [P, TB, D])
        ident = sb("ident", [P, P])
        ones = sb("ones", [P, P])
        nhalf = sb("nhalf", [P, 64])
        small = sb("small", [P, 256])
        stats = sb("stats", [P, TB, 4, 6])
        mv = sb("mv", [P, TB, 2])
        rstd = sb("rstd", [P, TB])
        vec = sb("vec", [P, 256])
        cosb = sb("cosb", [P, TB, 64])
        sinb = sb("sinb", [P, TB, 64])
        WORK = 19200
        work = sb("work", [P, WORK])
        ps = ctx.enter_context(nc.psum_tensor("ps", [P, 8, N], F32))
        Q = 4

        class Carve:
            def __init__(self, at=0):
                self.at = at

            def __call__(self, *shape):
                n = int(np.prod(shape))
                ap = work[:, self.at:self.at + n]
                self.at += n
                assert self.at <= WORK, self.at
                if len(shape) > 1:
                    names = "abcd"[:len(shape)]
                    ap = ap.rearrange(f"p ({' '.join(names)}) -> p {' '.join(names)}",
                                      **dict(zip(names, shape)))
                return ap

        c = pr.track("const")
        t = c.do("pool", lambda: pool.memset(ident[:, :], 0.0))
        t_ident = c.do("pool", lambda: pool.affine_select(
            out=ident[:, :], in_=ident[:, :], compare_op=ALU.not_equal, fill=1.0, base=0,
            pattern=[[-1, P]], channel_multiplier=1), t)
        c.do("pool", lambda: pool.memset(ones[:, :], 1.0))
        t_const = c.do("pool", lambda: pool.memset(nhalf[:, :], -0.5))

        ring = pr.track("ring")
        ring.fix({"act": 8, "dve": 8, "pe": 8, **{f"raw{j}": 32 for j in range(4)}})
        nstep = [1]
        AHEAD = 3

        def slot(k):
            return whi[:, k % 4], wlo[:, k % 4]

        def split(step, k):
            if k >= 8:
                step, k = step + 1, k - 8
            w = raw[:, k // 2, 2 * (k % 2):2 * (k % 2) + 2, :]
            hi, lo = slot(k)
            d = Tok(ring, f"raw{k // 2}", step, 32)
            used = Tok(ring, "pe", step, k - 3) if k >= 4 else Tok(ring, "pe", step + -1, k + 5)
            ring.do("act", lambda: act.copy(hi, w), d, used)
            th = Tok(ring, "act", step, k + 1)
            ring.do("dve", lambda: dve.tensor_tensor(lo, w, hi.bitcast(F32), ALU.subtract), th, d, used)

        def stream(units, side=None, step=None, last=False):
            if step is None:
                step = nstep[0]
                nstep[0] += 1
            if not ring.started:
                for k in range(AHEAD):
                    split(index(step), k)
            step = index(step)
            ring.started = True
            ring.step = step
            t = None
            for j, (halves, n, mm, waits, done) in enumerate(units):
                free = Tok(ring, "dve", step + -1, 2 * j + 2)
                for dst, src in halves:
                    ring.do("sp", lambda dst=dst, src=src, j=j: nc.sync.dma_start(
                        dst(raw[:, j]), src()), free, sem=f"raw{j}", inc=16)
                for s in range(2):
                    k = 2 * j + s
                    if k + AHEAD < 8 or not last:
                        split(step, k + AHEAD)
                    hi, lo = (v[:, :, 0:n] for v in slot(k))
                    ring.do("pe", lambda mm=mm, s=s, hi=hi, lo=lo: mm(s, hi, lo),
                            Tok(ring, "dve", step, k + 1), waits)
                    t = Tok(ring, "pe", step, k + 1)
                    if s == 1 and done:
                        done(t)
                    if side is not None:
                        next(side, None)
            return t

        def products(xh_, xl_, g0, hi, lo, n, bank, start, stop):
            for l in range(2):
                for tb in range(TB):
                    o = ps[:, bank + tb, 0:n]
                    sh = xh_[:, g0 + l, tb * P:(tb + 1) * P]
                    sl = xl_[:, g0 + l, tb * P:(tb + 1) * P]
                    pe.matmul(o, sh, hi[:, l, :], start=start and l == 0, stop=False)
                    pe.matmul(o, sh, lo[:, l, :], start=False, stop=False)
                    m = pe.matmul(o, sl, hi[:, l, :], start=False, stop=stop and l == 1)
            return m

        def project(w, cols, bank, waits, side=None, step=None, last=False):
            n = sum(k for _, k in cols)
            units = []
            for j in range(4):
                halves = []
                for s in range(2):
                    if len(cols) == 1:
                        c0, k = cols[0]
                        r0 = (4 * j + 2 * s) * P
                        halves.append((lambda r, s=s, k=k: r[:, 2 * s:2 * s + 2, 0:k],
                                       lambda r0=r0, c0=c0, k=k: w[r0:r0 + 2 * P, ds(index(c0).v, k)]
                                       .rearrange("(t p) n -> p t n", p=P)))
                    else:
                        c0, k = cols[s]
                        r0 = 4 * j * P
                        halves.append((lambda r, s=s, k=k: r[:, :, s * k:(s + 1) * k],
                                       lambda r0=r0, c0=c0, k=k: w[r0:r0 + 4 * P, ds(index(c0).v, k)]
                                       .rearrange("(t p) n -> p t n", p=P)))
                units.append((halves, n, lambda s, hi, lo, j=j: products(
                    xh, xl, 4 * j + 2 * s, hi, lo, n, bank, j == 0 and s == 0, j == 3 and s == 1),
                    waits if j == 0 else [], None))
            return stream(units, side, step, last)

        def transposed(tr, src, nk, dh, dl, waits, gain=None, wait_bank=None):
            freed = list(wait_bank or [None, None])
            tok = []
            for g in range(nk // 2):
                b = Q + g % 2

                def tp(g=g, b=b):
                    for l in range(2):
                        for tb in range(TB):
                            m = pe.transpose(ps[:, b, (l * TB + tb) * P:(l * TB + tb + 1) * P],
                                             src(tb, 2 * g + l), ident[:, :])
                    return m
                t = tr.do("pe", tp, waits if g == 0 else [], freed[g % 2], t_ident)
                if gain is None:
                    pv = ps[:, b, :].rearrange("p (l t) -> p l t", l=2)
                    hh, ll = dh[:, 2 * g:2 * g + 2, :], dl[:, 2 * g:2 * g + 2, :]
                    th = tr.do("act", lambda hh=hh, pv=pv: act.copy(hh, pv), t)
                    tl = tr.do("dve", lambda hh=hh, ll=ll, pv=pv: dve.tensor_tensor(
                        ll, pv, hh.bitcast(F32), ALU.subtract), t, th)
                else:
                    ops = []
                    for l in range(2):
                        k = 2 * g + l
                        ops.append((ps[:, b, l * S:(l + 1) * S], dh[:, k, :], dl[:, k, :], gain[:, k:k + 1]))
                    for pv, hh, _, gg in ops:
                        th = tr.do("act", lambda hh=hh, pv=pv, gg=gg: act.activation(
                            hh, pv, ACT.Copy, scale=gg), t)
                    for pv, hh, ll, gg in ops:
                        tl = tr.do("dve", lambda hh=hh, ll=ll, pv=pv, gg=gg: dve.scalar_tensor_tensor(
                            out=ll, in0=pv, scalar=gg, in1=hh.bitcast(F32), op0=ALU.mult,
                            op1=ALU.subtract), t, th)
                freed[g % 2] = tl
                tok = [th, tl]
            return tok

        def silu_into(tr, dst, src, after, scratch):
            t = tr.do("act", lambda: act.activation(scratch(), src(), ACT.Tanh), after)
            return tr.do("dve", lambda: dve.scalar_tensor_tensor(
                out=dst(), in0=scratch(), scalar=1.0, in1=src(), op0=ALU.add, op1=ALU.mult), t, after)

        def root_inverse(tr, dst, src, k, eps, scale, waits):
            t = tr.do("dve", lambda: dve.tensor_scalar(dst, src, scale, eps, ALU.mult, ALU.add), waits)
            return tr.do("pool", lambda: pool.tensor_tensor(
                dst, dst, nhalf[:, 0:k], ALU.pow), t, t_const)

        def bc(ap, dim, n):
            u = ap.unsqueeze(dim)
            shape = list(u.shape)
            shape[dim] = n
            return u.broadcast_to(shape)

        def load(name, dst, src, *after, scattered=False):
            return pr.track("ld_" + name).do("pool", lambda: pool.dma_start(
                dst, src(), allow_slow_non_contiguous=scattered), *after,
                                             sem="dma", inc=16)

        def row(v, n):
            return bass.AP(v.tensor, v.offset, [[0, P], [1, n]])

        t_x = load("x", x[:, :, :], lambda: a["x"][0].rearrange("(t p) d -> p t d", p=P))
        rows = [("cd", a["od_conv_d_w_2"][0].rearrange("j (c p) -> (j c) p", p=P), 96),
                ("cw", a["od_conv_c_w_2"][0].rearrange("j (c p) -> (j c) p", p=P), 32),
                ("cb", a["od_conv_c_b_2"][0].rearrange("(c p) -> c p", p=P), 8),
                ("gb", a["od_gate_b_2"][0].rearrange("(c p) -> c p", p=P), 16),
                ("lam", a["od_lambda_2"][0].rearrange("(c p) -> c p", p=P), 8),
                ("ev", a["ev_norm_2"][0].rearrange("(c p) -> c p", p=P), 16),
                ("od", a["od_norm_2"][0].rearrange("(c p) -> c p", p=P), 16),
                ("qn", a["ev_qn_gain_2"], 1), ("kn", a["ev_kn_gain_2"], 1),
                ("mq", a["mla_q_norm"][0].rearrange("(c p) -> c p", p=P), 4),
                ("mk", a["mla_kv_norm"][0].rearrange("(c p) -> c p", p=P), 4)]
        setup = pr.track("setup")
        vrows = y[:, 0, 0:2 * P].rearrange("p (g c) -> p g c", g=2)
        col, at, tl = {}, 0, []
        t_vz = setup.do("dve", lambda: dve.memset(vrows, 0.0))
        for name, src, n in rows:
            g = 0 if at < 96 else 1
            o = at if g == 0 else at - 96
            tl.append(setup.do("sp", lambda g=g, o=o, n=n, src=src: nc.sync.dma_start(
                vrows[o:o + n, g, :], src), t_vz, sem="vec", inc=16))
            col[name] = g * P + o
            at += n
        t = setup.do("pe", lambda: [pe.transpose(ps[:, 7, g * P:(g + 1) * P], vrows[:, g, :], ident[:, :])
                                    for g in range(2)][-1], tl[-1], t_ident)
        t_vec = setup.do("dve", lambda: dve.tensor_copy(vec[:, :], ps[:, 7, 0:2 * P]), t)

        def vcol(name, n, k=0):
            return vec[:, col[name] + k:col[name] + k + n]

        class Heads:
            def __init__(self, tr, step, n):
                self.tr, self.step, self.n, self.tok = tr, index(step), n, {}
                tr.begin(step)

            def do(self, eng, stage, h, fn, *after, **kw):
                t = self.tr.do(eng, fn, *after, name=f"{stage}{h}", **kw)
                self.tok[stage, h] = t
                return t

            def before(self, stage, h):
                if h:
                    return self.tok[stage, h - 1]
                return self.tr.at(self.step + -1, f"{stage}{self.n - 1}")

            def prior(self, name):
                return self.tr.at(self.step + -1, name)

        def attend(hd, h, scores, ready, parts, scale, nblk, tbank, pt, pv, fin, sc, gap=1):
            mx, nb, den, rden = (sc[:, 2 * i:2 * i + 2] for i in range(4))
            t = hd.do("pe", "sc", h, scores, ready, hd.before("mask", h), hd.before("pt", h))
            for tb, (s_, m_, w_) in enumerate(parts):
                t1 = hd.do("dve", "mask", h, lambda s_=s_, m_=m_, w_=w_, tb=tb: dve.tensor_tensor_reduce(
                    w_, s_, m_() if callable(m_) else m_, 1.0, LOWEST, ALU.add, ALU.max, mx[:, tb:tb + 1]),
                    t, hd.before("tp", h), hd.before("fin", h),
                    by_itself=lambda: dve.memset(small[:, 255:256], 0.0))
            t2 = hd.do("dve", "nb", h, lambda: dve.tensor_scalar(nb, mx, -scale, None, ALU.mult), t1)
            for tb, (s_, m_, w_) in enumerate(parts):
                t3 = hd.do("act", "exp", h, lambda w_=w_, tb=tb: act.activation(
                    w_, w_, ACT.Exp, bias=nb[:, tb:tb + 1], scale=scale, accum_out=den[:, tb:tb + 1]), t2)
            t4 = hd.do("dve", "rden", h, lambda: dve.reciprocal(rden, den), t3)
            for _ in range(gap):
                yield
            w0 = parts[0][2]
            blocks = bass.AP(w0.tensor, w0.offset, [list(w0.ap[0]), [P, nblk], [1, P]])

            def turn():
                for b in range(nblk):
                    m = pe.transpose(tbank[:, b * P:(b + 1) * P], blocks[:, b, :], ident[:, :])
                return m
            t5 = hd.do("pe", "tp", h, turn, t3, t1, hd.before("pt", h))
            t6 = hd.do("act", "pt", h, lambda: act.copy(pt, tbank[:, 0:nblk * P]), t5, hd.before("pv", h))
            yield
            t7 = hd.do("pe", "pv", h, pv, t6, hd.before("fin", h))
            hd.do("dve", "fin", h, lambda: fin(rden), t7, t4)
            yield

        def gates(name, w, c0, y0, nslab, waits, scratch, side=None):
            tr = pr.track(name)
            base = nstep[0]
            nstep[0] += nslab
            def two_slabs(i):
                tr.begin(i + 1)
                for s in range(2):
                    free = tr.at(i, f"g{s}")
                    tm = project(w, [((i * (2 * N)) + (c0 + s * N), N)], 2 * s, [waits, free],
                                 side, step=(i * 2) + (base + s))
                    gate_out(tr, f"g{s}", ps[:, 2 * s:2 * s + 2, :],
                             (i * (2 * N)) + (y0 + s * N), N, tm, scratch,
                             tr.at(i, "g1") if s == 0 else tr.at(i + 1, "g0"))
            if nslab > 2:
                with pr.loop(0, nslab // 2) as i:
                    two_slabs(i)
            else:
                two_slabs(index(0))
            return tr.at(nslab // 2, "g1")

        def gate_out(tr, name, src, c, n, ready, scratch, scratch_free):
            t1 = tr.do("act", lambda: act.activation(y[:, :, ds(c.v, n)], src, ACT.Copy, scale=0.5), ready)
            t2 = tr.do("act", lambda: act.activation(scratch, src, ACT.Tanh, scale=0.5), ready, scratch_free)
            return tr.do("dve", lambda: dve.scalar_tensor_tensor(
                out=y[:, :, ds(c.v, n)], in0=scratch, scalar=1.0, in1=y[:, :, ds(c.v, n)],
                op0=ALU.add, op1=ALU.mult), t1, t2, name=name)

        def last_product(name, w, ready, alpha, last):
            ty = transposed(pr.track(name + "_t"), lambda tb, k: y[:, tb, k * P:(k + 1) * P], KT, xh, xl, ready)
            ev = pr.track(name)
            base = nstep[0]
            nstep[0] += 4

            def two_slabs(i):
                ev.begin(i + 1)
                for s in range(2):
                    c = (i * (2 * N)) + s * N
                    tm = project(w, [(c, N)], 2 * s, [ty, ev.at(i, f"add{s}")], step=(i * 2) + (base + s),
                                 last=last and i.loop is None and s == 1)
                    t = ev.do("dve", lambda s=s, c=c: dve.scalar_tensor_tensor(
                        out=x[:, :, ds(c.v, N)], in0=x[:, :, ds(c.v, N)], scalar=alpha,
                        in1=ps[:, 2 * s:2 * s + 2, :], op0=ALU.mult, op1=ALU.add), tm, name=f"add{s}")
                    if alpha != 1.0:
                        for tb in range(TB):
                            ev.do("dve", lambda s=s, c=c, tb=tb, i=i: dve.bn_stats(
                                stats[:, tb, ds((i * 2 + s).v, 1), :].rearrange("p a b -> p (a b)"),
                                x[:, tb, ds(c.v, N)]), t, name="end")
            if last:
                with pr.loop(0, 1) as i:
                    two_slabs(i)
                two_slabs(index(1))
            else:
                with pr.loop(0, 2) as i:
                    two_slabs(i)
            return ev.at(2, "end" if alpha != 1.0 else "add1")

        LN = WORK - 2 * D

        def layer_norm(layer, ready, free):
            tr = pr.track(f"ln{layer}")
            c_ = Carve(LN)
            g, b = c_(D), c_(D)
            tg = [load(f"lng{layer}", g, lambda: row(a["ln_g"][layer], D), free),
                  load(f"lnb{layer}", b, lambda: row(a["ln_b"][layer], D), free)]
            for tb in range(TB):
                t = tr.do("dve", lambda tb=tb: dve.bn_aggr(
                    mv[:, tb, :], stats[:, tb].rearrange("p a b -> p (a b)")), ready)
            tv = tr.do("dve", lambda: dve.tensor_scalar(rstd[:, :], mv[:, :, 1], LN_EPS, None, ALU.add), t)
            tv = tr.do("pool", lambda: pool.tensor_tensor(rstd[:, :], rstd[:, :], nhalf[:, 0:TB], ALU.pow),
                       tv, t_const)
            out_ = []
            for tb in range(TB):
                e, en = (dve, "dve") if tb == 0 else (pool, "pool")
                t = tr.do("dve", lambda tb=tb: dve.tensor_scalar(
                    x[:, tb], x[:, tb], mv[:, tb, 0:1], rstd[:, tb:tb + 1], ALU.subtract, ALU.mult), tv, t, ready)
                t2 = tr.do(en, lambda e=e, tb=tb: e.tensor_tensor(x[:, tb], x[:, tb], g, ALU.mult), t, tg)
                out_.append(tr.do(en, lambda e=e, tb=tb: e.tensor_tensor(x[:, tb], x[:, tb], b, ALU.add), t2, tg))
            return out_

        def rms_scale(name, ready, free):
            tr = pr.track(name)
            ts = [tr.do("act", lambda tb=tb: act.activation(
                y[:, tb], x[:, tb], ACT.Square, accum_out=small[:, tb:tb + 1]), ready, free) for tb in range(TB)]
            t = root_inverse(tr, small[:, 2:4], small[:, 0:2], TB, EPS, 1.0 / D, ts)
            e = [tr.do("dve", lambda tb=tb: dve.tensor_scalar(
                y[:, tb], x[:, tb], small[:, 2 + tb:3 + tb], None, ALU.mult), t, ts) for tb in range(TB)]
            return e

        def rope_tables(cosa, sina, base):
            tr = pr.track("rope")
            FA, FB = 64, 32
            F = FA + FB
            c_ = Carve(base)
            inv, pos = c_(F), c_(TB)
            ang, kk, r, rc, m = (c_(TB, F) for _ in range(5))
            posi = small[:, 8:8 + TB].bitcast(I32)
            t = load("pos", posi, lambda: a["positions"][0].rearrange("(t p) -> p t", p=P), scattered=True)
            ti = load("inv", inv, lambda: row(a["inv_freq"], F))
            t = tr.do("dve", lambda: dve.tensor_copy(pos, posi), t)
            for tb in range(TB):
                t = tr.do("dve", lambda tb=tb: dve.tensor_scalar(
                    ang[:, tb], inv, pos[:, tb:tb + 1], None, ALU.mult), t, ti)
            two_pi = 2 * math.pi
            c1 = 6.28125
            c2 = float(np.float32(math.floor((two_pi - c1) * 2.0 ** 22) / 2.0 ** 22))
            c3 = two_pi - c1 - c2
            magic = 1.5 * 2.0 ** 23
            t = tr.do("dve", lambda: dve.tensor_scalar(kk, ang, 1 / two_pi, magic, ALU.mult, ALU.add), t)
            t = tr.do("dve", lambda: dve.tensor_scalar(kk, kk, magic, None, ALU.subtract), t)
            src = ang
            for cc in (c1, c2, c3):
                t = tr.do("dve", lambda cc=cc, src=src: dve.scalar_tensor_tensor(
                    out=r, in0=kk, scalar=-cc, in1=src, op0=ALU.mult, op1=ALU.add), t)
                src = r
            lim = 3.1415925
            t = tr.do("dve", lambda: dve.tensor_scalar(r, r, lim, -lim, ALU.min, ALU.max), t)
            t = tr.do("dve", lambda: dve.tensor_scalar(rc, r, math.pi / 2, None, ALU.add), t)
            t = tr.do("dve", lambda: dve.tensor_scalar(m, rc, math.pi, None, ALU.is_gt), t)
            t = tr.do("dve", lambda: dve.scalar_tensor_tensor(
                out=rc, in0=m, scalar=-two_pi, in1=rc, op0=ALU.mult, op1=ALU.add), t)
            t = tr.do("dve", lambda: dve.tensor_scalar(rc, rc, lim, -lim, ALU.min, ALU.max), t)
            for tb in range(TB):
                for half in range(2):
                    sg = -1.0 if half == 0 else 1.0
                    for hh in range(2):
                        o = slice(half * FA, half * FA + FA)
                        tr.do("act", lambda tb=tb, hh=hh, o=o: act.activation(
                            cosa[:, 2 * tb + hh, o], rc[:, tb, 0:FA], ACT.Sin), t)
                        tr.do("act", lambda tb=tb, hh=hh, o=o, sg=sg: act.activation(
                            sina[:, 2 * tb + hh, o], r[:, tb, 0:FA], ACT.Sin, scale=sg), t)
                    o = slice(half * FB, half * FB + FB)
                    tr.do("act", lambda tb=tb, o=o: act.activation(cosb[:, tb, o], rc[:, tb, FA:F], ACT.Sin), t)
                    te = tr.do("act", lambda tb=tb, o=o, sg=sg: act.activation(
                        sinb[:, tb, o], r[:, tb, FA:F], ACT.Sin, scale=sg), t)
            return te

        def causal(tr, m, w, base, t, strict=False):
            return tr.do("pool", lambda: pool.affine_select(
                out=m, in_=m, compare_op=ALU.is_gt if strict else ALU.is_ge, fill=NEG, base=base,
                pattern=[[-1, w]], channel_multiplier=1), t)

        ROPE_AT = 14592 + 1152
        t_rope = rope_tables(work[:, ROPE_AT:ROPE_AT + 512].rearrange("p (a b) -> p a b", a=4),
                             work[:, ROPE_AT + 512:ROPE_AT + 1024].rearrange("p (a b) -> p a b", a=4), ROPE_AT + 1024)

        def layer0(ready, last):
            G = 3
            PAIRS = 8
            c_ = Carve()
            h = c_(10, TB, HALF)
            t1, t2 = c_(4, P), c_(4, P)
            qk = c_(6, 2, S)
            vb = c_(G, TB, HALF)
            zs = c_(TB, HALF)
            sm = c_(9 * P)
            pt = c_(9 * P)
            mask = c_(9 * P)
            c_.at = ROPE_AT
            cosa, sina = c_(4, P), c_(4, P)
            tr = pr.track("mask0")
            iv = t1.rearrange("p a b -> p (a b)")[:, 0:S].bitcast(I32)
            t = tr.do("pool", lambda: pool.iota(iv, [[-1, S]], base=S, channel_multiplier=1))
            m0 = mask[:, 0:G * P].rearrange("p (g k) -> p g k", g=G)
            m1 = mask[:, G * P:].rearrange("p (g k) -> p g k", g=G)
            tm = tr.do("pool", lambda: pool.memset(mask, 0.0))
            it = t2.rearrange("p a b -> p (a b)")[:, 0:S].bitcast(I32)
            for g, dil in ((1, 4), (2, 16)):
                t = tr.do("dve", lambda dil=dil: dve.tensor_scalar(it, iv, dil - 1, None, ALU.bitwise_and), t, tm)
                t = tr.do("dve", lambda g=g: dve.tensor_scalar(m0[:, g], it[:, 0:P], 1.0, NEG, ALU.min, ALU.mult), t, tm)
                t = tr.do("dve", lambda g=g: dve.tensor_scalar(m1[:, g], it, 1.0, NEG, ALU.min, ALU.mult), t, tm)
            for g in range(G):
                t = causal(tr, m0[:, g], P, 0, t)
                t = causal(tr, m1[:, g], S, P, t)
            t_mask = tr.do("pool", lambda: pool.affine_select(
                out=m1[:, 0], in_=m1[:, 0], compare_op=ALU.is_ge, fill=NEG, base=0,
                pattern=[[1, S]], channel_multiplier=-1), t)

            tx = transposed(pr.track("xt0"), lambda tb, k: x[:, tb, k * P:(k + 1) * P], KT, xh, xl, [ready, t_vec])
            w = a["dsa_w_in"][0]
            ev = pr.track("ev0")
            tr = pr.track("att0")
            BLOCKS = [(0, 0), (0, 1), (0, 2), (1, 0), (1, 1), (1, 2), (2, 0), (2, 1), (2, 2), (3, 0)]
            ROT = [0, 1, 3, 4, 6, 7]

            def pair_projection(pair, side, base):
                ev.begin(pair + 1)
                for s in range(5):
                    cols = [(pair * HALF + (3 * g + t) * D, HALF) for g, t in BLOCKS[2 * s:2 * s + 2]]
                    b = 2 * (s % 2)
                    free = ev.at(pair + 1, f"out{s - 2}") if s >= 2 else \
                        ev.at(pair, "out4" if s == 0 else "out3")
                    tm = project(w, cols, b, [tx, free], side, step=(pair * 5) + (base + s))
                    dst = h[:, 2 * s:2 * s + 2].rearrange("p b t c -> p t b c")
                    src = ps[:, b:b + 2, :].rearrange("p t (b c) -> p t b c", b=2)
                    took = [tr.at(pair, f"took{k}") for k in (2 * s, 2 * s + 1)]
                    if s < 4:
                        ev.do("act", lambda dst=dst, src=src: act.copy(dst, src), tm, took, name=f"out{s}")
                    else:
                        ev.do("act", lambda: act.copy(h[:, 8], ps[:, 0:2, 0:HALF]), tm, took)
                        ev.do("act", lambda: act.activation(h[:, 9], ps[:, 0:2, HALF:N], ACT.Copy, scale=0.5),
                              tm, took, name="out4")

            def pair_attention(pair):
                step = pair + 1
                hd = Heads(tr, step, 2)
                for g in range(G):
                    tv = tr.do("act", lambda g=g: act.copy(vb[:, g], h[:, 3 * g + 2]),
                               ev.at(step, "out4"), hd.prior("pv1"), name=f"took{3 * g + 2}")
                tz = tr.do("act", lambda: act.activation(zs, h[:, 9], ACT.Tanh), ev.at(step, "out4"), hd.prior("fin1"))
                tz = tr.do("dve", lambda: dve.scalar_tensor_tensor(
                    out=zs, in0=zs, scalar=1.0, in1=h[:, 9], op0=ALU.add, op1=ALU.mult), tz, name="took9")
                yield
                pend = []

                def turn(n, blk, tr_):
                    b = Q + n % 3
                    v = h[:, blk].rearrange("p t (h d) -> p h t d", h=2)

                    def f():
                        for hh in range(2):
                            for tb in range(TB):
                                m = pe.transpose(ps[:, b, (hh * TB + tb) * P:(hh * TB + tb + 1) * P],
                                                 v[:, hh, tb, :], ident[:, :])
                        return m
                    t = tr.do("pe", f, tr_, pend[n - 3] if n >= 3 else hd.prior("pt1"),
                              hd.prior("mask1") if n < 3 else None, name=f"took{blk}")
                    pend.append(tr.do("act", lambda: act.copy(qk[:, n], ps[:, b, :].rearrange(
                        "p (h t) -> p h t", h=2)), t, hd.prior("sc1"), name=f"qk{n}"))

                wait = None
                last = [tz]
                for n, blk in enumerate(ROT):
                    xv = h[:, blk].rearrange("p t (h d) -> p (t h) d", h=2)
                    ta = tr.do("pool", lambda xv=xv: pool.tensor_tensor(t1, xv, cosa, ALU.mult),
                               ev.at(step, "out4"), t_rope, t_mask, last)
                    tb1 = tr.do("dve", lambda xv=xv: dve.tensor_tensor(
                        t2[:, :, 0:64], xv[:, :, 64:P], sina[:, :, 0:64], ALU.mult), ev.at(step, "out4"), t_rope, t_mask, last)
                    tb2 = tr.do("dve", lambda xv=xv: dve.tensor_tensor(
                        t2[:, :, 64:P], xv[:, :, 0:64], sina[:, :, 64:P], ALU.mult), t_rope, t_mask, last)
                    last = [tr.do("dve", lambda xv=xv: dve.tensor_tensor(xv, t1, t2, ALU.add), ta, tb1, tb2)]
                    if wait:
                        turn(*wait)
                    wait = (n, blk, last)
                    yield
                turn(*wait)
                yield

                def head(hh):
                    def scores():
                        for g in range(G):
                            q, k = qk[:, 2 * g, hh, :], qk[:, 2 * g + 1, hh, :]
                            pe.matmul(flat4[:, g * P:(g + 1) * P], q[:, 0:P], k[:, 0:P], start=True, stop=True)
                        for g in range(G):
                            q, k = qk[:, 2 * g, hh, :], qk[:, 2 * g + 1, hh, :]
                            m = pe.matmul(flat4[:, N + g * S:N + (g + 1) * S], q[:, P:S], k[:, 0:S], start=True, stop=True)
                        return m

                    def pv():
                        for tb in range(TB):
                            o = ps[:, Q + 3, tb * P:(tb + 1) * P]
                            for g in range(G):
                                for kb in range(tb + 1):
                                    blk = g if tb == 0 else G + 2 * g + kb
                                    m = pe.matmul(o, pt[:, blk * P:(blk + 1) * P], vb[:, g, kb, hh * P:(hh + 1) * P],
                                                  start=g == 0 and kb == 0, stop=g == G - 1 and kb == tb)
                        return m

                    def fin(rden):
                        for tb in range(TB):
                            c = index(pair) * HALF + hh * P
                            m = dve.scalar_tensor_tensor(
                                out=y[:, tb, ds(c.v, P)], in0=ps[:, Q + 3, tb * P:(tb + 1) * P],
                                scalar=rden[:, tb:tb + 1], in1=zs[:, tb, hh * P:(hh + 1) * P],
                                op0=ALU.mult, op1=ALU.mult)
                        return m
                    parts = [(flat4[:, 0:G * P], mask[:, 0:G * P], sm[:, 0:G * P]),
                             (flat4[:, N:N + G * S], mask[:, G * P:], sm[:, G * P:])]
                    return attend(hd, hh, scores, [pend, t_mask], parts, P ** -0.5, 9, flat4, pt, pv, fin,
                                  small[:, 16 + 8 * hh:24 + 8 * hh], gap=2)
                flat4 = ps[:, Q:Q + 4, :].rearrange("p b n -> p (b n)")
                for hh in range(2):
                    for k, _ in enumerate(head(hh)):
                        yield

            base = nstep[0]
            nstep[0] += 5 * PAIRS
            pair_projection(index(0), None, base)
            with pr.loop(1, PAIRS) as i:
                side = pair_attention(i + -1)
                pair_projection(i, side, base)
                quiet(side)
            quiet(pair_attention(index(PAIRS - 1)))
            t = last_product("out0", a["dsa_w_out"][0], [tr.at(PAIRS, "fin1")], ALPHA, last)
            return layer_norm(0, t, tr.at(PAIRS, "fin1"))

        def unit_products(sh, sl, g0, bank):
            def mm(s, hi, lo):
                return products(sh, sl, g0 + 2 * s, hi, lo, hi.shape[-1], bank, s == 0, s == 1)
            return mm

        def layer1(ready, last):
            NOPE, ROPE, R = P, 64, 512
            QH, KH = NOPE + ROPE, 2 * P
            QUADS, HQ = 4, 4
            c_ = Carve()
            cc = c_(2, TB, R)
            hq = c_(TB, HQ * QH)
            hkv = c_(TB, HQ * KH)
            v = c_(TB, HQ, P)
            qt, kt, qpt = c_(HQ, S), c_(HQ, S), c_(HQ, S)
            kpt = c_(S)
            t1, t2 = c_(TB, HQ, ROPE), c_(TB, HQ, ROPE)
            kp = c_(TB, ROPE)
            sm, pt, mask = c_(3 * P), c_(3 * P), c_(3 * P)
            scratch = c_(TB, N)
            w = a["mla_w_in"][0]
            tr = pr.track("mask1")
            t = tr.do("pool", lambda: pool.memset(mask, 0.0), ready)
            t = causal(tr, mask[:, 0:P], P, 0, t)
            t_mask = causal(tr, mask[:, P:], S, P, t)

            tx = transposed(pr.track("xt1"), lambda tb, k: x[:, tb, k * P:(k + 1) * P], KT, xh, xl, ready)
            la = pr.track("lat")
            outs = []
            for s, (c0, n) in enumerate(((0, R), (2 * R, ROPE), (R, R))):
                b = 2 * (s % 2)
                tm = project(w, [(c0, n)], b, [tx, outs[0] if s == 2 else None])
                dst = kp if s == 1 else cc[:, s // 2]
                outs.append(la.do("act", lambda b=b, dst=dst, n=n: act.copy(dst, ps[:, b:b + 2, 0:n]), tm, ready))

            def norms():
                t = None
                for s in range(2):
                    for tb in range(TB):
                        t = la.do("act", lambda s=s, tb=tb: act.activation(
                            scratch2[:, tb], cc[:, s, tb], ACT.Square,
                            accum_out=small[:, 2 * s + tb:2 * s + tb + 1]), outs, ready, t)
                t = root_inverse(la, small[:, 4:8], small[:, 0:4], 4, EPS, 1.0 / R, t)
                yield
                for s in range(2):
                    for tb in range(TB):
                        k = 4 + 2 * s + tb
                        tn = la.do("dve", lambda s=s, tb=tb, k=k: dve.tensor_scalar(
                            cc[:, s, tb], cc[:, s, tb], small[:, k:k + 1], None, ALU.mult), t)
                la.normed = tn
                yield
                ta = la.do("dve", lambda: dve.tensor_tensor(t1[:, :, 0], kp, cosb[:, :, :], ALU.mult), outs)
                la.do("dve", lambda: dve.tensor_tensor(t2[:, :, 0, 0:32], kp[:, :, 32:64], sinb[:, :, 0:32], ALU.mult), outs)
                tb_ = la.do("dve", lambda: dve.tensor_tensor(t2[:, :, 0, 32:64], kp[:, :, 0:32], sinb[:, :, 32:64], ALU.mult))
                t = la.do("dve", lambda: dve.tensor_tensor(kp, t1[:, :, 0], t2[:, :, 0], ALU.add), ta, tb_)
                yield
                t = la.do("pe", lambda: [pe.transpose(ps[0:ROPE, Q + 3, tb * P:(tb + 1) * P], kp[:, tb], ident[:, :])
                                         for tb in range(TB)][-1], t)
                la.kpt = la.do("act", lambda: act.copy(kpt[0:ROPE], ps[0:ROPE, Q + 3, 0:S]), t)
                yield
            scratch2 = hq.rearrange("p a b -> p (a b)")[:, 0:TB * R].rearrange("p (t n) -> p t n", t=TB)
            quiet(norms())
            tg = gates("gate1", w, 2 * R + ROPE, 0, 4, [tx, outs], scratch)
            ct = pr.track("ct")
            tq = transposed(ct, lambda tb, k: cc[:, 0, tb, k * P:(k + 1) * P], 4, xh[:, 0:4], xl[:, 0:4],
                            [la.normed, tg], gain=vcol("mq", 4), wait_bank=[la.kpt, la.kpt])
            tk = transposed(ct, lambda tb, k: cc[:, 1, tb, k * P:(k + 1) * P], 4, xh[:, 4:8], xl[:, 4:8],
                            [la.normed, tg], gain=vcol("mk", 4), wait_bank=[tq, tq])

            ev, tr = pr.track("ev1"), pr.track("att1")
            wq, wkv = a["mla_w_uq"][0], a["mla_w_ukv"][0]

            def quad_projection(quad, side, base):
                ev.begin(quad + 1)
                units = []
                for p in range(2):
                    for kind in range(2):
                        n = 2 * (QH, KH)[kind]
                        b = 2 * kind
                        c0 = quad * (2 * n) + p * n
                        wsrc = (wq, wkv)[kind]
                        halves = [(lambda r, s=s, n=n: r[:, 2 * s:2 * s + 2, 0:n],
                                   lambda s=s, n=n, c0=c0, wsrc=wsrc: wsrc[2 * s * P:2 * (s + 1) * P, ds(c0.v, n)]
                                   .rearrange("(t p) n -> p t n", p=P)) for s in range(2)]
                        free = ev.at(quad + (p and 1), f"out{1 - p}{kind}")

                        def done(t, p=p, kind=kind, n=n, b=b):
                            dst = (hq, hkv)[kind][:, :, p * n:(p + 1) * n]
                            ev.do("act", lambda: act.copy(dst, ps[:, b:b + 2, 0:n]), t,
                                  tr.at(quad, "tookq" if kind == 0 else "tookk"), tr.at(quad, "tookv"),
                                  name=f"out{p}{kind}")
                        units.append((halves, n, unit_products(xh, xl, 4 * kind, b),
                                      [tq, tk, tg, outs, free], done))
                stream(units, side, step=quad + base)

            def quad_attention(quad):
                step = quad + 1
                hd = Heads(tr, step, HQ)
                here = [ev.at(step, "out10"), ev.at(step, "out11")]
                kv = hkv.rearrange("p t (h c) -> p t h c", h=HQ)
                tv = tr.do("act", lambda: act.copy(v, kv[:, :, :, P:]), here, hd.prior(f"pv{HQ - 1}"), name="tookv")
                qv = hq.rearrange("p t (h c) -> p t h c", h=HQ)
                qr = qv[:, :, :, NOPE:]
                cb, sn = bc(cosb[:, :, :], 2, HQ), bc(sinb[:, :, :], 2, HQ)
                ta = tr.do("dve", lambda: dve.tensor_tensor(t1, qr, cb, ALU.mult), here, la.kpt)
                tr.do("dve", lambda: dve.tensor_tensor(t2[:, :, :, 0:32], qr[:, :, :, 32:64], sn[:, :, :, 0:32], ALU.mult), here)
                tb_ = tr.do("dve", lambda: dve.tensor_tensor(t2[:, :, :, 32:64], qr[:, :, :, 0:32], sn[:, :, :, 32:64], ALU.mult), here)
                t = tr.do("dve", lambda: dve.tensor_tensor(qr, t1, t2, ALU.add), ta, tb_)
                yield
                copies = []
                jobs = [(qv, 0, P, qt, 0, "q"), (qv, 0, P, qt, 2, "q"), (kv, 0, P, kt, 0, "k"), (kv, 0, P, kt, 2, "k"),
                        (qv, NOPE, ROPE, qpt, 0, "p"), (qv, NOPE, ROPE, qpt, 2, "p")]
                for n, (src, c, m, dst, h0, kind) in enumerate(jobs):
                    b = Q + 1 + n % 3

                    def f(src=src, c=c, m=m, h0=h0, b=b):
                        for hh in range(2):
                            for tb in range(TB):
                                r = pe.transpose(ps[0:m, b, (hh * TB + tb) * P:(hh * TB + tb + 1) * P],
                                                 src[:, tb, h0 + hh, c:c + m], ident[:, :])
                        return r
                    tt = tr.do("pe", f, here, t, copies[n - 3] if n >= 3 else
                               [hd.prior(f"pt{HQ - 1}"), hd.prior(f"fin{HQ - 1}")],
                               name={3: "tookk", 5: "tookq"}.get(n),
                               by_itself=(lambda b=b: pe.transpose(ps[:, b, 0:P], ident[:, :], ident[:, :]))
                               if kind == "p" else None)
                    copies.append(tr.do("act", lambda m=m, dst=dst, h0=h0, b=b: act.copy(
                        dst[0:m, h0:h0 + 2], ps[0:m, b, :].rearrange("p (h t) -> p h t", h=2)),
                        tt, hd.prior(f"sc{HQ - 1}")))
                    if n % 2:
                        yield
                for hh in range(HQ):
                    def scores(hh=hh):
                        for tb, (o, n) in enumerate(((0, P), (P, S))):
                            out_ = ps[:, Q, o:o + n]
                            pe.matmul(out_, qt[:, hh, tb * P:(tb + 1) * P], kt[:, hh, 0:n], start=True, stop=False)
                            m = pe.matmul(out_, qpt[0:ROPE, hh, tb * P:(tb + 1) * P], kpt[0:ROPE, 0:n],
                                          start=False, stop=True)
                        return m

                    def pv(hh=hh):
                        for tb in range(TB):
                            for kb in range(tb + 1):
                                m = pe.matmul(ps[:, Q + 2, tb * P:(tb + 1) * P], pt[:, (tb + kb) * P:(tb + kb + 1) * P],
                                              v[:, kb, hh, :], start=kb == 0, stop=kb == tb)
                        return m

                    def fin(rden, hh=hh):
                        for tb in range(TB):
                            c = index(quad) * (HQ * P) + hh * P
                            yy = y[:, tb, ds(c.v, P)]
                            m = dve.scalar_tensor_tensor(out=yy, in0=ps[:, Q + 2, tb * P:(tb + 1) * P],
                                                         scalar=rden[:, tb:tb + 1], in1=yy, op0=ALU.mult, op1=ALU.mult)
                        return m
                    parts = [(ps[:, Q, 0:P], mask[:, 0:P], sm[:, 0:P]), (ps[:, Q, P:3 * P], mask[:, P:], sm[:, P:])]
                    for _ in attend(hd, hh, scores, [copies, tv, la.kpt, t_mask, tg], parts, QH ** -0.5, 3, ps[:, Q + 1, :],
                                    pt, pv, fin, small[:, 16 + 8 * hh:24 + 8 * hh], gap=0):
                        yield

            base = nstep[0]
            nstep[0] += QUADS
            quad_projection(index(0), None, base)
            with pr.loop(1, QUADS) as i:
                side = quad_attention(i + -1)
                for _ in range(4):
                    next(side)
                quad_projection(i, side, base)
                quiet(side)
            quiet(quad_attention(index(QUADS - 1)))
            end = tr.at(QUADS, f"fin{HQ - 1}")
            t = last_product("out1", a["mla_w_out"][0], [end], ALPHA, last)
            return layer_norm(1, t, end)

        def token_rows(tr, dst, src, n, bank, after, free):
            t = tr.do("pe", lambda: [pe.transpose(ps[0:n, bank, tb * P:(tb + 1) * P], src(tb), ident[:, :])
                                     for tb in range(TB)][-1], after, free)
            return tr.do("dve", lambda: dve.tensor_copy(dst, ps[0:n, bank, 0:S]), t)

        def token_cols(tr, dst, src, n, bank, after, free):
            def f():
                for tb in range(TB):
                    m = pe.transpose(ps[:, bank, tb * n:(tb + 1) * n], src[0:n, tb * P:(tb + 1) * P], ident[0:n, 0:n])
                return m
            t = tr.do("pe", f, after, free)
            return tr.do("dve", lambda: dve.tensor_copy(
                dst, ps[:, bank, 0:TB * n].rearrange("p (t n) -> p t n", t=TB)), t)

        def selector(tr, sel, n, after):
            t = tr.do("pool", lambda: pool.memset(sel, 1.0), after)
            return tr.do("pool", lambda: pool.affine_select(
                out=sel, in_=sel, compare_op=ALU.is_equal, fill=0.0, base=0,
                pattern=[[-1, n], [0, P]], channel_multiplier=1), t)

        def ln_of_1_plus_exp(tr, dst, src, tmp, after, sign):
            t = tr.do("dve", lambda: dve.tensor_scalar(tmp, src, -1.0, None, ALU.mult), after)
            t = tr.do("dve", lambda: dve.tensor_tensor(tmp, tmp, src, ALU.min), t)
            t = tr.do("act", lambda: act.activation(tmp, tmp, ACT.Exp), t)
            t = tr.do("act", lambda: act.activation(tmp, tmp, ACT.Ln, bias=1.0), t)
            t2 = tr.do("dve", lambda: dve.tensor_scalar(dst, src, sign, 0.0, ALU.mult, ALU.max), after, t)
            return tr.do("dve", lambda: dve.tensor_tensor(dst, dst, tmp, ALU.add), t, t2)

        def layer2(ready, last):
            HA, W = 8, 1024
            HB, DB = 4, 256
            c_ = Carve()
            bias = c_(HA, 3 * P)
            braw = c_(HA, 3 * P)
            scratch = c_(TB, N)
            hqk = c_(2, TB, HALF)
            hv = c_(TB, HALF)
            v = c_(TB, HALF)
            sq = c_(2, TB, HALF)
            qt, kt = c_(2, S), c_(2, S)
            sm, pt = c_(3 * P), c_(3 * P)
            maskt = c_(3 * P)
            gif = c_(TB, 2 * HB)
            li, lf, tmp = c_(TB, HB), c_(TB, HB), c_(TB, HB)
            ifb = c_(2 * HB)
            rli, rlf, rb, ra, rm, rone = c_(S), c_(S), c_(S), c_(S), c_(S), c_(S)
            acol, ecol = c_(TB, HB), c_(TB, HB)
            sel = c_(HB, P)
            gq = c_(1)
            hbias = c_(2, 3 * P)
            w = a["ev_w_in_2"][0]
            rbias = a["ev_rel_bias_2"]
            NB = rbias.shape[2]
            tb_ = load("relb", braw, lambda: bass.AP(rbias.tensor, rbias.offset + 1, [[1, P], [NB, HA], [1, 3 * P]]), ready)
            t_ifb = load("ifb", ifb, lambda: row(a["ev_if_bias_2"], 2 * HB), ready)
            tr = pr.track("const2")
            for blk, (o, n) in enumerate(((0, P), (P, S))):
                off = braw.offset + (2 * P - 1 if blk == 0 else 3 * P - 1)
                rev = bass.AP(braw.tensor, off, [list(braw.ap[0]), [3 * P, HA], [-1, n]])
                t_bias = tr.do("dve", lambda o=o, n=n, rev=rev: dve.tensor_copy(bias[:, :, o:o + n], rev), tb_, ready)
            for o in (64, P + P + 64):
                t_bias = tr.do("dve", lambda o=o: dve.memset(bias[0:64, :, o:o + 64], NEG), t_bias)
            t = tr.do("pool", lambda: pool.memset(maskt, 0.0), ready)
            for o in (0, 2 * P):
                t = tr.do("pool", lambda o=o: pool.affine_select(
                    out=maskt[:, o:o + P], in_=maskt[:, o:o + P], compare_op=ALU.is_ge, fill=NEG, base=0,
                    pattern=[[1, P]], channel_multiplier=-1), t)
            t_maskt = t
            t_sel = selector(tr, sel[0:HB], HB, ready)
            t_one = tr.do("pool", lambda: pool.memset(rone[0:HB], 1.0), ready)
            t_gq = tr.do("dve", lambda: dve.tensor_scalar(gq, vcol("qn", 1), P ** -0.5, None, ALU.mult), ready)

            t = rms_scale("rms2", ready, None)
            tx = transposed(pr.track("xt2"), lambda tb, k: y[:, tb, k * P:(k + 1) * P], KT, xh, xl, t,
                            gain=vcol("ev", KT))
            ev, tr = pr.track("ev2"), pr.track("att2")
            PAIRS = HA // 2

            def pair_projection(pair, side, base, between=None):
                ev.begin(pair + 1)
                tm = project(w, [(pair * HALF, HALF), (pair * HALF + W, HALF)], 0,
                             [tx, ev.at(pair, "outq")], side, step=(pair * 2) + base)
                ev.do("act", lambda: act.copy(hqk.rearrange("p b t c -> p t b c"),
                                              ps[:, 0:2, :].rearrange("p t (b c) -> p t b c", b=2)),
                      tm, tr.at(pair, "tookk"), name="outq")
                tm = project(w, [(pair * HALF + 2 * W, HALF), (pair * HALF + 3 * W, HALF)], 2,
                             [tx, ev.at(pair, "outv"), ev.at(pair, "gate")], side, step=(pair * 2) + (base + 1))
                tv = ev.do("act", lambda: act.copy(hv, ps[:, 2:4, 0:HALF]), tm, tr.at(pair, "tookv"), name="outv")
                gate_out(ev, "gate", ps[:, 2:4, HALF:N], pair * HALF, HALF, tm,
                         scratch[:, :, 0:HALF], ev.at(pair, "gate"))

            def pair_attention(pair):
                step = pair + 1
                hd = Heads(tr, step, 2)
                here = [ev.at(step, "outq"), ev.at(step, "outv"), ev.at(step, "gate")]
                tv = tr.do("act", lambda: act.copy(v, hv), here, hd.prior("pv1"), name="tookv")
                t_hb = tr.do("dve", lambda: dve.tensor_copy(hbias, bias[:, ds((index(pair) * 2).v, 2), :]),
                             t_bias, hd.prior("mask1"))
                t = tr.do("act", lambda: act.activation(sq, hqk, ACT.Square), here)
                t = tr.do("dve", lambda: dve.tensor_reduce(
                    small[:, 32:40], sq.rearrange("p b t (h d) -> p (b t h) d", h=2), AX.X, ALU.add), t)
                yield
                t = root_inverse(tr, small[:, 40:48], small[:, 32:40], 8, EPS, 1.0 / P, t)
                yield
                xv = hqk.rearrange("p b t (h d) -> p (b t h) d", h=2)
                t = tr.do("dve", lambda: dve.tensor_tensor(xv, xv, bc(small[:, 40:48], 2, P), ALU.mult), t)
                yield
                copies = []
                for n, (dst, g) in enumerate(((qt, gq), (kt, vcol("kn", 1)))):
                    def f(n=n):
                        for hh in range(2):
                            for tb in range(TB):
                                m = pe.transpose(ps[:, Q + 2 + n, (hh * TB + tb) * P:(hh * TB + tb + 1) * P],
                                                 hqk[:, n, tb, hh * P:(hh + 1) * P], ident[:, :])
                        return m
                    tt = tr.do("pe", f, t, hd.prior("fin1"), hd.prior("copy"), name="tookk" if n else None)
                    copies.append(tr.do("act", lambda n=n, dst=dst, g=g: act.activation(
                        dst, ps[:, Q + 2 + n, :].rearrange("p (h t) -> p h t", h=2), ACT.Copy, scale=g),
                        tt, t_gq, hd.prior("sc1"), name="copy"))
                yield
                for hh in range(2):
                    def scores(hh=hh):
                        for tb, (o, n) in enumerate(((0, P), (P, S))):
                            m = pe.matmul(ps[:, Q, o:o + n], qt[:, hh, tb * P:(tb + 1) * P], kt[:, hh, 0:n],
                                          start=True, stop=True)
                        return m

                    def pv(hh=hh):
                        for tb in range(TB):
                            for kb in range(tb + 1):
                                m = pe.matmul(ps[:, Q + 2, tb * P:(tb + 1) * P], pt[:, (tb + kb) * P:(tb + kb + 1) * P],
                                              v[:, kb, hh * P:(hh + 1) * P], start=kb == 0, stop=kb == tb)
                        return m

                    def fin(rden, hh=hh):
                        for tb in range(TB):
                            c = index(pair) * HALF + hh * P
                            yy = y[:, tb, ds(c.v, P)]
                            m = dve.scalar_tensor_tensor(out=yy, in0=ps[:, Q + 2, tb * P:(tb + 1) * P],
                                                         scalar=rden[:, tb:tb + 1], in1=yy, op0=ALU.mult, op1=ALU.mult)
                        return m
                    parts = [(ps[:, Q, 0:P], hbias[:, hh, 0:P], sm[:, 0:P]),
                             (ps[:, Q, P:3 * P], hbias[:, hh, P:], sm[:, P:])]
                    for _ in attend(hd, hh, scores, [copies, tv, t_hb], parts, 1.0, 3, ps[:, Q + 1, :],
                                    pt, pv, fin, small[:, 16 + 8 * hh:24 + 8 * hh], gap=0):
                        yield

            base = nstep[0]
            nstep[0] += 2 * PAIRS
            pair_projection(index(0), None, base)
            with pr.loop(1, PAIRS) as i:
                side = pair_attention(i + -1)
                for _ in range(4):
                    next(side)
                pair_projection(i, side, base)
                quiet(side)

            def gate_vectors():
                g = pr.track("mg")
                t = g.do("act", lambda: act.copy(gif, ps[:, 0:2, 0:2 * HB]), tgm, ready)
                mgate["read"] = t
                t = g.do("dve", lambda: dve.tensor_tensor(gif, gif, bc(ifb, 1, TB), ALU.add), t, t_ifb)
                yield
                t = g.do("dve", lambda: dve.tensor_copy(li, gif[:, :, 0:HB]), t)
                t = ln_of_1_plus_exp(g, lf, gif[:, :, HB:], tmp, t, -1.0)
                yield
                t1 = token_rows(g, rli[0:HB], lambda tb: li[:, tb], HB, Q + 3, t, side_end())
                t2 = token_rows(g, rlf[0:HB], lambda tb: lf[:, tb], HB, Q + 3, t1, None)
                yield
                t = g.do("dve", lambda: dve.tensor_tensor_scan(
                    rb[0:HB], rone[0:HB], rlf[0:HB], 0.0, ALU.mult, ALU.subtract), t2, t_one)
                t = g.do("dve", lambda: dve.tensor_tensor(ra[0:HB], rli[0:HB], rb[0:HB], ALU.subtract), t, t1)
                t = g.do("dve", lambda: dve.tensor_tensor_scan(
                    rm[0:HB], ra[0:HB], ra[0:HB], 0.0, ALU.max, ALU.max), t)
                t = g.do("dve", lambda: dve.tensor_tensor(rb[0:HB], rb[0:HB], rm[0:HB], ALU.add), t)
                yield
                t3 = token_cols(g, acol, ra, HB, Q + 3, t, t2)
                t4 = token_cols(g, ecol, rb, HB, Q + 3, t, t3)
                mgate["t"] = [g.do("act", lambda: act.activation(ecol, ecol, ACT.Exp, scale=-1.0), t4), t3, t]
                yield

            mgate = {}
            side = pair_attention(index(PAIRS - 1))
            side_end = lambda: tr.at(PAIRS, "fin1")
            for _ in range(4):
                next(side)
            tgm = project(w, [(9 * W, 2 * HB)], 0, [tx, ev.at(PAIRS, "outq"), ev.at(PAIRS, "outv")], side)
            quiet(side)
            gv = gate_vectors()
            next(gv)
            tz = gates("gate2", w, 8 * W, W, 2, [tx, mgate["read"], ev.at(PAIRS, "gate"), ev.at(PAIRS, "outv")],
                       scratch, gv)
            quiet(gv)

            c_ = Carve()
            mqk = c_(TB, 2 * DB)
            hvo = c_(TB, 2 * DB)
            va = c_(TB, DB + 1)
            mqt, mkt = c_(2, S), c_(2, S)
            wt = c_(3 * P)
            sT = c_(3 * P)
            assert c_.at <= 2 * HA * 3 * P
            em, tm_ = pr.track("ev2m"), pr.track("mlstm")
            t_va = pr.track("va").do("pool", lambda: pool.memset(va[:, :, DB:], 1.0), side_end())

            def head_projection(head, side, base):
                em.begin(head + 1)
                tm = project(w, [(head * DB + 4 * W, DB), (head * DB + 5 * W, DB)], 0,
                             [tx, em.at(head, "outq"), mgate["read"], tz], side, step=(head * 2) + base)
                em.do("act", lambda: act.copy(mqk, ps[:, 0:2, :]), tm, tm_.at(head, "tookk"), side_end(), name="outq")
                tm = project(w, [(head * DB + 6 * W, DB), (head * DB + 7 * W, DB)], 2,
                             [tx, em.at(head, "outv"), tz], side, step=(head * 2) + (base + 1))
                em.do("act", lambda: act.copy(hvo[:, :, 0:DB], ps[:, 2:4, 0:DB]), tm, tm_.at(head, "tookv"), side_end())
                em.do("act", lambda: act.activation(hvo[:, :, DB:], ps[:, 2:4, DB:], ACT.Tanh, scale=0.5),
                      tm, tm_.at(head, "tooko"), name="outv")

            def head_mlstm(head):
                step = head + 1
                tr = tm_
                tr.begin(step)
                prior = lambda n: tr.at(index(step) + -1, n)
                here = [em.at(step, "outq"), em.at(step, "outv")]
                c = index(head) * DB + W
                tv = tr.do("act", lambda: act.copy(va[:, :, 0:DB], hvo[:, :, 0:DB]), here, t_va, prior("pv"), name="tookv")
                tg = tr.do("dve", lambda: dve.scalar_tensor_tensor(
                    out=y[:, :, ds(c.v, DB)], in0=hvo[:, :, DB:], scalar=1.0, in1=y[:, :, ds(c.v, DB)],
                    op0=ALU.add, op1=ALU.mult), here, tz, name="tooko")
                copies = []
                for n, dst in enumerate((mqt, mkt)):
                    def f(n=n):
                        for kd in range(2):
                            for tb in range(TB):
                                o = n * DB + kd * P
                                m = pe.transpose(ps[:, Q + n, (kd * TB + tb) * P:(kd * TB + tb + 1) * P],
                                                 mqk[:, tb, o:o + P], ident[:, :])
                        return m
                    tt = tr.do("pe", f, here, prior("wt") if n == 0 else prior("st"), prior("fin"),
                               name="tookk" if n else None)
                    copies.append(tr.do("act", lambda n=n, dst=dst: act.activation(
                        dst, ps[:, Q + n, :].rearrange("p (k t) -> p k t", k=2), ACT.Copy,
                        scale=DB ** -0.5 if n == 0 else 1.0), tt, prior("sc"), name=f"copy{n}"))
                yield
                tsel = tr.do("dve", lambda: dve.tensor_copy(selh, sel[0:HB, ds(index(head).v, 1), :]
                                                            .rearrange("p a b -> p (a b)")),
                             t_sel, mgate["t"], prior("wt"))
                t = tr.do("pe", lambda: pe.matmul(ps[:, Q, 0:S], selh, rm[0:HB], start=True, stop=True),
                          copies, tsel, mgate["t"])
                t1 = tr.do("dve", lambda: dve.scalar_tensor_tensor(
                    out=wt[:, 0:S], in0=ps[:, Q, 0:S], scalar=-1.0, in1=maskt[:, 0:S], op0=ALU.mult, op1=ALU.add),
                    t, t_maskt, prior("st"))
                t2 = tr.do("dve", lambda: dve.scalar_tensor_tensor(
                    out=wt[:, S:], in0=ps[:, Q, P:S], scalar=-1.0, in1=maskt[:, S:], op0=ALU.mult, op1=ALU.add),
                    t, t_maskt, prior("st"), name="wt")
                ac = lambda tb: acolh[:, tb:tb + 1]
                tac = tr.do("dve", lambda: dve.tensor_copy(
                    headcols[:, 0:2], acol[:, :, ds(index(head).v, 1)]
                    .rearrange("p t a -> p (t a)")), mgate["t"], prior("fin"), prior("exp"))
                tec = tr.do("dve", lambda: dve.tensor_copy(
                    headcols[:, 2:4], ecol[:, :, ds(index(head).v, 1)]
                    .rearrange("p t a -> p (t a)")), mgate["t"], prior("fin"))
                te = tr.do("act", lambda: act.activation(wt[:, 0:S], wt[:, 0:S], ACT.Exp, bias=ac(0)), t1, tac)
                te = tr.do("act", lambda: act.activation(wt[:, S:], wt[:, S:], ACT.Exp, bias=ac(1)), t2, tac, name="exp")

                def scores():
                    for kb, (o, n, t0) in enumerate(((0, S, 0), (S, P, P))):
                        for kd in range(2):
                            m = pe.matmul(ps[:, Q + 1, o:o + n], mkt[:, kd, kb * P:(kb + 1) * P], mqt[:, kd, t0:t0 + n],
                                          start=kd == 0, stop=kd == 1)
                    return m
                t = tr.do("pe", scores, copies, name="sc")
                tst = tr.do("dve", lambda: dve.tensor_tensor(sT, ps[:, Q + 1, 0:3 * P], wt, ALU.mult), t, te,
                            prior("pv"), name="st")
                yield
                yield

                def pv():
                    for tb in range(TB):
                        for kb in range(tb + 1):
                            o = tb * P if kb == 0 else S
                            m = pe.matmul(ps[:, Q + 2 + tb, 0:DB + 1], sT[:, o:o + P], va[:, kb, :],
                                          start=kb == 0, stop=kb == tb)
                    return m
                tp = tr.do("pe", pv, tst, tv, prior("fin"), name="pv")
                den, neg = headcols[:, 4:6], headcols[:, 6:8]
                dsrc = ps[:, Q + 2:Q + 4, DB]
                t = tr.do("dve", lambda: dve.tensor_copy(den, dsrc), tp)
                t = tr.do("dve", lambda: dve.tensor_scalar(neg, den, -1.0, None, ALU.mult), t)
                t = tr.do("dve", lambda: dve.tensor_tensor(den, den, neg, ALU.max), t)
                t = tr.do("dve", lambda: dve.tensor_tensor(den, den, headcols[:, 2:4], ALU.max), t, tec)
                t = tr.do("dve", lambda: dve.tensor_scalar(den, den, 2.0, None, ALU.mult), t)
                t = tr.do("dve", lambda: dve.reciprocal(den, den), t)
                for tb in range(TB):
                    tf = tr.do("dve", lambda tb=tb: dve.scalar_tensor_tensor(
                        out=y[:, tb, ds(c.v, DB)], in0=ps[:, Q + 2 + tb, 0:DB], scalar=den[:, tb:tb + 1],
                        in1=y[:, tb, ds(c.v, DB)], op0=ALU.mult, op1=ALU.mult), t, tg, tp, name="fin")
                yield

            headcols = small[:, 64:72]
            acolh = headcols[:, 0:2]
            selh = rlf[0:HB, 0:P]
            base = nstep[0]
            nstep[0] += 2 * HB
            head_projection(index(0), None, base)
            with pr.loop(1, HB) as i:
                side = head_mlstm(i + -1)
                next(side)
                head_projection(i, side, base)
                quiet(side)
            quiet(head_mlstm(index(HB - 1)))
            end = [tm_.at(HB, "fin"), side_end()]
            return last_product("out2", a["ev_w_out_2"][0], end, 1.0, last)

        def layer3(ready, last):
            H, W = 8, 1024
            HP = H // 2
            PAD = 4
            c_ = Carve()
            A, L, X = c_(H, S), c_(H, S), c_(H, S)
            hx = c_(TB, HALF)
            cp = c_(2, PAD + S)
            xc = c_(2, S)
            gt = c_(2, S)
            gw = c_(H, 2 * P)
            scratch = c_(TB, HALF)
            sp = c_(H)
            tmp8, hgb = c_(H), c_(2 * H)
            ab = c_(TB, 2 * H)
            alog, dtb = c_(H), c_(H)
            beta, gg, gtmp = c_(TB, H), c_(TB, H), c_(TB, H)
            rg, rdec, rone = c_(S), c_(S), c_(S)
            dcol = c_(TB, H)
            sel = c_(H, P)
            mincl = c_(3 * P)
            strict = c_(P)
            lev = c_(7, P)
            onorm = c_(P)
            w = a["od_w_in_2"][0]

            t_gw = load("gw", gw, lambda: a["od_gate_w_2"][0].rearrange("n c d -> c n d"), ready)
            t_al = load("alog", alog, lambda: row(a["od_a_log_2"], H), ready)
            t_dt = load("dtb", dtb, lambda: row(a["od_dt_bias_2"], H), ready)
            t_on = load("onorm", onorm, lambda: row(a["od_onorm_2"], P), ready)
            tr = pr.track("const3")
            t = tr.do("pool", lambda: pool.memset(mincl, 0.0), ready)
            t = causal(tr, mincl[:, 0:P], P, 0, t)
            t_incl = causal(tr, mincl[:, 2 * P:], P, 0, t)
            t = tr.do("pool", lambda: pool.memset(strict, 1.0), ready)
            t_strict = tr.do("pool", lambda: pool.affine_select(
                out=strict, in_=strict, compare_op=ALU.is_gt, fill=0.0, base=0,
                pattern=[[-1, P]], channel_multiplier=1), t)
            ia, ib = (X[:, n, 0:P].bitcast(I32) for n in (0, 1))
            t = tr.do("pool", lambda: pool.iota(ia, [[0, P]], base=0, channel_multiplier=1), ready)
            t = tr.do("pool", lambda: pool.iota(ib, [[1, P]], base=0, channel_multiplier=0), t)
            t = tr.do("dve", lambda: dve.tensor_tensor(ia, ia, ib, ALU.bitwise_xor), t)
            for l in range(7):
                t = tr.do("dve", lambda l=l: dve.tensor_scalar(ib, ia, l, None, ALU.logical_shift_right), t)
                t = tr.do("dve", lambda l=l: dve.tensor_scalar(lev[:, l], ib, 1.0, None, ALU.is_equal), t)
            t_lev = t
            t_cp = tr.do("pool", lambda: pool.memset(cp[:, :, 0:PAD], 0.0), ready)
            t_sel = selector(tr, sel[0:H], H, ready)
            t_one = tr.do("pool", lambda: pool.memset(rone[0:H], 1.0), ready)
            t = ln_of_1_plus_exp(tr, sp, vcol("lam", H), tmp8, ready, -1.0)
            t_sp = tr.do("dve", lambda: dve.tensor_scalar(sp, sp, 4.0, None, ALU.mult), t)
            t_gb = tr.do("dve", lambda: dve.tensor_scalar(hgb, vcol("gb", 2 * H), 0.5, None, ALU.mult), ready)

            t = rms_scale("rms3", ready, None)
            tx = transposed(pr.track("xt3"), lambda tb, k: y[:, tb, k * P:(k + 1) * P], KT, xh, xl, t,
                            gain=vcol("od", KT))

            def taps(tr, out_, src, wc, bias, after):
                s0 = lambda j: src[:, PAD - 3 + j:PAD - 3 + j + S]
                if bias is None:
                    t = tr.do("dve", lambda: dve.tensor_scalar(out_, s0(0), wc(0), None, ALU.mult), after)
                else:
                    t = tr.do("dve", lambda: dve.tensor_scalar(out_, s0(0), wc(0), bias, ALU.mult, ALU.add), after)
                for j in range(1, 4):
                    t = tr.do("dve", lambda j=j: dve.scalar_tensor_tensor(
                        out=out_, in0=s0(j), scalar=wc(j), in1=out_, op0=ALU.mult, op1=ALU.add), t)
                return t

            ev, rg_ = pr.track("ev3"), pr.track("lru")

            def blocks_projection(pair, side, base, b):
                ev.begin(pair + 1)
                tm = project(w, [(pair * HALF, HALF), (pair * HALF + W, HALF)], b,
                             [tx, ev.at(pair, "gate")], side, step=pair + base)
                ev.do("act", lambda: act.copy(hx, ps[:, b:b + 2, 0:HALF]), tm, rg_.at(pair, "took"), name="out")
                gate_out(ev, "gate", ps[:, b:b + 2, HALF:N], pair * HALF, HALF, tm, scratch, ev.at(pair, "gate"))

            def blocks_lru(pair):
                tr = rg_
                tr.begin(pair + 1)
                prior = lambda n: tr.at(index(pair), n)
                here = [ev.at(pair + 1, "out"), ev.at(pair + 1, "gate")]

                def f():
                    for n in range(2):
                        for tb in range(TB):
                            m = pe.transpose(ps[:, Q, (n * TB + tb) * P:(n * TB + tb + 1) * P],
                                             hx[:, tb, n * P:(n + 1) * P], ident[:, :])
                    return m
                t = tr.do("pe", f, here, prior("cp"), name="took")
                t = tr.do("act", lambda: act.copy(cp[:, :, PAD:], ps[:, Q, :].rearrange("p (n t) -> p n t", n=2)),
                          t, t_cp, prior("conv"), name="cp")
                yield
                hc = small[:, 80:80 + 16]
                o = col["cw"]
                cwv = vec[:, o:o + 32].rearrange("p (j c) -> p c j", c=8)
                bk = lambda: (index(pair) * 2).v
                tcs = [tr.do("dve", lambda: dve.tensor_copy(
                    hc[:, 0:8].rearrange("p (c j) -> p c j", c=2), cwv[:, ds(bk(), 2), :]), prior("conv"), ready),
                    tr.do("dve", lambda: dve.tensor_copy(hc[:, 8:10], vec[:, ds(bk() + col["cb"], 2)]), prior("conv"), ready),
                    tr.do("dve", lambda: dve.tensor_copy(hc[:, 10:12], hgb[:, ds(bk(), 2)]), prior("i1"), t_gb),
                    tr.do("dve", lambda: dve.tensor_copy(hc[:, 12:14], hgb[:, ds(bk() + H, 2)]), prior("i1"), t_gb),
                    tr.do("dve", lambda: dve.tensor_copy(hc[:, 14:16], sp[:, ds(bk(), 2)]), prior("i1"), t_sp)]
                tgc = tr.do("dve", lambda: dve.tensor_copy(gwc, gw[:, ds(bk(), 2), :]), t_gw, prior("gates"))
                for n in range(2):
                    t = taps(tr, xc[:, n], cp[:, n], lambda j, n=n: hc[:, 4 * n + j:4 * n + j + 1],
                             hc[:, 8 + n:9 + n], [t, tcs, prior("gates"), prior("ix")])
                tconv = tr.do("dve", lambda: dve.memset(small[:, 254:255], 0.0), t, name="conv")
                yield
                for n in range(2):
                    bank = Q + 1 + n

                    def g(n=n, bank=bank):
                        for s in range(2):
                            m = pe.matmul(ps[:, bank, s * S:(s + 1) * S], gwc[:, n, s * P:(s + 1) * P], xc[:, n],
                                          start=True, stop=True)
                        return m
                    t = tr.do("pe", g, tconv, tgc, prior("i1"), name="gates")
                    blk = lambda buf, n=n: buf[:, ds((index(pair) * 2 + n).v, 1), :].rearrange("p a b -> p (a b)")
                    t1 = tr.do("act", lambda n=n, bank=bank: act.activation(
                        gt[:, 0], ps[:, bank, 0:S], ACT.Tanh, scale=0.5, bias=hc[:, 10 + n:11 + n]), t,
                        gfree[0] if n else prior("ix"))
                    t2 = tr.do("act", lambda n=n, bank=bank: act.activation(
                        gt[:, 1], ps[:, bank, S:N], ACT.Tanh, scale=0.5, bias=hc[:, 12 + n:13 + n]), t,
                        gfree[0] if n else prior("ix"), name="i1")
                    t3 = tr.do("dve", lambda n=n, blk=blk: dve.tensor_scalar(
                        blk(L), gt[:, 0], 1.0, hc[:, 14 + n:15 + n], ALU.add, ALU.mult), t1, t_lev)
                    t4 = tr.do("act", lambda blk=blk: act.activation(blk(A), blk(L), ACT.Exp, scale=-1.0), t3,
                               by_itself=carry)
                    gfree[0] = tr.do("dve", lambda n=n, blk=blk: dve.scalar_tensor_tensor(
                        out=blk(X), in0=gt[:, 1], scalar=1.0, in1=xc[:, n], op0=ALU.add, op1=ALU.mult),
                        t2, t_lev, name="ix")
                    tr.do("act", lambda blk=blk: act.activation(blk(L), blk(L), ACT.Tanh), t3, t4, name="th",
                          by_itself=carry)
                    yield
            gfree = [None]
            carry = lambda: act.copy(small[:, 252:253], ones[:, 0:1])
            gwc = c_(2, 2 * P)
            base = nstep[0]
            nstep[0] += HP
            blocks_projection(index(0), None, base, 0)
            with pr.loop(1, HP) as i:
                side = blocks_lru(i + -1)
                next(side)
                blocks_projection(i, side, base, 0)
                quiet(side)
            side = blocks_lru(index(HP - 1))

            tgm = project(w, [(6 * W, 2 * H)], 2, [tx], side)
            quiet(side)
            lru_t = [rg_.at(HP, n) for n in ("th", "ix", "i1")]

            def recurrence():
                tr = pr.track("scan")
                v = lambda buf, g: buf[:, 4 * g:4 * g + 4].rearrange("p a b -> p (a b)")
                ts = []
                for g in range(2):
                    t = tr.do("dve", lambda g=g: dve.tensor_scalar(v(tw, 0), v(L, g), 1.0, None, ALU.add), lru_t,
                              ts[-1] if ts else None)
                    t = tr.do("dve", lambda g=g: dve.reciprocal(v(tw, 0), v(tw, 0)), t)
                    t = tr.do("dve", lambda g=g: dve.scalar_tensor_tensor(
                        out=v(L, g), in0=v(L, g), scalar=2.0, in1=v(tw, 0), op0=ALU.mult, op1=ALU.mult), t)
                    ts.append(t)
                    yield
                t = tr.do("act", lambda: act.activation(
                    L.rearrange("p a b -> p (a b)"), L.rearrange("p a b -> p (a b)"), ACT.Sqrt), ts)
                yield
                last_ = None
                for n in range(H):
                    t1 = tr.do("dve", lambda n=n: dve.scalar_tensor_tensor(
                        out=X[:, n], in0=X[:, n], scalar=0.5, in1=L[:, n], op0=ALU.mult, op1=ALU.mult), t)
                    t2 = tr.do("dve", lambda n=n: dve.tensor_tensor_scan(
                        L[:, n], A[:, n], X[:, n], 0.0, ALU.mult, ALU.add), t1)
                    if n % 2:
                        yield

                        def f(n=n):
                            for l in range(2):
                                for tb in range(TB):
                                    o = (tb * TB + l) * P
                                    m = pe.transpose(ps[:, Q + 3, o:o + P],
                                                     L[:, n - 1 + l, tb * P:(tb + 1) * P], ident[:, :])
                            return m
                        t3 = tr.do("pe", f, t2, last_)
                        last_ = tr.do("dve", lambda n=n: dve.tensor_tensor(
                            y[:, :, (n - 1) * P:(n + 1) * P], ps[:, Q + 3, :].rearrange("p (t c) -> p t c", t=TB),
                            y[:, :, (n - 1) * P:(n + 1) * P], ALU.mult), t3, ev.at(HP, "gate"))
                        yield
                done3["scan"] = last_

            tw = c_(4, S)
            done3 = {}

            def delta_gates():
                tr = pr.track("dg")
                t = tr.do("act", lambda: act.copy(ab, ps[:, 2:4, 0:2 * H]), tgm, ready)
                done3["read"] = t
                tbt = tr.do("act", lambda: act.activation(beta, ab[:, :, H:], ACT.Tanh, scale=0.5), t)
                tbt = tr.do("dve", lambda: dve.tensor_scalar(beta, beta, 0.5, 0.5, ALU.mult, ALU.add), tbt)
                te = tr.do("act", lambda: act.activation(alog, alog, ACT.Exp), t_al)
                t = tr.do("dve", lambda: dve.tensor_tensor(ab[:, :, 0:H], ab[:, :, 0:H], bc(dtb, 1, TB), ALU.add), t, t_dt)
                yield
                t = ln_of_1_plus_exp(tr, gg, ab[:, :, 0:H], gtmp, t, 1.0)
                t = tr.do("dve", lambda: dve.tensor_tensor(gg, gg, bc(alog, 1, TB), ALU.mult), t, te)
                yield
                t = token_rows(tr, rg[0:H], lambda tb: gg[:, tb], H, Q + 2, t, lru_t)
                for tb in range(TB):
                    o = slice(tb * P, (tb + 1) * P)
                    t = tr.do("dve", lambda o=o: dve.tensor_tensor_scan(
                        rdec[0:H, o], rone[0:H, o], rg[0:H, o], 0.0, ALU.mult, ALU.subtract), t, t_one)
                yield
                done3["t"] = [token_cols(tr, dcol, rdec, H, Q + 2, t, None), t, tbt]
                yield

            hh4 = c_(3, TB, HALF)
            selc = c_(2, P)
            c_ = Carve()
            cpd = c_(6, PAD + S)
            QT, KTt, VT = c_(2, S), c_(2, S), c_(2, S)
            E = c_(2, 3 * P)
            u = c_(2, TB, P)
            TRN = c_(2, 4 * P)
            AD = c_(4, P)
            M, Mt, Z, B = c_(4, P), c_(4, P), c_(4, P), c_(4, P)
            assert c_.at <= 3 * H * S + TB * HALF + 2 * (PAD + S) + 4 * S
            evd, dl = pr.track("evd"), pr.track("delta")

            def delta_projection(pair, side, base):
                evd.begin(pair + 1)
                tm = project(w, [(pair * HALF + 2 * W, HALF), (pair * HALF + 3 * W, HALF)], 0,
                             [tx, evd.at(pair, "outq"), done3["read"], ev.at(HP, "gate")], side, step=(pair * 2) + base)
                evd.do("act", lambda: act.copy(hh4[:, 0:2].rearrange("p b t c -> p t b c"),
                                               ps[:, 0:2, :].rearrange("p t (b c) -> p t b c", b=2)),
                       tm, dl.at(pair, "took"), name="outq")
                tm = project(w, [(pair * HALF + 4 * W, HALF), (pair * HALF + 5 * W, HALF)], 2,
                             [tx, evd.at(pair, "gate"), done3["read"]], side, step=(pair * 2) + (base + 1))
                evd.do("act", lambda: act.copy(hh4[:, 2], ps[:, 2:4, 0:HALF]), tm, dl.at(pair, "took"), name="outv")
                gate_out(evd, "gate", ps[:, 2:4, HALF:N], pair * HALF + W, HALF, tm, scratch,
                         evd.at(pair, "gate"))

            def delta_heads(pair):
                tr = dl
                tr.begin(pair + 1)
                prior = lambda n: tr.at(index(pair), n)
                here = [evd.at(pair + 1, "outq"), evd.at(pair + 1, "outv"), evd.at(pair + 1, "gate")]
                hidx = lambda: (index(pair) * 2).v
                cps = []
                for n in range(3):
                    bank = Q + n % 2

                    def f(n=n, bank=bank):
                        for hh in range(2):
                            for tb in range(TB):
                                m = pe.transpose(ps[:, bank, (hh * TB + tb) * P:(hh * TB + tb + 1) * P],
                                                 hh4[:, n, tb, hh * P:(hh + 1) * P], ident[:, :])
                        return m
                    t = tr.do("pe", f, here, cps[0] if n == 2 else [prior("od1"), prior("qk1"), prior("lvl")],
                              name="took")
                    cps.append(tr.do("act", lambda n=n, bank=bank: act.copy(
                        cpd[:, 2 * n:2 * n + 2, PAD:], ps[:, bank, :].rearrange("p (h t) -> p h t", h=2)),
                        t, t_cpd, prior("conv")))
                yield
                hc = small[:, 100:140]
                cdv = vec[:, 0:96].rearrange("p (j c) -> p c j", c=24)
                tcs = [tr.do("dve", lambda n=n: dve.tensor_copy(
                    hc[:, 8 * n:8 * n + 8].rearrange("p (c j) -> p c j", c=2),
                    cdv[:, ds(hidx() + 8 * n, 2), :]), prior("conv"), ready) for n in range(3)]
                tcs += [tr.do("dve", lambda o=o, src=src: dve.tensor_copy(
                    hc[:, o:o + 4].rearrange("p (t c) -> p t c", t=TB), src[:, :, ds(hidx(), 2)]),
                    prior("fin1"), prior("E1"), done3["t"]) for o, src in ((24, beta), (28, dcol))]
                tsel = tr.do("dve", lambda: dve.tensor_copy(selc[0:H], sel[0:H, ds(hidx(), 2), :]), t_sel, prior("R1"))
                bcol = lambda hh, tb: hc[:, 24 + 2 * tb + hh:25 + 2 * tb + hh]
                dec = lambda hh, tb: hc[:, 28 + 2 * tb + hh:29 + 2 * tb + hh]
                dsts = (QT, KTt, VT)
                outs_ = []
                for n in range(3):
                    for hh in range(2):
                        c = 2 * n + hh
                        dst = dsts[n][:, hh]
                        t = taps(tr, dst, cpd[:, c], lambda j, c=c: hc[:, 4 * c + j:4 * c + j + 1], None,
                                 [cps, tcs, prior("kk1"), prior("qk1"), prior("vt")])
                        if n == 2 and hh == 1:
                            tr.do("dve", lambda: dve.memset(small[:, 253:254], 0.0), t, name="conv")
                        s_ = E.rearrange("p a b -> p (a b)")[:, 0:S] if hh == 0 else \
                            TRN.rearrange("p a b -> p (a b)")[:, 0:S]
                        t1 = tr.do("act", lambda dst=dst, s_=s_: act.activation(s_, dst, ACT.Tanh, scale=0.5),
                                   t, outs_[-2] if len(outs_) > 1 else [prior("st"), prior("uu"), prior("od1")])
                        t2 = tr.do("dve", lambda dst=dst, s_=s_: dve.scalar_tensor_tensor(
                            out=dst, in0=s_, scalar=1.0, in1=dst, op0=ALU.add, op1=ALU.mult), t1)
                        outs_.append(tr.do("dve", lambda dst=dst: dve.tensor_scalar(
                            dst, dst, 0.5, None, ALU.mult), t2))
                    yield
                for n in range(2):
                    ts_ = tr.do("act", lambda n=n: act.activation(
                        (M if n == 0 else Mt).rearrange("p a b -> p (a b)"),
                        dsts[n].rearrange("p a b -> p (a b)"), ACT.Square), outs_, prior("lvl"), prior("uu"))
                yield

                def ssq():
                    for n, m_ in enumerate((M, Mt)):
                        for k in range(4):
                            r = pe.matmul(ps[:, Q, 4 * n + k:4 * n + k + 1], m_[:, k, :], ones[:, 0:1],
                                          start=True, stop=True)
                    return r
                t = tr.do("pe", ssq, ts_, cps)
                def vturn():
                    for hh in range(2):
                        for tb in range(TB):
                            m = pe.transpose(ps[:, Q + 1, (hh * TB + tb) * P:(hh * TB + tb + 1) * P],
                                             VT[:, hh, tb * P:(tb + 1) * P], ident[:, :])
                    return m
                tvt = tr.do("pe", vturn, outs_, cps, name="vt")
                sc = small[:, 144:176]
                t = tr.do("dve", lambda: dve.tensor_scalar(sc[:, 0:8], ps[:, Q, 0:8], EPS, None, ALU.add), t, prior("fin1"))
                t = tr.do("pool", lambda: pool.tensor_tensor(sc[:, 0:8], sc[:, 0:8], nhalf[:, 0:8], ALU.pow), t)
                yield
                bh = hc[:, 24:28].rearrange("p (t h) -> p h t", t=TB)
                rk = sc[:, 4:8].rearrange("p (h t) -> p h t", h=2)
                rb_ = sc[:, 8:12].rearrange("p (h t) -> p h t", h=2)
                c2 = sc[:, 12:16].rearrange("p (h t) -> p h t", h=2)
                t1 = tr.do("dve", lambda: dve.tensor_tensor(rb_, rk, bh, ALU.mult), t, tcs)
                t2 = tr.do("dve", lambda: dve.tensor_tensor(c2, rk, rb_, ALU.mult), t1)
                rq = tr.do("dve", lambda: dve.tensor_scalar(sc[:, 16:20], sc[:, 0:4], P ** -0.5, None, ALU.mult), t)
                tu = tr.do("dve", lambda: dve.tensor_tensor(
                    u.rearrange("p h t d -> p (h t) d"), ps[:, Q + 1, :].rearrange("p (k d) -> p k d", k=4),
                    bc(sc[:, 8:12], 2, P), ALU.mult), t1, tvt, prior("od1"), prior("uu"))
                yield
                for hh in range(2):
                    t = tr.do("pe", lambda hh=hh: pe.matmul(ps[:, Q, 0:S], selc[0:H, hh, :], rdec[0:H],
                                                            start=True, stop=True),
                              tsel, done3["t"], tu, prior("lvl"), dfree[0] if hh else None, name=f"R{hh}")
                    td = tr.do("dve", lambda hh=hh: dve.tensor_tensor(
                        sc[:, 20:21], ps[:, Q, P - 1:P], dec(hh, 1), ALU.add), t, tcs, dfree[0] if hh else None)
                    e0 = E[:, hh]
                    te = tr.do("dve", lambda hh=hh, e0=e0: dve.scalar_tensor_tensor(
                        out=e0[:, 0:P], in0=ps[:, Q, 0:P], scalar=-1.0, in1=mincl[:, 0:P],
                        op0=ALU.mult, op1=ALU.add), t, t_incl, outs_)
                    te = tr.do("dve", lambda hh=hh, e0=e0: dve.tensor_scalar(
                        e0[:, P:S], ps[:, Q, 0:P], -1.0, None, ALU.mult), t, outs_)
                    te = tr.do("dve", lambda hh=hh, e0=e0: dve.scalar_tensor_tensor(
                        out=e0[:, S:], in0=ps[:, Q, P:S], scalar=-1.0, in1=mincl[:, S:],
                        op0=ALU.mult, op1=ALU.add), t, t_incl, outs_)
                    for n, bcol_ in enumerate((dec(hh, 0), sc[:, 20:21], dec(hh, 1))):
                        te2 = tr.do("act", lambda n=n, e0=e0, bcol_=bcol_: act.activation(
                            e0[:, n * P:(n + 1) * P], e0[:, n * P:(n + 1) * P], ACT.Exp, bias=bcol_), te, td, tcs,
                            name=f"E{hh}")

                    def kk(hh=hh, other=KTt, bank=Q + 1):
                        pe.matmul(ps[:, bank, 0:P], other[:, hh, 0:P], KTt[:, hh, 0:P], start=True, stop=True)
                        return pe.matmul(ps[:, bank, P:3 * P], other[:, hh, P:S], KTt[:, hh, :], start=True, stop=True)
                    tk = tr.do("pe", kk, outs_, tu, name=f"kk{hh}")
                    tq_ = tr.do("pe", lambda kk=kk: kk(other=QT, bank=Q + 2), outs_, prior("od1"), dfree[1] if hh else None,
                                name=f"qk{hh}")
                    yield
                    ta_ = []
                    T4 = TRN[:, hh]
                    for n, (s0, cc_) in enumerate(((0, 0), (1, 1), (2, 1))):
                        col_ = sc[:, 12 + 2 * hh + cc_:13 + 2 * hh + cc_]
                        dst = AD[:, 2 * hh] if n == 0 else (AD[:, 2 * hh + 1] if n == 2 else T4[:, 0:P])
                        ta_.append(tr.do("dve", lambda n=n, dst=dst, col_=col_, e0=e0: dve.scalar_tensor_tensor(
                            out=dst, in0=ps[:, Q + 1, n * P:(n + 1) * P], scalar=col_, in1=e0[:, n * P:(n + 1) * P],
                            op0=ALU.mult, op1=ALU.mult), tk, te2, t2, outs_))
                    for n in range(2):
                        ta_.append(tr.do("dve", lambda n=n, hh=hh: dve.tensor_tensor(
                            AD[:, 2 * hh + n], AD[:, 2 * hh + n], strict, ALU.mult), ta_[0], ta_[2], t_strict))
                    tqk = tr.do("dve", lambda hh=hh, T4=T4, e0=e0: dve.tensor_tensor(
                        T4[:, P:], ps[:, Q + 2, 0:3 * P], e0, ALU.mult), tq_, te2, outs_)
                    yield

                    def turn4(T4=T4):
                        for n in range(4):
                            m = pe.transpose(ps[:, Q + 3, n * P:(n + 1) * P], T4[:, n * P:(n + 1) * P], ident[:, :])
                        return m
                    tt = tr.do("pe", turn4, tqk, ta_, done3.get("scan"), prior("fin1"), dfree[2] if hh else None)
                    tn_ = tr.do("act", lambda T4=T4: act.copy(T4, ps[:, Q + 3, :]), tt, name="st")
                    dfree[0:3] = [[te, ta_], tqk, tn_]
                    yield
                four = lambda b_: b_.rearrange("p a b -> p (a b)")
                tb0 = tr.do("pool", lambda: pool.tensor_tensor(B, AD, bc(lev[:, 0], 1, 4), ALU.mult), ta_, dfree[0],
                            t_lev, prior("lvl"))
                tm_ = tr.do("dve", lambda: dve.tensor_tensor(M, bc(ident[:, :], 1, 4), B, ALU.subtract), tb0, ts_, t)

                def mturn():
                    for n in range(4):
                        m = pe.transpose(ps[:, Q, n * P:(n + 1) * P], M[:, n, :], ident[:, :])
                    return m
                t = tr.do("pe", mturn, tm_, te)
                tmt = tr.do("act", lambda: act.copy(four(Mt), ps[:, Q, :]), t)
                for l in range(1, 7):
                    tb_ = tr.do("pool", lambda l=l: pool.tensor_tensor(B, AD, bc(lev[:, l], 1, 4), ALU.mult),
                                tb0, tm_)

                    def z():
                        for n in range(4):
                            m = pe.matmul(ps[:, Q, n * P:(n + 1) * P], B[:, n, :], Mt[:, n, :], start=True, stop=True)
                        return m
                    tz = tr.do("pe", z, tb_, tmt)
                    tb0 = tz
                    tzc = tr.do("act", lambda: act.copy(four(Z), ps[:, Q, :]), tz)
                    yield

                    def dm(l=l):
                        for n in range(4):
                            m = pe.matmul(ps[:, Q + 1, n * P:(n + 1) * P], M[:, n, :], Z[:, n, :], start=True, stop=True)
                        if l < 6:
                            for n in range(4):
                                m = pe.matmul(ps[:, Q + 2, n * P:(n + 1) * P], Z[:, n, :], M[:, n, :], start=True, stop=True)
                        return m
                    t = tr.do("pe", dm, tzc, tm_, tqk if l == 1 else None, ta_ if l == 1 else None)
                    tmt = tr.do("dve", lambda: dve.tensor_tensor(four(Mt), four(Mt), ps[:, Q + 1, :], ALU.subtract), t,
                                name="lvl" if l == 6 else None)
                    if l < 6:
                        tm_ = tr.do("dve", lambda: dve.tensor_tensor(four(M), four(M), ps[:, Q + 2, :], ALU.subtract), t)
                    yield
                def u0():
                    for hh in range(2):
                        m = pe.matmul(ps[:, Q, hh * P:(hh + 1) * P], Mt[:, 2 * hh, :], u[:, hh, 0], start=True, stop=True)
                    return m
                t = tr.do("pe", u0, tmt, tu)
                t = tr.do("dve", lambda: dve.tensor_copy(u[:, :, 0], ps[:, Q, 0:S].rearrange("p (h d) -> p h d", h=2)), t)
                yield

                def a10():
                    for hh in range(2):
                        m = pe.matmul(ps[:, Q + 1, hh * P:(hh + 1) * P], TRN[:, hh, 0:P], u[:, hh, 0], start=True, stop=True)
                    return m
                t = tr.do("pe", a10, t, tn_, tmt)
                t = tr.do("dve", lambda: dve.tensor_tensor(
                    u[:, :, 1], u[:, :, 1], ps[:, Q + 1, 0:S].rearrange("p (h d) -> p h d", h=2), ALU.subtract), t)
                yield

                def u1():
                    for hh in range(2):
                        m = pe.matmul(ps[:, Q, hh * P:(hh + 1) * P], Mt[:, 2 * hh + 1, :], u[:, hh, 1], start=True, stop=True)
                    return m
                t = tr.do("pe", u1, t)
                t = tr.do("dve", lambda: dve.tensor_copy(u[:, :, 1], ps[:, Q, 0:S].rearrange("p (h d) -> p h d", h=2)), t,
                          name="uu")
                yield

                def o_():
                    for hh in range(2):
                        for tb in range(TB):
                            for kb in range(tb + 1):
                                m = pe.matmul(ps[:, Q + 2, (hh * TB + tb) * P:(hh * TB + tb + 1) * P],
                                              TRN[:, hh, (1 + tb + kb) * P:(2 + tb + kb) * P], u[:, hh, kb],
                                              start=kb == 0, stop=kb == tb)
                    return m
                t = tr.do("pe", o_, t, tn_, tmt, tm_)
                od = Z
                t = tr.do("dve", lambda: dve.tensor_tensor(od, ps[:, Q + 2, :].rearrange("p (k d) -> p k d", k=4),
                                                           bc(sc[:, 16:20], 2, P), ALU.mult), t, rq, name="od1")
                tsq = tr.do("act", lambda: act.activation(B, od, ACT.Square), t)
                yield
                t = tr.do("dve", lambda: dve.tensor_reduce(sc[:, 24:28], B, AX.X, ALU.add), tsq)
                t = root_inverse(tr, sc[:, 28:32], sc[:, 24:28], 4, EPS, 1.0 / P, t)
                yield
                t = tr.do("dve", lambda: dve.tensor_tensor(od, od, bc(sc[:, 28:32], 2, P), ALU.mult), t)
                t = tr.do("dve", lambda: dve.tensor_tensor(od, od, bc(onorm, 1, 4), ALU.mult), t, t_on)
                c = index(pair) * HALF + W
                yv = lambda: y[:, :, ds(c.v, HALF)].rearrange("p t (h d) -> p t h d", h=2)
                tr.do("dve", lambda: dve.tensor_tensor(yv(), yv(), od.rearrange("p (h t) d -> p t h d", h=2), ALU.mult),
                      t, here, name="fin1")
                yield
            dfree = [None, None, None]

            def before():
                yield from delta_gates()
                yield from recurrence()
            side = before()
            next(side)
            base = nstep[0]
            nstep[0] += 2 * HP
            delta_projection(index(0), side, base)
            quiet(side)
            done3["t"] = [done3["t"], done3["scan"]]
            t_cpd = pr.track("cpd").do("pool", lambda: pool.memset(cpd[:, :, 0:PAD], 0.0), done3["scan"])
            with pr.loop(1, HP) as i:
                side = delta_heads(i + -1)
                next(side)
                delta_projection(i, side, base)
                quiet(side)
            quiet(delta_heads(index(HP - 1)))
            return last_product("out3", a["od_w_out_2"][0], [dl.at(HP, "fin1"), done3["scan"]], 1.0, last)

        t = [t_x, t_vec, t_rope]
        for n in layers:
            t = {0: layer0, 1: layer1, 2: layer2, 3: layer3}[n](t, n == layers[-1])
        fin = pr.track("store")
        t = fin.do("sp", lambda: nc.sync.dma_start(out[0].rearrange("(t p) d -> p t d", p=P), x[:, :, :]),
                   t, sem="out", inc=16)
        fin.do("sp", lambda: nc.sync.nop(), t)
        block = ctx.enter_context(nc.Block())

        @block.tensor
        def _(eng):
            pr.emit("pe", eng)

        @block.scalar
        def _(eng):
            pr.emit("act", eng)

        @block.vector
        def _(eng):
            pr.emit("dve", eng)

        @block.gpsimd
        def _(eng):
            pr.emit("pool", eng)

        @block.sync
        def _(eng):
            pr.emit("sp", eng)


def frequencies():
    return np.concatenate([1.0 / (np.float32(THETA) ** (np.arange(0, n, 2, dtype=np.float32) / np.float32(n)))
                           for n in (128, 64)]).astype(np.float32)


def declare(nc, inputs, layers=(0, 1, 2, 3)):
    arrays = {f"in_{name}": np.ascontiguousarray(v) for name, v in inputs.items()}
    arrays["in_inv_freq"] = frequencies()
    args = {name[3:]: nc.dram_tensor(name, v.shape, mybir.dt.from_np(v.dtype), kind="ExternalInput").ap()
            for name, v in arrays.items()}
    out = nc.dram_tensor("out_x", (1, S, D), F32, kind="ExternalOutput").ap()
    build_program(nc, args, out, layers)
    return arrays


def kernel(**inputs):
    import concourse.bacc as bacc
    from concourse.bass_utils import run_bass_kernel_spmd

    nc = bacc.Bacc("TRN2", target_bir_lowering=False, num_devices=1)
    arrays = declare(nc, inputs)
    r = run_bass_kernel_spmd(nc, [arrays], core_ids=[0])
    return r.results[0]["out_x"]
```

```python
from contextlib import ExitStack, contextmanager
import math

import numpy as np
import concourse.bass as bass
import concourse.mybir as mybir

F32 = mybir.dt.float32
F32R = mybir.dt.float32r
I32 = mybir.dt.int32
ALU = mybir.AluOpType
ACT = mybir.ActivationFunctionType
AX = mybir.AxisListType
ds = bass.ds

P = 128
D = 2048
S = 256
TB = S // P
KT = D // P
N = 512
HALF = N // 2
NEG = -1e30
LOWEST = -3e38
DEPTH = 2
ALPHA = (2 * DEPTH) ** 0.25
LN_EPS = 1e-5
EPS = 1e-6
THETA = 10000.0
ENGINES = ("pe", "act", "dve", "pool", "sp")


class Loop:
    reg = None


class Index:
    def __init__(self, b, loop=None, a=0):
        self.loop, self.a, self.b = loop, a, b

    @property
    def v(self):
        return self.b if self.loop is None else self.loop.reg * self.a + self.b

    def __add__(self, k):
        return Index(self.b + k, self.loop, self.a)

    def __mul__(self, k):
        return Index(self.b * k, self.loop, self.a * k)


def index(i):
    return i if isinstance(i, Index) else Index(i)


class Program:
    def __init__(self, nc, ctx):
        self.nc, self.ctx = nc, ctx
        self.items = {e: [] for e in ENGINES}
        self.tracks = []

    @contextmanager
    def loop(self, lo, hi):
        lp = Loop()
        outer = self.items
        self.items = {e: [] for e in ENGINES}
        yield Index(0, lp, 1)
        inner, self.items = self.items, outer
        for e in ENGINES:
            if inner[e]:
                self.items[e].append(("loop", lp, lo, hi, inner[e]))

    def track(self, name):
        t = Track(self, name)
        self.tracks.append(t)
        return t

    def put(self, eng, fn, *after, signal=None, inc=1, by_itself=None):
        self.items[eng].append(("op", list(flat(after)), fn, signal, inc, by_itself))

    def emit(self, name, eng):
        for t in self.tracks:
            t.close()
            for key, owner in t.owner.items():
                if t.repeats and owner == name:
                    eng.sem_inc(t.sem(key), t.per[key])
        self._emit(eng, self.items[name], {})

    def _emit(self, eng, items, seen):
        for it in items:
            if it[0] == "loop":
                _, lp, lo, hi, inner = it
                with eng.Fori(lo, hi) as i:
                    lp.reg = i
                    self._emit(eng, inner, {})
                lp.reg = None
                continue
            _, after, fn, sem, inc, by_itself = it
            looped = False
            waits = {}
            for t in after:
                sem_, val = t.resolve()
                if val.loop is None:
                    key = (sem_, None)
                    if val.b <= 0:
                        continue
                else:
                    key = (sem_, val.loop, val.a)
                if key not in waits or waits[key][1].b < val.b:
                    waits[key] = (t.track.sem(sem_[1]), val)
            for key, (s, val) in waits.items():
                if seen.get(key, -1 << 30) >= val.b:
                    continue
                seen[key] = val.b
                eng.wait_ge(s, val.v)
                looped = looped or val.loop is not None
            if by_itself and looped:
                by_itself()
            r = fn()
            if sem:
                r.then_inc(sem[0].sem(sem[1]), inc)


def flat(after):
    for t in after:
        if t is None:
            continue
        if isinstance(t, (list, tuple)):
            yield from flat(t)
        else:
            yield t


class Tok:
    def __init__(self, track, key, step, n):
        self.track, self.key, self.step, self.n = track, key, step, n

    def resolve(self):
        key, n = (self.key, self.n) if self.key else self.track.names[self.n]
        per = self.track.per[key]
        st = self.step
        return (self.track.name, key), Index(st.b * per + n, st.loop if st.a else None, st.a * per)


class Track:
    def __init__(self, prog, name):
        self.prog, self.name = prog, name
        self.sems, self.per, self.names, self.count, self.owner = {}, {}, {}, {}, {}
        self.step, self.repeats, self.fixed, self.started = Index(0), False, False, False

    def sem(self, key):
        return self.sems[key]

    def own(self, key, eng):
        if key not in self.sems:
            self.sems[key] = self.prog.ctx.enter_context(self.prog.nc.semaphore(f"{self.name}_{key}"))
            self.owner[key] = eng

    def close(self):
        if self.count and not self.fixed:
            assert not self.per or self.per == self.count, (self.name, self.per, self.count)
            self.per = dict(self.count)
        self.count = {}

    def fix(self, per):
        self.fixed, self.repeats, self.per = True, True, per

    def begin(self, step):
        self.close()
        self.step, self.repeats = index(step), True
        return self

    def do(self, eng, fn, *after, sem=None, inc=1, name=None, by_itself=None):
        key = sem or eng
        self.own(key, eng)
        self.count[key] = self.count.get(key, 0) + inc
        tok = Tok(self, key, self.step, self.count[key])
        if name:
            self.names[name] = (key, self.count[key])
        self.prog.put(eng, fn, *after, signal=(self, key), inc=inc, by_itself=by_itself)
        return tok

    def at(self, step, name):
        return Tok(self, None, index(step), name)


def quiet(side):
    for _ in side:
        pass


def turns(n):
    for _ in range(n):
        yield


def paced(side, n):
    for _ in side:
        for _ in range(n):
            yield


def build_program(nc, a, out, layers=(0, 1, 2, 3)):
    pe, act, dve, pool = nc.tensor, nc.scalar, nc.vector, nc.gpsimd
    ctx = ExitStack()
    with ctx:
        pr = Program(nc, ctx)

        def sb(name, shape, dt=F32):
            return ctx.enter_context(nc.sbuf_tensor(name, shape, dt))

        raw = sb("raw", [P, 4, 4, N])
        whi = sb("whi", [P, 4, 2, N], F32R)
        wlo = sb("wlo", [P, 4, 2, N], F32R)
        xh = sb("xh", [P, KT, S], F32R)
        xl = sb("xl", [P, KT, S], F32R)
        x = sb("x", [P, TB, D])
        y = sb("y", [P, TB, D])
        ident = sb("ident", [P, P])
        ones = sb("ones", [P, P])
        nhalf = sb("nhalf", [P, 64])
        small = sb("small", [P, 256])
        stats = sb("stats", [P, TB, 4, 6])
        mv = sb("mv", [P, TB, 2])
        rstd = sb("rstd", [P, TB])
        hrstd = sb("hrstd", [P, TB])
        vec = sb("vec", [P, 256])
        cosb = sb("cosb", [P, TB, 64])
        sinb = sb("sinb", [P, TB, 64])
        WORK = 19200
        work = sb("work", [P, WORK])
        ps = ctx.enter_context(nc.psum_tensor("ps", [P, 8, N], F32))
        Q = 4

        class Carve:
            def __init__(self, at=0):
                self.at = at

            def __call__(self, *shape):
                n = int(np.prod(shape))
                ap = work[:, self.at:self.at + n]
                self.at += n
                assert self.at <= WORK, self.at
                if len(shape) > 1:
                    names = "abcd"[:len(shape)]
                    ap = ap.rearrange(f"p ({' '.join(names)}) -> p {' '.join(names)}",
                                      **dict(zip(names, shape)))
                return ap

        c = pr.track("const")
        t = c.do("pool", lambda: pool.memset(ident[:, :], 0.0))
        t_ident = c.do("pool", lambda: pool.affine_select(
            out=ident[:, :], in_=ident[:, :], compare_op=ALU.not_equal, fill=1.0, base=0,
            pattern=[[-1, P]], channel_multiplier=1), t)
        c.do("pool", lambda: pool.memset(ones[:, :], 1.0))
        t_const = c.do("pool", lambda: pool.memset(nhalf[:, :], -0.5))

        ring = pr.track("ring")
        ring.fix({"act": 8, "dve": 8, "pe": 8, **{f"raw{j}": 32 for j in range(4)}})
        ring.own("pe", "pe")
        nstep = [1]
        fine = [False]
        AHEAD = 3

        def slot(k):
            return whi[:, k % 4], wlo[:, k % 4]

        def split(step, k):
            if k >= 8:
                step, k = step + 1, k - 8
            w = raw[:, k // 2, 2 * (k % 2):2 * (k % 2) + 2, :]
            hi, lo = slot(k)
            d = Tok(ring, f"raw{k // 2}", step, 32)
            used = Tok(ring, "pe", step, k - 3) if k >= 4 else Tok(ring, "pe", step + -1, k + 5)
            ring.do("act", lambda: act.copy(hi, w), d, used)
            th = Tok(ring, "act", step, k + 1)
            ring.do("dve", lambda: dve.tensor_tensor(lo, w, hi.bitcast(F32), ALU.subtract), th, d, used)

        def stream(units, side=None, step=None, last=False):
            if step is None:
                step = nstep[0]
                nstep[0] += 1
            if not ring.started:
                for k in range(AHEAD):
                    split(index(step), k)
            step = index(step)
            ring.started = True
            ring.step = step
            t = None
            for j, (halves, n, mm, waits, done) in enumerate(units):
                free = Tok(ring, "dve", step + -1, 2 * j + 2)
                for dst, src in halves:
                    ring.do("sp", lambda dst=dst, src=src, j=j: nc.sync.dma_start(
                        dst(raw[:, j]), src()), free, sem=f"raw{j}", inc=16)
                for s in range(2):
                    k = 2 * j + s
                    if k + AHEAD < 8 or not last:
                        split(step, k + AHEAD)
                    hi, lo = (v[:, :, 0:n] for v in slot(k))
                    for l in range(2):
                        for tb in range(TB):
                            end = l == 1 and tb == TB - 1
                            pr.put("pe", lambda mm=mm, s=s, l=l, tb=tb, hi=hi, lo=lo: mm(s, l, tb, hi, lo),
                                   Tok(ring, "dve", step, k + 1), waits, signal=(ring, "pe") if end else None)
                            if side is not None and not end and (tb == TB - 1 or fine[0]):
                                next(side, None)
                    t = Tok(ring, "pe", step, k + 1)
                    if s == 1 and done:
                        done(t)
                    if side is not None:
                        next(side, None)
            return t

        def products(xh_, xl_, g, tb, l, hi, lo, n, bank, start, stop):
            o = ps[:, bank + tb, 0:n]
            sh = xh_[:, g, tb * P:(tb + 1) * P]
            sl = xl_[:, g, tb * P:(tb + 1) * P]
            pe.matmul(o, sh, hi[:, l, :], start=start, stop=False)
            pe.matmul(o, sh, lo[:, l, :], start=False, stop=False)
            return pe.matmul(o, sl, hi[:, l, :], start=False, stop=stop)

        IN_ORDER = tuple(range(KT // 2))

        def unit(w, cols, j, bank, waits, tx=None, done=None, pairs=IN_ORDER):
            n = sum(k for _, k in cols)
            halves = []
            for s in range(2):
                if len(cols) == 1:
                    c0, k = cols[0]
                    r0 = 2 * pairs[2 * j + s] * P
                    halves.append((lambda r, s=s, k=k: r[:, 2 * s:2 * s + 2, 0:k],
                                   lambda r0=r0, c0=c0, k=k: w[r0:r0 + 2 * P, ds(index(c0).v, k)]
                                   .rearrange("(t p) n -> p t n", p=P)))
                else:
                    c0, k = cols[s]
                    r0 = 4 * j * P
                    halves.append((lambda r, s=s, k=k: r[:, :, s * k:(s + 1) * k],
                                   lambda r0=r0, c0=c0, k=k: w[r0:r0 + 4 * P, ds(index(c0).v, k)]
                                   .rearrange("(t p) n -> p t n", p=P)))
            return (halves, n, lambda s, l, tb, hi, lo: products(
                xh, xl, 4 * j + 2 * s + l, tb, l, hi, lo, n, bank, j == 0 and s + l == 0, j == 3 and s + l == 2),
                [waits, tx[2 * j:2 * j + 2] if tx else []], done)

        def project(w, cols, bank, waits, side=None, step=None, last=False, tx=None, pairs=IN_ORDER):
            return stream([unit(w, cols, j, bank, waits, tx, None, pairs) for j in range(4)], side, step, last)

        def transposed(tr, src, nk, dh, dl, waits, gain=None, wait_bank=None, banks=(4, 5, 6, 7)):
            freed = [wait_bank] * len(banks)
            tok = []
            for g in range(nk // 2):
                b = banks[g % len(banks)]

                def tp(g=g, b=b):
                    for l in range(2):
                        for tb in range(TB):
                            m = pe.transpose(ps[:, b, (l * TB + tb) * P:(l * TB + tb + 1) * P],
                                             src(tb, 2 * g + l), ident[:, :])
                    return m
                t = tr.do("pe", tp, waits(g) if callable(waits) else waits if g == 0 else [],
                          freed[g % len(banks)], t_ident)
                if gain is None:
                    pv = ps[:, b, :].rearrange("p (l t) -> p l t", l=2)
                    hh, ll = dh[:, 2 * g:2 * g + 2, :], dl[:, 2 * g:2 * g + 2, :]
                    th = tr.do("act", lambda hh=hh, pv=pv: act.copy(hh, pv), t)
                    tl = tr.do("dve", lambda hh=hh, ll=ll, pv=pv: dve.tensor_tensor(
                        ll, pv, hh.bitcast(F32), ALU.subtract), t, th)
                else:
                    ops = []
                    for l in range(2):
                        k = 2 * g + l
                        ops.append((ps[:, b, l * S:(l + 1) * S], dh[:, k, :], dl[:, k, :], gain[:, k:k + 1]))
                    for pv, hh, _, gg in ops:
                        th = tr.do("act", lambda hh=hh, pv=pv, gg=gg: act.activation(
                            hh, pv, ACT.Copy, scale=gg), t)
                    for pv, hh, ll, gg in ops:
                        tl = tr.do("dve", lambda hh=hh, ll=ll, pv=pv, gg=gg: dve.scalar_tensor_tensor(
                            out=ll, in0=pv, scalar=gg, in1=hh.bitcast(F32), op0=ALU.mult,
                            op1=ALU.subtract), t, th)
                freed[g % len(banks)] = tl
                tok.append([th, tl])
            return tok

        def root_inverse(tr, dst, src, k, eps, scale, waits):
            t = tr.do("dve", lambda: dve.tensor_scalar(dst, src, scale, eps, ALU.mult, ALU.add), waits)
            return tr.do("pool", lambda: pool.tensor_tensor(
                dst, dst, nhalf[:, 0:k], ALU.pow), t, t_const)

        def bc(ap, dim, n):
            u = ap.unsqueeze(dim)
            shape = list(u.shape)
            shape[dim] = n
            return u.broadcast_to(shape)

        def load(name, dst, src, *after, scattered=False):
            return pr.track("ld_" + name).do("pool", lambda: pool.dma_start(
                dst, src(), allow_slow_non_contiguous=scattered), *after,
                                             sem="dma", inc=16)

        def row(v, n):
            return bass.AP(v.tensor, v.offset, [[0, P], [1, n]])

        ldx = pr.track("ld_x")
        t_x = [ldx.do("sp", lambda q=q: nc.sync.dma_start(
            x[:, :, q * N:(q + 1) * N], a["x"][0].rearrange("(t p) d -> p t d", p=P)[:, :, q * N:(q + 1) * N]),
            sem=f"q{q}", inc=16) for q in range(4)]
        rows = [("cd", a["od_conv_d_w_2"][0].rearrange("j (c p) -> (j c) p", p=P), 96),
                ("cw", a["od_conv_c_w_2"][0].rearrange("j (c p) -> (j c) p", p=P), 32),
                ("cb", a["od_conv_c_b_2"][0].rearrange("(c p) -> c p", p=P), 8),
                ("gb", a["od_gate_b_2"][0].rearrange("(c p) -> c p", p=P), 16),
                ("lam", a["od_lambda_2"][0].rearrange("(c p) -> c p", p=P), 8),
                ("ev", a["ev_norm_2"][0].rearrange("(c p) -> c p", p=P), 16),
                ("od", a["od_norm_2"][0].rearrange("(c p) -> c p", p=P), 16),
                ("qn", a["ev_qn_gain_2"], 1), ("kn", a["ev_kn_gain_2"], 1),
                ("mq", a["mla_q_norm"][0].rearrange("(c p) -> c p", p=P), 4),
                ("mk", a["mla_kv_norm"][0].rearrange("(c p) -> c p", p=P), 4)]
        setup = pr.track("setup")
        vrows = y[:, 0, 0:2 * P].rearrange("p (g c) -> p g c", g=2)
        col, at, tl = {}, 0, []
        t_vz = setup.do("dve", lambda: dve.memset(vrows, 0.0))
        for name, src, n in rows:
            g = 0 if at < 96 else 1
            o = at if g == 0 else at - 96
            tl.append(setup.do("sp", lambda g=g, o=o, n=n, src=src: nc.sync.dma_start(
                vrows[o:o + n, g, :], src), t_vz, sem="vec", inc=16))
            col[name] = g * P + o
            at += n
        t_vec, t_rope = [], []

        def small_vectors():
            t = setup.do("pe", lambda: [pe.transpose(ps[:, 7, g * P:(g + 1) * P], vrows[:, g, :], ident[:, :])
                                        for g in range(2)][-1], tl[-1], t_ident)
            t_vec.append(setup.do("dve", lambda: dve.tensor_copy(vec[:, :], ps[:, 7, 0:2 * P]), t))

        def vcol(name, n, k=0):
            return vec[:, col[name] + k:col[name] + k + n]

        class Heads:
            def __init__(self, tr, step, n):
                self.tr, self.step, self.n, self.tok = tr, index(step), n, {}
                tr.begin(step)

            def do(self, eng, stage, h, fn, *after, **kw):
                t = self.tr.do(eng, fn, *after, name=f"{stage}{h}", **kw)
                self.tok[stage, h] = t
                return t

            def before(self, stage, h):
                if h:
                    return self.tok[stage, h - 1]
                return self.tr.at(self.step + -1, f"{stage}{self.n - 1}")

            def prior(self, name):
                return self.tr.at(self.step + -1, name)

        def attend(hd, h, scores, ready, parts, scale, nblk, tbank, pt, pv, fin, sc, gap=1):
            mx, nb, den, rden = (sc[:, 2 * i:2 * i + 2] for i in range(4))
            t = hd.do("pe", "sc", h, scores, ready, hd.before("mask", h), hd.before("pt", h))
            for tb, (s_, m_, w_) in enumerate(parts):
                t1 = hd.do("dve", "mask", h, lambda s_=s_, m_=m_, w_=w_, tb=tb: dve.tensor_tensor_reduce(
                    w_, s_, m_() if callable(m_) else m_, 1.0, LOWEST, ALU.add, ALU.max, mx[:, tb:tb + 1]),
                    t, hd.before("tp", h), hd.before("fin", h),
                    by_itself=lambda: dve.memset(small[:, 255:256], 0.0))
            t2 = hd.do("dve", "nb", h, lambda: dve.tensor_scalar(nb, mx, -scale, None, ALU.mult), t1)
            for tb, (s_, m_, w_) in enumerate(parts):
                t3 = hd.do("act", "exp", h, lambda w_=w_, tb=tb: act.activation(
                    w_, w_, ACT.Exp, bias=nb[:, tb:tb + 1], scale=scale, accum_out=den[:, tb:tb + 1]), t2)
            t4 = hd.do("dve", "rden", h, lambda: dve.reciprocal(rden, den), t3)
            for _ in range(gap):
                yield
            w0 = parts[0][2]
            blocks = bass.AP(w0.tensor, w0.offset, [list(w0.ap[0]), [P, nblk], [1, P]])

            def turn():
                for b in range(nblk):
                    m = pe.transpose(tbank[:, b * P:(b + 1) * P], blocks[:, b, :], ident[:, :])
                return m
            t5 = hd.do("pe", "tp", h, turn, t3, t1, hd.before("pt", h))
            t6 = hd.do("act", "pt", h, lambda: act.copy(pt, tbank[:, 0:nblk * P]), t5, hd.before("pv", h))
            yield
            t7 = hd.do("pe", "pv", h, pv, t6, hd.before("fin", h))
            hd.do("dve", "fin", h, lambda: fin(rden), t7, t4)
            yield

        def gates(name, w, c0, y0, nslab, waits, scratch, side=None, half=None, tx=None):
            tr = pr.track(name)
            base = nstep[0]
            nstep[0] += nslab

            def two_slabs(i, side):
                tr.begin(i + 1)
                for s in range(2):
                    free = tr.at(i, f"g{s}")
                    tm = project(w, [((i * (2 * N)) + (c0 + s * N), N)], 2 * s, [waits, free],
                                 side, step=(i * 2) + (base + s), tx=tx)
                    gate_out(tr, f"g{s}", ps[:, 2 * s:2 * s + 2, :],
                             (i * (2 * N)) + (y0 + s * N), N, tm, scratch,
                             tr.at(i, "g1") if s == 0 else tr.at(i + 1, "g0"), half)
            two_slabs(index(0), side)
            if nslab > 2:
                with pr.loop(1, nslab // 2) as i:
                    two_slabs(i, None)
            return tr.at(nslab // 2, "g1")

        def gate_out(tr, name, src, c, n, ready, scratch, scratch_free, half=None):
            if half is None:
                tr.do("act", lambda: act.activation(y[:, :, ds(c.v, n)], src, ACT.Copy, scale=0.5), ready)
                t = tr.do("act", lambda: act.activation(scratch, src, ACT.Tanh, scale=0.5), ready, scratch_free)
            else:
                for tb in range(TB):
                    tr.do("act", lambda tb=tb: act.activation(
                        y[:, tb, ds(c.v, n)], src[:, tb], ACT.Copy, scale=half[:, tb:tb + 1]), ready)
                for tb in range(TB):
                    t = tr.do("act", lambda tb=tb: act.activation(
                        scratch[:, tb], src[:, tb], ACT.Tanh, scale=half[:, tb:tb + 1]), ready, scratch_free)
            return tr.do("dve", lambda: dve.scalar_tensor_tensor(
                out=y[:, :, ds(c.v, n)], in0=scratch, scalar=1.0, in1=y[:, :, ds(c.v, n)],
                op0=ALU.add, op1=ALU.mult), t, name=name)

        def last_product(name, w, side, early, end, free, alpha, last, pairs=IN_ORDER):
            src = lambda tb, k: y[:, tb, (2 * pairs[k // 2] + k % 2) * P:(2 * pairs[k // 2] + k % 2 + 1) * P]
            tt = pr.track(name + "_t")
            ev = pr.track(name)
            LATE = KT - 4
            ty = transposed(tt, src, LATE, xh, xl, [early, free], banks=(2, 3))
            late = []

            def late_tiles(_):
                quiet(side)
                late.extend(transposed(tt, lambda tb, k: src(tb, LATE + k), 4,
                                       xh[:, LATE:], xl[:, LATE:], end))

            def add(i, s):
                def done(tm):
                    c = slice((2 * i + s) * N, (2 * i + s + 1) * N)
                    t = ev.do("dve", lambda: dve.scalar_tensor_tensor(
                        out=x[:, :, c], in0=x[:, :, c], scalar=alpha,
                        in1=ps[:, 2 * s:2 * s + 2, :], op0=ALU.mult, op1=ALU.add), tm, name=f"add{s}")
                    if alpha != 1.0:
                        for tb in range(TB):
                            ev.do("dve", lambda tb=tb: dve.bn_stats(
                                stats[:, tb, 2 * i + s], x[:, tb, c]), t, name="end")
                return done
            ev.begin(1)
            early_units = [unit(w, [(s * N, N)], j, 2 * s, [free, ty[-2:] if s else []], ty,
                                late_tiles if (s, j) == (1, 2) else None, pairs)
                           for s in range(2) for j in range(3)]
            late_units = [unit(w, [(s * N, N)], 3, 2 * s, late, None, add(0, s), pairs) for s in range(2)]
            stream(early_units[:4], side)
            stream(early_units[4:] + late_units, side)
            ev.begin(2)
            for s in range(2):
                c = (2 + s) * N
                add(1, s)(project(w, [(c, N)], 2 * s, [ev.at(1, f"add{s}")], last=last and s == 1, pairs=pairs))
            return [ev.at(2, "end")] if alpha != 1.0 else [ev.at(1 + s // 2, f"add{s % 2}") for s in range(4)]

        LN = WORK - 2 * D

        def layer_norm(layer, ready, free):
            tr = pr.track(f"ln{layer}")
            c_ = Carve(LN)
            g, b = c_(D), c_(D)
            tg = [load(f"lng{layer}", g, lambda: row(a["ln_g"][layer], D), free),
                  load(f"lnb{layer}", b, lambda: row(a["ln_b"][layer], D), free)]
            for tb in range(TB):
                t = tr.do("dve", lambda tb=tb: dve.bn_aggr(
                    mv[:, tb, :], stats[:, tb].rearrange("p a b -> p (a b)")), ready)
            tv = tr.do("dve", lambda: dve.tensor_scalar(rstd[:, :], mv[:, :, 1], LN_EPS, None, ALU.add), t)
            tv = tr.do("pool", lambda: pool.tensor_tensor(rstd[:, :], rstd[:, :], nhalf[:, 0:TB], ALU.pow),
                       tv, t_const)
            tv = tr.do("dve", lambda: dve.scalar_tensor_tensor(
                out=hrstd[:, :], in0=mv[:, :, 0], scalar=-1.0, in1=rstd[:, :], op0=ALU.mult, op1=ALU.mult), tv, t)
            out_ = []
            for q in range(4):
                xq = x[:, :, q * N:(q + 1) * N]
                for tb in range(TB):
                    t = tr.do("act", lambda tb=tb, xq=xq: act.activation(
                        xq[:, tb], xq[:, tb], ACT.Identity, bias=hrstd[:, tb:tb + 1], scale=rstd[:, tb:tb + 1]), tv, ready)
                for v, op in ((g, ALU.mult), (b, ALU.add)):
                    t = tr.do("dve", lambda xq=xq, v=v, q=q, op=op: dve.tensor_tensor(
                        xq, xq, bc(v[:, q * N:(q + 1) * N], 1, TB), op), t, tg)
                out_.append(t)
            return out_

        def rms_columns(name, ready, scales):
            tr = pr.track(name)
            ts = []
            for tb in range(TB):
                ts.append(tr.do("act", lambda tb=tb: act.activation(
                    y[:, tb], x[:, tb], ACT.Square, accum_out=small[:, tb:tb + 1]), ready))
                for _ in range(3):
                    yield
            t = root_inverse(tr, rstd[:, :], small[:, 0:2], TB, EPS, 1.0 / D, ts)
            scales.append(tr.do("dve", lambda: dve.tensor_scalar(hrstd[:, :], rstd[:, :], 0.5, None, ALU.mult), t))

        def scaled_out(tr, dst, src, *after, name=None):
            for tb in range(TB):
                t = tr.do("act", lambda tb=tb: act.activation(
                    dst(tb), src(tb), ACT.Copy, scale=rstd[:, tb:tb + 1]), *after, name=name)
            return t

        def rope_tables(cosa, sina, base):
            tr = pr.track("rope")
            FA, FB = 64, 32
            F = FA + FB
            c_ = Carve(base)
            inv, pos = c_(F), c_(TB)
            ang, kk, r, rc, m = (c_(TB, F) for _ in range(5))
            posi = small[:, 8:8 + TB].bitcast(I32)
            t = load("pos", posi, lambda: a["positions"][0].rearrange("(t p) -> p t", p=P), scattered=True)
            ti = load("inv", inv, lambda: row(a["inv_freq"], F))
            for _ in range(6):
                yield
            small_vectors()
            t = tr.do("dve", lambda: dve.tensor_copy(pos, posi), t)
            for tb in range(TB):
                t = tr.do("dve", lambda tb=tb: dve.tensor_scalar(
                    ang[:, tb], inv, pos[:, tb:tb + 1], None, ALU.mult), t, ti)
            two_pi = 2 * math.pi
            c1 = 6.28125
            c2 = float(np.float32(math.floor((two_pi - c1) * 2.0 ** 22) / 2.0 ** 22))
            c3 = two_pi - c1 - c2
            magic = 1.5 * 2.0 ** 23
            t = tr.do("dve", lambda: dve.tensor_scalar(kk, ang, 1 / two_pi, magic, ALU.mult, ALU.add), t)
            t = tr.do("dve", lambda: dve.tensor_scalar(kk, kk, magic, None, ALU.subtract), t)
            src = ang
            for cc in (c1, c2, c3):
                t = tr.do("dve", lambda cc=cc, src=src: dve.scalar_tensor_tensor(
                    out=r, in0=kk, scalar=-cc, in1=src, op0=ALU.mult, op1=ALU.add), t)
                src = r
            lim = 3.1415925
            t = tr.do("dve", lambda: dve.tensor_scalar(r, r, lim, -lim, ALU.min, ALU.max), t)
            t = tr.do("dve", lambda: dve.tensor_scalar(rc, r, math.pi / 2, None, ALU.add), t)
            t = tr.do("dve", lambda: dve.tensor_scalar(m, rc, math.pi, None, ALU.is_gt), t)
            t = tr.do("dve", lambda: dve.scalar_tensor_tensor(
                out=rc, in0=m, scalar=-two_pi, in1=rc, op0=ALU.mult, op1=ALU.add), t)
            t = tr.do("dve", lambda: dve.tensor_scalar(rc, rc, lim, -lim, ALU.min, ALU.max), t)
            for tb in range(TB):
                for half in range(2):
                    sg = -1.0 if half == 0 else 1.0
                    for hh in range(2):
                        o = slice(half * FA, half * FA + FA)
                        tr.do("act", lambda tb=tb, hh=hh, o=o: act.activation(
                            cosa[:, 2 * tb + hh, o], rc[:, tb, 0:FA], ACT.Sin), t)
                        tr.do("act", lambda tb=tb, hh=hh, o=o, sg=sg: act.activation(
                            sina[:, 2 * tb + hh, o], r[:, tb, 0:FA], ACT.Sin, scale=sg), t)
                    o = slice(half * FB, half * FB + FB)
                    tr.do("act", lambda tb=tb, o=o: act.activation(cosb[:, tb, o], rc[:, tb, FA:F], ACT.Sin), t)
                    te = tr.do("act", lambda tb=tb, o=o, sg=sg: act.activation(
                        sinb[:, tb, o], r[:, tb, FA:F], ACT.Sin, scale=sg), t)
                yield
            t_rope.append(te)

        def causal(tr, m, w, base, t, strict=False):
            return tr.do("pool", lambda: pool.affine_select(
                out=m, in_=m, compare_op=ALU.is_gt if strict else ALU.is_ge, fill=NEG, base=base,
                pattern=[[-1, w]], channel_multiplier=1), t)

        ROPE_AT = 14592 + 1152
        tables = rope_tables(work[:, ROPE_AT:ROPE_AT + 512].rearrange("p (a b) -> p a b", a=4),
                             work[:, ROPE_AT + 512:ROPE_AT + 1024].rearrange("p (a b) -> p a b", a=4), ROPE_AT + 1024)

        def layer0(ready, last):
            G = 3
            PAIRS = 8
            PACE0 = 3
            c_ = Carve()
            h = c_(10, TB, HALF)
            t1, t2 = c_(4, P), c_(4, P)
            qk = c_(6, 2, S)
            vb = c_(G, TB, HALF)
            zs = c_(TB, HALF)
            sm = c_(9 * P)
            pt = c_(9 * P)
            mask = c_(9 * P)
            c_.at = ROPE_AT
            cosa, sina = c_(4, P), c_(4, P)
            tx = transposed(pr.track("xt0"), lambda tb, k: x[:, tb, k * P:(k + 1) * P], KT, xh, xl, lambda g: ready[g // 2])
            tr = pr.track("mask0")
            iv = t1.rearrange("p a b -> p (a b)")[:, 0:S].bitcast(I32)
            t = tr.do("pool", lambda: pool.iota(iv, [[-1, S]], base=S, channel_multiplier=1))
            m0 = mask[:, 0:G * P].rearrange("p (g k) -> p g k", g=G)
            m1 = mask[:, G * P:].rearrange("p (g k) -> p g k", g=G)
            tm = tr.do("pool", lambda: pool.memset(mask, 0.0))
            it = t2.rearrange("p a b -> p (a b)")[:, 0:S].bitcast(I32)
            for g, dil in ((1, 4), (2, 16)):
                t = tr.do("dve", lambda dil=dil: dve.tensor_scalar(it, iv, dil - 1, None, ALU.bitwise_and), t, tm)
                t = tr.do("dve", lambda g=g: dve.tensor_scalar(m0[:, g], it[:, 0:P], 1.0, NEG, ALU.min, ALU.mult), t, tm)
                t = tr.do("dve", lambda g=g: dve.tensor_scalar(m1[:, g], it, 1.0, NEG, ALU.min, ALU.mult), t, tm)
            for g in range(G):
                t = causal(tr, m0[:, g], P, 0, t)
                t = causal(tr, m1[:, g], S, P, t)
            t_mask = tr.do("pool", lambda: pool.affine_select(
                out=m1[:, 0], in_=m1[:, 0], compare_op=ALU.is_ge, fill=NEG, base=0,
                pattern=[[1, S]], channel_multiplier=-1), t)
            w = a["dsa_w_in"][0]
            ev = pr.track("ev0")
            tr = pr.track("att0")
            BLOCKS = [(0, 0), (0, 1), (0, 2), (1, 0), (1, 1), (1, 2), (2, 0), (2, 1), (2, 2), (3, 0)]
            ROT = [0, 1, 3, 4, 6, 7]

            def pair_projection(pair, side, base):
                ev.begin(pair + 1)
                for s in range(5):
                    cols = [(pair * HALF + (3 * g + t) * D, HALF) for g, t in BLOCKS[2 * s:2 * s + 2]]
                    b = 2 * (s % 2)
                    free = ev.at(pair + 1, f"out{s - 2}") if s >= 2 else \
                        ev.at(pair, "out4" if s == 0 else "out3")
                    tm = project(w, cols, b, [free], side, step=(pair * 5) + (base + s), tx=tx)
                    dst = h[:, 2 * s:2 * s + 2].rearrange("p b t c -> p t b c")
                    src = ps[:, b:b + 2, :].rearrange("p t (b c) -> p t b c", b=2)
                    took = [tr.at(pair, f"took{k}") for k in (2 * s, 2 * s + 1)]
                    if s < 4:
                        ev.do("act", lambda dst=dst, src=src: act.copy(dst, src), tm, took, name=f"out{s}")
                    else:
                        ev.do("act", lambda: act.copy(h[:, 8], ps[:, 0:2, 0:HALF]), tm, took)
                        ev.do("act", lambda: act.activation(h[:, 9], ps[:, 0:2, HALF:N], ACT.Copy, scale=0.5),
                              tm, took, name="out4")

            def pair_attention(pair):
                step = pair + 1
                hd = Heads(tr, step, 2)
                for g in range(G):
                    tv = tr.do("act", lambda g=g: act.copy(vb[:, g], h[:, 3 * g + 2]),
                               ev.at(step, "out4"), hd.prior("pv1"), name=f"took{3 * g + 2}")
                tz = tr.do("act", lambda: act.activation(zs, h[:, 9], ACT.Tanh), ev.at(step, "out4"), hd.prior("fin1"))
                tz = tr.do("dve", lambda: dve.scalar_tensor_tensor(
                    out=zs, in0=zs, scalar=1.0, in1=h[:, 9], op0=ALU.add, op1=ALU.mult), tz, name="took9")
                yield
                pend = []

                def turn(n, blk, tr_):
                    b = Q + n % 3
                    v = h[:, blk].rearrange("p t (h d) -> p h t d", h=2)

                    def f():
                        for hh in range(2):
                            for tb in range(TB):
                                m = pe.transpose(ps[:, b, (hh * TB + tb) * P:(hh * TB + tb + 1) * P],
                                                 v[:, hh, tb, :], ident[:, :])
                        return m
                    t = tr.do("pe", f, tr_, pend[n - 3] if n >= 3 else hd.prior("pt1"),
                              hd.prior("mask1") if n < 3 else None, name=f"took{blk}")
                    pend.append(tr.do("act", lambda: act.copy(qk[:, n], ps[:, b, :].rearrange(
                        "p (h t) -> p h t", h=2)), t, hd.prior("sc1"), name=f"qk{n}"))

                wait = None
                last = [tz]
                for n, blk in enumerate(ROT):
                    xv = h[:, blk].rearrange("p t (h d) -> p (t h) d", h=2)
                    ta = tr.do("pool", lambda xv=xv: pool.tensor_tensor(t1, xv, cosa, ALU.mult),
                               ev.at(step, "out4"), t_rope, t_mask, last)
                    tb1 = tr.do("dve", lambda xv=xv: dve.tensor_tensor(
                        t2[:, :, 0:64], xv[:, :, 64:P], sina[:, :, 0:64], ALU.mult), ev.at(step, "out4"), t_rope, t_mask, last)
                    tb2 = tr.do("dve", lambda xv=xv: dve.tensor_tensor(
                        t2[:, :, 64:P], xv[:, :, 0:64], sina[:, :, 64:P], ALU.mult), t_rope, t_mask, last)
                    last = [tr.do("dve", lambda xv=xv: dve.tensor_tensor(xv, t1, t2, ALU.add), ta, tb1, tb2)]
                    if wait:
                        turn(*wait)
                    wait = (n, blk, last)
                    yield
                turn(*wait)
                yield

                def head(hh):
                    def scores():
                        for g in range(G):
                            q, k = qk[:, 2 * g, hh, :], qk[:, 2 * g + 1, hh, :]
                            pe.matmul(flat4[:, g * P:(g + 1) * P], q[:, 0:P], k[:, 0:P], start=True, stop=True)
                        for g in range(G):
                            q, k = qk[:, 2 * g, hh, :], qk[:, 2 * g + 1, hh, :]
                            m = pe.matmul(flat4[:, N + g * S:N + (g + 1) * S], q[:, P:S], k[:, 0:S], start=True, stop=True)
                        return m

                    def pv():
                        for tb in range(TB):
                            o = ps[:, Q + 3, tb * P:(tb + 1) * P]
                            for g in range(G):
                                for kb in range(tb + 1):
                                    blk = g if tb == 0 else G + 2 * g + kb
                                    m = pe.matmul(o, pt[:, blk * P:(blk + 1) * P], vb[:, g, kb, hh * P:(hh + 1) * P],
                                                  start=g == 0 and kb == 0, stop=g == G - 1 and kb == tb)
                        return m

                    def fin(rden):
                        for tb in range(TB):
                            c = index(pair) * HALF + hh * P
                            m = dve.scalar_tensor_tensor(
                                out=y[:, tb, ds(c.v, P)], in0=ps[:, Q + 3, tb * P:(tb + 1) * P],
                                scalar=rden[:, tb:tb + 1], in1=zs[:, tb, hh * P:(hh + 1) * P],
                                op0=ALU.mult, op1=ALU.mult)
                        return m
                    parts = [(flat4[:, 0:G * P], mask[:, 0:G * P], sm[:, 0:G * P]),
                             (flat4[:, N:N + G * S], mask[:, G * P:], sm[:, G * P:])]
                    return attend(hd, hh, scores, [pend, t_mask], parts, P ** -0.5, 9, flat4, pt, pv, fin,
                                  small[:, 16 + 8 * hh:24 + 8 * hh], gap=3)
                flat4 = ps[:, Q:Q + 4, :].rearrange("p b n -> p (b n)")
                for hh in range(2):
                    for k, _ in enumerate(head(hh)):
                        yield

            base = nstep[0]
            nstep[0] += 5 * PAIRS
            pair_projection(index(0), tables, base)
            with pr.loop(1, PAIRS) as i:
                side = paced(pair_attention(i + -1), PACE0)
                pair_projection(i, side, base)
                quiet(side)
            end = tr.at(PAIRS, "fin1")
            t = last_product("out0", a["dsa_w_out"][0], pair_attention(index(PAIRS - 1)), tr.at(PAIRS - 1, "fin1"), end,
                             [ev.at(PAIRS, "out3"), ev.at(PAIRS, "out4")], ALPHA, last)
            return layer_norm(0, t, end)

        def unit_products(sh, sl, g0, bank):
            def mm(s, l, tb, hi, lo):
                return products(sh, sl, g0 + 2 * s + l, tb, l, hi, lo, hi.shape[-1], bank, s + l == 0, s + l == 2)
            return mm

        def layer1(ready, last):
            NOPE, ROPE, R = P, 64, 512
            QH, KH = NOPE + ROPE, 2 * P
            QUADS, HQ = 4, 4
            c_ = Carve()
            cc = c_(2, TB, R)
            hq = c_(TB, HQ * QH)
            hkv = c_(TB, HQ * KH)
            v = c_(TB, HQ, P)
            qt, kt, qpt = c_(HQ, S), c_(HQ, S), c_(HQ, S)
            kpt = c_(S)
            t1, t2 = c_(TB, HQ, ROPE), c_(TB, HQ, ROPE)
            kp = c_(TB, ROPE)
            sm, pt, mask = c_(3 * P), c_(3 * P), c_(3 * P)
            scratch = c_(TB, N)
            w = a["mla_w_in"][0]
            tr = pr.track("mask1")
            t = tr.do("pool", lambda: pool.memset(mask, 0.0), ready)
            t = causal(tr, mask[:, 0:P], P, 0, t)
            t_mask = causal(tr, mask[:, P:], S, P, t)

            tx = transposed(pr.track("xt1"), lambda tb, k: x[:, tb, k * P:(k + 1) * P], KT, xh, xl, lambda g: ready[g // 2])
            la = pr.track("lat")
            outs = []
            for s, (c0, n) in enumerate(((0, R), (2 * R, ROPE), (R, R))):
                b = 2 * (s % 2)
                tm = project(w, [(c0, n)], b, [outs[0] if s == 2 else None], tx=tx)
                dst = kp if s == 1 else cc[:, s // 2]
                outs.append(la.do("act", lambda b=b, dst=dst, n=n: act.copy(dst, ps[:, b:b + 2, 0:n]), tm, ready))

            def norms():
                t = None
                for s in range(2):
                    for tb in range(TB):
                        t = la.do("act", lambda s=s, tb=tb: act.activation(
                            scratch2[:, tb], cc[:, s, tb], ACT.Square,
                            accum_out=small[:, 2 * s + tb:2 * s + tb + 1]), outs, ready, t)
                t = root_inverse(la, small[:, 4:8], small[:, 0:4], 4, EPS, 1.0 / R, t)
                yield
                for s in range(2):
                    for tb in range(TB):
                        k = 4 + 2 * s + tb
                        tn = la.do("dve", lambda s=s, tb=tb, k=k: dve.tensor_scalar(
                            cc[:, s, tb], cc[:, s, tb], small[:, k:k + 1], None, ALU.mult), t)
                la.normed = tn
                yield
                ta = la.do("dve", lambda: dve.tensor_tensor(t1[:, :, 0], kp, cosb[:, :, :], ALU.mult), outs)
                la.do("dve", lambda: dve.tensor_tensor(t2[:, :, 0, 0:32], kp[:, :, 32:64], sinb[:, :, 0:32], ALU.mult), outs)
                tb_ = la.do("dve", lambda: dve.tensor_tensor(t2[:, :, 0, 32:64], kp[:, :, 0:32], sinb[:, :, 32:64], ALU.mult))
                t = la.do("dve", lambda: dve.tensor_tensor(kp, t1[:, :, 0], t2[:, :, 0], ALU.add), ta, tb_)
                yield
                t = la.do("pe", lambda: [pe.transpose(ps[0:ROPE, Q + 3, tb * P:(tb + 1) * P], kp[:, tb], ident[:, :])
                                         for tb in range(TB)][-1], t)
                la.kpt = la.do("act", lambda: act.copy(kpt[0:ROPE], ps[0:ROPE, Q + 3, 0:S]), t)
                yield
            scratch2 = hq.rearrange("p a b -> p (a b)")[:, 0:TB * R].rearrange("p (t n) -> p t n", t=TB)
            beside = norms()
            tg = gates("gate1", w, 2 * R + ROPE, 0, 4, [outs], scratch, beside, tx=tx)
            quiet(beside)
            ct = pr.track("ct")
            tq = transposed(ct, lambda tb, k: cc[:, 0, tb, k * P:(k + 1) * P], 4, xh[:, 0:4], xl[:, 0:4],
                            [la.normed, tg], gain=vcol("mq", 4), wait_bank=la.kpt)
            tk = transposed(ct, lambda tb, k: cc[:, 1, tb, k * P:(k + 1) * P], 4, xh[:, 4:8], xl[:, 4:8],
                            [la.normed, tg], gain=vcol("mk", 4), wait_bank=tq)

            ev, tr = pr.track("ev1"), pr.track("att1")
            wq, wkv = a["mla_w_uq"][0], a["mla_w_ukv"][0]

            def quad_projection(quad, side, base):
                ev.begin(quad + 1)
                units = []
                for p in range(2):
                    for kind in range(2):
                        n = 2 * (QH, KH)[kind]
                        b = 2 * kind
                        c0 = quad * (2 * n) + p * n
                        wsrc = (wq, wkv)[kind]
                        halves = [(lambda r, s=s, n=n: r[:, 2 * s:2 * s + 2, 0:n],
                                   lambda s=s, n=n, c0=c0, wsrc=wsrc: wsrc[2 * s * P:2 * (s + 1) * P, ds(c0.v, n)]
                                   .rearrange("(t p) n -> p t n", p=P)) for s in range(2)]
                        free = ev.at(quad + (p and 1), f"out{1 - p}{kind}")

                        def done(t, p=p, kind=kind, n=n, b=b):
                            dst = (hq, hkv)[kind][:, :, p * n:(p + 1) * n]
                            ev.do("act", lambda: act.copy(dst, ps[:, b:b + 2, 0:n]), t,
                                  tr.at(quad, "tookq" if kind == 0 else "tookk"), tr.at(quad, "tookv"),
                                  name=f"out{p}{kind}")
                        units.append((halves, n, unit_products(xh, xl, 4 * kind, b),
                                      [tq, tk, tg, outs, free], done))
                stream(units, side, step=quad + base)

            def quad_attention(quad):
                step = quad + 1
                hd = Heads(tr, step, HQ)
                here = [ev.at(step, "out10"), ev.at(step, "out11")]
                kv = hkv.rearrange("p t (h c) -> p t h c", h=HQ)
                tv = tr.do("act", lambda: act.copy(v, kv[:, :, :, P:]), here, hd.prior(f"pv{HQ - 1}"), name="tookv")
                qv = hq.rearrange("p t (h c) -> p t h c", h=HQ)
                qr = qv[:, :, :, NOPE:]
                cb, sn = bc(cosb[:, :, :], 2, HQ), bc(sinb[:, :, :], 2, HQ)
                ta = tr.do("dve", lambda: dve.tensor_tensor(t1, qr, cb, ALU.mult), here, la.kpt)
                tr.do("dve", lambda: dve.tensor_tensor(t2[:, :, :, 0:32], qr[:, :, :, 32:64], sn[:, :, :, 0:32], ALU.mult), here)
                tb_ = tr.do("dve", lambda: dve.tensor_tensor(t2[:, :, :, 32:64], qr[:, :, :, 0:32], sn[:, :, :, 32:64], ALU.mult), here)
                t = tr.do("dve", lambda: dve.tensor_tensor(qr, t1, t2, ALU.add), ta, tb_)
                yield
                copies = []
                jobs = [(qv, 0, P, qt, 0, "q"), (qv, 0, P, qt, 2, "q"), (kv, 0, P, kt, 0, "k"), (kv, 0, P, kt, 2, "k"),
                        (qv, NOPE, ROPE, qpt, 0, "p"), (qv, NOPE, ROPE, qpt, 2, "p")]
                for n, (src, c, m, dst, h0, kind) in enumerate(jobs):
                    b = Q + 1 + n % 3

                    def f(src=src, c=c, m=m, h0=h0, b=b):
                        for hh in range(2):
                            for tb in range(TB):
                                r = pe.transpose(ps[0:m, b, (hh * TB + tb) * P:(hh * TB + tb + 1) * P],
                                                 src[:, tb, h0 + hh, c:c + m], ident[:, :])
                        return r
                    tt = tr.do("pe", f, here, t if kind == "p" else None, copies[n - 3] if n >= 3 else
                               [hd.prior(f"pt{HQ - 1}"), hd.prior(f"fin{HQ - 1}")],
                               name={3: "tookk", 5: "tookq"}.get(n),
                               by_itself=(lambda b=b: pe.transpose(ps[:, b, 0:P], ident[:, :], ident[:, :]))
                               if kind == "p" else None)
                    copies.append(tr.do("act", lambda m=m, dst=dst, h0=h0, b=b: act.copy(
                        dst[0:m, h0:h0 + 2], ps[0:m, b, :].rearrange("p (h t) -> p h t", h=2)),
                        tt, hd.prior(f"sc{HQ - 1}")))
                    if n % 2:
                        yield
                for hh in range(HQ):
                    def scores(hh=hh):
                        for tb, (o, n) in enumerate(((0, P), (P, S))):
                            out_ = ps[:, Q, o:o + n]
                            pe.matmul(out_, qt[:, hh, tb * P:(tb + 1) * P], kt[:, hh, 0:n], start=True, stop=False)
                            m = pe.matmul(out_, qpt[0:ROPE, hh, tb * P:(tb + 1) * P], kpt[0:ROPE, 0:n],
                                          start=False, stop=True)
                        return m

                    def pv(hh=hh):
                        for tb in range(TB):
                            for kb in range(tb + 1):
                                m = pe.matmul(ps[:, Q + 2, tb * P:(tb + 1) * P], pt[:, (tb + kb) * P:(tb + kb + 1) * P],
                                              v[:, kb, hh, :], start=kb == 0, stop=kb == tb)
                        return m

                    def fin(rden, hh=hh):
                        for tb in range(TB):
                            c = index(quad) * (HQ * P) + hh * P
                            yy = y[:, tb, ds(c.v, P)]
                            m = dve.scalar_tensor_tensor(out=yy, in0=ps[:, Q + 2, tb * P:(tb + 1) * P],
                                                         scalar=rden[:, tb:tb + 1], in1=yy, op0=ALU.mult, op1=ALU.mult)
                        return m
                    parts = [(ps[:, Q, 0:P], mask[:, 0:P], sm[:, 0:P]), (ps[:, Q, P:3 * P], mask[:, P:], sm[:, P:])]
                    for _ in attend(hd, hh, scores, [copies, tv, la.kpt, t_mask, tg], parts, QH ** -0.5, 3, ps[:, Q + 1, :],
                                    pt, pv, fin, small[:, 16 + 8 * hh:24 + 8 * hh], gap=2):
                        yield

            base = nstep[0]
            nstep[0] += QUADS
            quad_projection(index(0), None, base)
            with pr.loop(1, QUADS) as i:
                side = quad_attention(i + -1)
                for _ in range(2):
                    next(side)
                quad_projection(i, side, base)
                quiet(side)
            end = tr.at(QUADS, f"fin{HQ - 1}")
            t = last_product("out1", a["mla_w_out"][0], quad_attention(index(QUADS - 1)), tr.at(QUADS - 1, f"fin{HQ - 1}"), end,
                             [ev.at(QUADS, "out10"), ev.at(QUADS, "out11")], ALPHA, last)
            return layer_norm(1, t, end)

        def token_rows(tr, dst, src, n, bank, after, free):
            t = tr.do("pe", lambda: [pe.transpose(ps[0:n, bank, tb * P:(tb + 1) * P], src(tb), ident[:, :])
                                     for tb in range(TB)][-1], after, free)
            return tr.do("dve", lambda: dve.tensor_copy(dst, ps[0:n, bank, 0:S]), t)

        def token_cols(tr, dst, src, n, bank, after, free):
            def f():
                for tb in range(TB):
                    m = pe.transpose(ps[:, bank, tb * n:(tb + 1) * n], src[0:n, tb * P:(tb + 1) * P], ident[0:n, 0:n])
                return m
            t = tr.do("pe", f, after, free)
            return tr.do("dve", lambda: dve.tensor_copy(
                dst, ps[:, bank, 0:TB * n].rearrange("p (t n) -> p t n", t=TB)), t)

        def selector(tr, sel, n, after):
            t = tr.do("pool", lambda: pool.memset(sel, 1.0), after)
            return tr.do("pool", lambda: pool.affine_select(
                out=sel, in_=sel, compare_op=ALU.is_equal, fill=0.0, base=0,
                pattern=[[-1, n], [0, P]], channel_multiplier=1), t)

        def ln_of_1_plus_exp(tr, dst, src, tmp, after, sign):
            t = tr.do("dve", lambda: dve.tensor_scalar(tmp, src, -1.0, None, ALU.mult), after)
            t = tr.do("dve", lambda: dve.tensor_tensor(tmp, tmp, src, ALU.min), t)
            t = tr.do("act", lambda: act.activation(tmp, tmp, ACT.Exp), t)
            t = tr.do("act", lambda: act.activation(tmp, tmp, ACT.Ln, bias=1.0), t)
            t2 = tr.do("dve", lambda: dve.tensor_scalar(dst, src, sign, 0.0, ALU.mult, ALU.max), after, t)
            return tr.do("dve", lambda: dve.tensor_tensor(dst, dst, tmp, ALU.add), t, t2)

        def layer2(ready, last):
            HA, W = 8, 1024
            HB, DB = 4, 256
            c_ = Carve()
            bias = c_(HA, 3 * P)
            braw = c_(HA, 3 * P)
            scratch = c_(TB, N)
            hqk = c_(2, TB, HALF)
            hv = c_(TB, HALF)
            v = c_(TB, HALF)
            sq = c_(2, TB, HALF)
            qt, kt = c_(2, S), c_(2, S)
            sm, pt = c_(3 * P), c_(3 * P)
            maskt = c_(3 * P)
            gif = c_(TB, 2 * HB)
            li, lf, tmp = c_(TB, HB), c_(TB, HB), c_(TB, HB)
            ifb = c_(2 * HB)
            rli, rlf, rb, ra, rm, rone = c_(S), c_(S), c_(S), c_(S), c_(S), c_(S)
            acol, ecol = c_(TB, HB), c_(TB, HB)
            sel = c_(HB, P)
            gq = c_(1)
            hbias = c_(2, 3 * P)
            w = a["ev_w_in_2"][0]
            rbias = a["ev_rel_bias_2"]
            tx = transposed(pr.track("xt2"), lambda tb, k: x[:, tb, k * P:(k + 1) * P], KT, xh, xl, lambda g: ready[g // 2],
                            gain=vcol("ev", KT))
            t_rms = []
            rms = rms_columns("rms2", ready, t_rms)
            NB = rbias.shape[2]
            tb_ = load("relb", braw, lambda: bass.AP(rbias.tensor, rbias.offset + 1, [[1, P], [NB, HA], [1, 3 * P]]), ready)
            t_ifb = load("ifb", ifb, lambda: row(a["ev_if_bias_2"], 2 * HB), ready)
            tr = pr.track("const2")
            for blk, (o, n) in enumerate(((0, P), (P, S))):
                off = braw.offset + (2 * P - 1 if blk == 0 else 3 * P - 1)
                rev = bass.AP(braw.tensor, off, [list(braw.ap[0]), [3 * P, HA], [-1, n]])
                t_bias = tr.do("dve", lambda o=o, n=n, rev=rev: dve.tensor_copy(bias[:, :, o:o + n], rev), tb_, ready)
            for o in (64, P + P + 64):
                t_bias = tr.do("dve", lambda o=o: dve.memset(bias[0:64, :, o:o + 64], NEG), t_bias)
            t = tr.do("pool", lambda: pool.memset(maskt, 0.0), ready)
            for o in (0, 2 * P):
                t = tr.do("pool", lambda o=o: pool.affine_select(
                    out=maskt[:, o:o + P], in_=maskt[:, o:o + P], compare_op=ALU.is_ge, fill=NEG, base=0,
                    pattern=[[1, P]], channel_multiplier=-1), t)
            t_maskt = t
            t_sel = selector(tr, sel[0:HB], HB, ready)
            t_one = tr.do("pool", lambda: pool.memset(rone[0:HB], 1.0), ready)
            t_gq = tr.do("dve", lambda: dve.tensor_scalar(gq, vcol("qn", 1), P ** -0.5, None, ALU.mult), ready)

            ev, tr = pr.track("ev2"), pr.track("att2")
            PAIRS = HA // 2

            def pair_projection(pair, side, base, between=None):
                ev.begin(pair + 1)
                tm = project(w, [(pair * HALF, HALF), (pair * HALF + W, HALF)], 0,
                             [ev.at(pair, "outq")], side, step=(pair * 2) + base, tx=tx)
                scaled_out(ev, lambda tb: hqk[:, :, tb], lambda tb: ps[:, tb, :].rearrange("p (b c) -> p b c", b=2),
                           tm, t_rms, tr.at(pair, "tookk"), name="outq")
                tm = project(w, [(pair * HALF + 2 * W, HALF), (pair * HALF + 3 * W, HALF)], 2,
                             [ev.at(pair, "outv"), ev.at(pair, "gate")], side, step=(pair * 2) + (base + 1), tx=tx)
                scaled_out(ev, lambda tb: hv[:, tb], lambda tb: ps[:, 2 + tb, 0:HALF],
                           tm, t_rms, tr.at(pair, "tookv"), name="outv")
                gate_out(ev, "gate", ps[:, 2:4, HALF:N], pair * HALF, HALF, tm,
                         scratch[:, :, 0:HALF], ev.at(pair, "gate"), hrstd)

            def pair_attention(pair):
                step = pair + 1
                hd = Heads(tr, step, 2)
                here = [ev.at(step, "outq"), ev.at(step, "outv"), ev.at(step, "gate")]
                tv = tr.do("act", lambda: act.copy(v, hv), here, hd.prior("pv1"), name="tookv")
                t_hb = tr.do("dve", lambda: dve.tensor_copy(hbias, bias[:, ds((index(pair) * 2).v, 2), :]),
                             t_bias, hd.prior("mask1"))
                t = tr.do("act", lambda: act.activation(sq, hqk, ACT.Square), here)
                t = tr.do("dve", lambda: dve.tensor_reduce(
                    small[:, 32:40], sq.rearrange("p b t (h d) -> p (b t h) d", h=2), AX.X, ALU.add), t)
                yield from turns(4)
                t = root_inverse(tr, small[:, 40:48], small[:, 32:40], 8, EPS, 1.0 / P, t)
                yield from turns(4)
                xv = hqk.rearrange("p b t (h d) -> p (b t h) d", h=2)
                t = tr.do("dve", lambda: dve.tensor_tensor(xv, xv, bc(small[:, 40:48], 2, P), ALU.mult), t)
                yield from turns(4)
                copies = []
                for n, (dst, g) in enumerate(((qt, gq), (kt, vcol("kn", 1)))):
                    def f(n=n):
                        for hh in range(2):
                            for tb in range(TB):
                                m = pe.transpose(ps[:, Q + 2 + n, (hh * TB + tb) * P:(hh * TB + tb + 1) * P],
                                                 hqk[:, n, tb, hh * P:(hh + 1) * P], ident[:, :])
                        return m
                    tt = tr.do("pe", f, t, hd.prior("fin1"), hd.prior("copy"), name="tookk" if n else None)
                    copies.append(tr.do("act", lambda n=n, dst=dst, g=g: act.activation(
                        dst, ps[:, Q + 2 + n, :].rearrange("p (h t) -> p h t", h=2), ACT.Copy, scale=g),
                        tt, t_gq, hd.prior("sc1"), name="copy"))
                yield
                for hh in range(2):
                    def scores(hh=hh):
                        for tb, (o, n) in enumerate(((0, P), (P, S))):
                            m = pe.matmul(ps[:, Q, o:o + n], qt[:, hh, tb * P:(tb + 1) * P], kt[:, hh, 0:n],
                                          start=True, stop=True)
                        return m

                    def pv(hh=hh):
                        for tb in range(TB):
                            for kb in range(tb + 1):
                                m = pe.matmul(ps[:, Q + 2, tb * P:(tb + 1) * P], pt[:, (tb + kb) * P:(tb + kb + 1) * P],
                                              v[:, kb, hh * P:(hh + 1) * P], start=kb == 0, stop=kb == tb)
                        return m

                    def fin(rden, hh=hh):
                        for tb in range(TB):
                            c = index(pair) * HALF + hh * P
                            yy = y[:, tb, ds(c.v, P)]
                            m = dve.scalar_tensor_tensor(out=yy, in0=ps[:, Q + 2, tb * P:(tb + 1) * P],
                                                         scalar=rden[:, tb:tb + 1], in1=yy, op0=ALU.mult, op1=ALU.mult)
                        return m
                    parts = [(ps[:, Q, 0:P], hbias[:, hh, 0:P], sm[:, 0:P]),
                             (ps[:, Q, P:3 * P], hbias[:, hh, P:], sm[:, P:])]
                    for _ in attend(hd, hh, scores, [copies, tv, t_hb], parts, 1.0, 3, ps[:, Q + 1, :],
                                    pt, pv, fin, small[:, 16 + 8 * hh:24 + 8 * hh], gap=3):
                        yield

            base = nstep[0]
            nstep[0] += 2 * PAIRS
            pair_projection(index(0), rms, base)
            with pr.loop(1, PAIRS) as i:
                side = pair_attention(i + -1)
                pair_projection(i, side, base)
                quiet(side)

            def gate_vectors():
                g = pr.track("mg")
                t = scaled_out(g, lambda tb: gif[:, tb], lambda tb: ps[:, tb, 0:2 * HB], tgm, t_rms, ready)
                mgate["read"] = t
                t = g.do("dve", lambda: dve.tensor_tensor(gif, gif, bc(ifb, 1, TB), ALU.add), t, t_ifb)
                yield
                t = g.do("dve", lambda: dve.tensor_copy(li, gif[:, :, 0:HB]), t)
                t = ln_of_1_plus_exp(g, lf, gif[:, :, HB:], tmp, t, -1.0)
                yield
                t1 = token_rows(g, rli[0:HB], lambda tb: li[:, tb], HB, Q + 3, t, side_end())
                t2 = token_rows(g, rlf[0:HB], lambda tb: lf[:, tb], HB, Q + 3, t1, None)
                yield
                t = g.do("dve", lambda: dve.tensor_tensor_scan(
                    rb[0:HB], rone[0:HB], rlf[0:HB], 0.0, ALU.mult, ALU.subtract), t2, t_one)
                t = g.do("dve", lambda: dve.tensor_tensor(ra[0:HB], rli[0:HB], rb[0:HB], ALU.subtract), t, t1)
                t = g.do("dve", lambda: dve.tensor_tensor_scan(
                    rm[0:HB], ra[0:HB], ra[0:HB], 0.0, ALU.max, ALU.max), t)
                t = g.do("dve", lambda: dve.tensor_tensor(rb[0:HB], rb[0:HB], rm[0:HB], ALU.add), t)
                yield
                t3 = token_cols(g, acol, ra, HB, Q + 3, t, t2)
                t4 = token_cols(g, ecol, rb, HB, Q + 3, t, t3)
                mgate["t"] = [g.do("act", lambda: act.activation(ecol, ecol, ACT.Exp, scale=-1.0), t4), t3, t]
                yield

            mgate = {}
            side = pair_attention(index(PAIRS - 1))
            side_end = lambda: tr.at(PAIRS, "fin1")
            tgm = project(w, [(9 * W, 2 * HB)], 0, [ev.at(PAIRS, "outq"), ev.at(PAIRS, "outv")], side, tx=tx)
            quiet(side)
            gv = gate_vectors()
            next(gv)
            tz = gates("gate2", w, 8 * W, W, 2, [mgate["read"], ev.at(PAIRS, "gate"), ev.at(PAIRS, "outv")],
                       scratch, gv, half=hrstd, tx=tx)
            quiet(gv)

            c_ = Carve()
            mqk = c_(TB, 2 * DB)
            hvo = c_(TB, 2 * DB)
            va = c_(TB, DB + 1)
            mqt, mkt = c_(2, S), c_(2, S)
            wt = c_(3 * P)
            sT = c_(3 * P)
            assert c_.at <= 2 * HA * 3 * P
            em, tm_ = pr.track("ev2m"), pr.track("mlstm")
            t_va = pr.track("va").do("pool", lambda: pool.memset(va[:, :, DB:], 1.0), side_end())

            def head_projection(head, side, base):
                em.begin(head + 1)
                tm = project(w, [(head * DB + 4 * W, DB), (head * DB + 5 * W, DB)], 0,
                             [em.at(head, "outq"), mgate["read"], tz], side, step=(head * 2) + base, tx=tx)
                scaled_out(em, lambda tb: mqk[:, tb], lambda tb: ps[:, tb, :],
                           tm, t_rms, tm_.at(head, "tookk"), side_end(), name="outq")
                tm = project(w, [(head * DB + 6 * W, DB), (head * DB + 7 * W, DB)], 2,
                             [em.at(head, "outv"), tz], side, step=(head * 2) + (base + 1), tx=tx)
                scaled_out(em, lambda tb: hvo[:, tb, 0:DB], lambda tb: ps[:, 2 + tb, 0:DB],
                           tm, t_rms, tm_.at(head, "tookv"), side_end())
                for tb in range(TB):
                    em.do("act", lambda tb=tb: act.activation(
                        hvo[:, tb, DB:], ps[:, 2 + tb, DB:], ACT.Tanh, scale=hrstd[:, tb:tb + 1]),
                        tm, tm_.at(head, "tooko"), name="outv")

            def head_mlstm(head):
                step = head + 1
                tr = tm_
                tr.begin(step)
                prior = lambda n: tr.at(index(step) + -1, n)
                here = [em.at(step, "outq"), em.at(step, "outv")]
                c = index(head) * DB + W
                tv = tr.do("act", lambda: act.copy(va[:, :, 0:DB], hvo[:, :, 0:DB]), here, t_va, prior("pv"), name="tookv")
                tg = tr.do("dve", lambda: dve.scalar_tensor_tensor(
                    out=y[:, :, ds(c.v, DB)], in0=hvo[:, :, DB:], scalar=1.0, in1=y[:, :, ds(c.v, DB)],
                    op0=ALU.add, op1=ALU.mult), here, tz, name="tooko")
                copies = []
                for n, dst in enumerate((mqt, mkt)):
                    def f(n=n):
                        for kd in range(2):
                            for tb in range(TB):
                                o = n * DB + kd * P
                                m = pe.transpose(ps[:, Q + n, (kd * TB + tb) * P:(kd * TB + tb + 1) * P],
                                                 mqk[:, tb, o:o + P], ident[:, :])
                        return m
                    tt = tr.do("pe", f, here, prior("wt") if n == 0 else prior("st"), prior("fin"),
                               name="tookk" if n else None)
                    copies.append(tr.do("act", lambda n=n, dst=dst: act.activation(
                        dst, ps[:, Q + n, :].rearrange("p (k t) -> p k t", k=2), ACT.Copy,
                        scale=DB ** -0.5 if n == 0 else 1.0), tt, prior("sc"), name=f"copy{n}"))
                yield
                tsel = tr.do("dve", lambda: dve.tensor_copy(selh, sel[0:HB, ds(index(head).v, 1), :]
                                                            .rearrange("p a b -> p (a b)")),
                             t_sel, mgate["t"], prior("wt"))
                t = tr.do("pe", lambda: pe.matmul(ps[:, Q, 0:S], selh, rm[0:HB], start=True, stop=True),
                          copies, tsel, mgate["t"])
                t1 = tr.do("dve", lambda: dve.scalar_tensor_tensor(
                    out=wt[:, 0:S], in0=ps[:, Q, 0:S], scalar=-1.0, in1=maskt[:, 0:S], op0=ALU.mult, op1=ALU.add),
                    t, t_maskt, prior("st"))
                t2 = tr.do("dve", lambda: dve.scalar_tensor_tensor(
                    out=wt[:, S:], in0=ps[:, Q, P:S], scalar=-1.0, in1=maskt[:, S:], op0=ALU.mult, op1=ALU.add),
                    t, t_maskt, prior("st"), name="wt")
                ac = lambda tb: acolh[:, tb:tb + 1]
                tac = tr.do("dve", lambda: dve.tensor_copy(
                    headcols[:, 0:2], acol[:, :, ds(index(head).v, 1)]
                    .rearrange("p t a -> p (t a)")), mgate["t"], prior("fin"), prior("exp"))
                tec = tr.do("dve", lambda: dve.tensor_copy(
                    headcols[:, 2:4], ecol[:, :, ds(index(head).v, 1)]
                    .rearrange("p t a -> p (t a)")), mgate["t"], prior("fin"))
                te = tr.do("act", lambda: act.activation(wt[:, 0:S], wt[:, 0:S], ACT.Exp, bias=ac(0)), t1, tac)
                te = tr.do("act", lambda: act.activation(wt[:, S:], wt[:, S:], ACT.Exp, bias=ac(1)), t2, tac, name="exp")

                def scores():
                    for kb, (o, n, t0) in enumerate(((0, S, 0), (S, P, P))):
                        for kd in range(2):
                            m = pe.matmul(ps[:, Q + 1, o:o + n], mkt[:, kd, kb * P:(kb + 1) * P], mqt[:, kd, t0:t0 + n],
                                          start=kd == 0, stop=kd == 1)
                    return m
                t = tr.do("pe", scores, copies, name="sc")
                tst = tr.do("dve", lambda: dve.tensor_tensor(sT, ps[:, Q + 1, 0:3 * P], wt, ALU.mult), t, te,
                            prior("pv"), name="st")
                yield
                yield

                def pv():
                    for tb in range(TB):
                        for kb in range(tb + 1):
                            o = tb * P if kb == 0 else S
                            m = pe.matmul(ps[:, Q + 2 + tb, 0:DB + 1], sT[:, o:o + P], va[:, kb, :],
                                          start=kb == 0, stop=kb == tb)
                    return m
                tp = tr.do("pe", pv, tst, tv, prior("fin"), name="pv")
                den, neg = headcols[:, 4:6], headcols[:, 6:8]
                dsrc = ps[:, Q + 2:Q + 4, DB]
                t = tr.do("dve", lambda: dve.tensor_copy(den, dsrc), tp)
                t = tr.do("dve", lambda: dve.tensor_scalar(neg, den, -1.0, None, ALU.mult), t)
                t = tr.do("dve", lambda: dve.tensor_tensor(den, den, neg, ALU.max), t)
                t = tr.do("dve", lambda: dve.tensor_tensor(den, den, headcols[:, 2:4], ALU.max), t, tec)
                t = tr.do("dve", lambda: dve.tensor_scalar(den, den, 2.0, None, ALU.mult), t)
                t = tr.do("dve", lambda: dve.reciprocal(den, den), t)
                for tb in range(TB):
                    tf = tr.do("dve", lambda tb=tb: dve.scalar_tensor_tensor(
                        out=y[:, tb, ds(c.v, DB)], in0=ps[:, Q + 2 + tb, 0:DB], scalar=den[:, tb:tb + 1],
                        in1=y[:, tb, ds(c.v, DB)], op0=ALU.mult, op1=ALU.mult), t, tg, tp, name="fin")
                yield

            headcols = small[:, 64:72]
            acolh = headcols[:, 0:2]
            selh = rlf[0:HB, 0:P]
            base = nstep[0]
            nstep[0] += 2 * HB
            head_projection(index(0), None, base)
            with pr.loop(1, HB) as i:
                side = head_mlstm(i + -1)
                head_projection(i, side, base)
                quiet(side)
            return last_product("out2", a["ev_w_out_2"][0], head_mlstm(index(HB - 1)), [tm_.at(HB - 1, "fin"), side_end()],
                                tm_.at(HB, "fin"), [em.at(HB, "outq"), em.at(HB, "outv")], 1.0, last)

        def layer3(ready, last):
            H, W = 8, 1024
            fine[0] = True
            HP = H // 2
            PAD = 4
            c_ = Carve()
            hx = c_(TB, HALF)
            cp = c_(2, PAD + S)
            xc, gt = c_(2, S), c_(2, S)
            A, L, X = c_(2, S), c_(2, S), c_(2, S)
            gw = c_(H, 2 * P)
            gwc = c_(2, 2 * P)
            scratch = c_(TB, HALF)
            sp = c_(H)
            tmp8, hgb = c_(H), c_(2 * H)
            ab = c_(TB, 2 * H)
            alog, dtb = c_(H), c_(H)
            beta, gg, gtmp = c_(TB, H), c_(TB, H), c_(TB, H)
            rdec = c_(S)
            dcol = c_(TB, H)
            sel = c_(H, P)
            mincl = c_(P)
            strict = c_(P)
            lev = c_(7, P)
            onorm = c_(P)
            hh4 = c_(3, TB, HALF)
            selc = c_(2, P)
            cpd = c_(6, PAD + S)
            QT, KTt, VT = c_(2, S), c_(2, S), c_(2, S)
            E = c_(2, 3 * P)
            u = c_(2, TB, P)
            TRN = c_(2, 4 * P)
            AD = c_(4, P)
            M, Mt, Z, B = c_(4, P), c_(4, P), c_(4, P), c_(4, P)
            rg = M.rearrange("p a b -> p (a b)")[:, 0:S]
            rone = Mt.rearrange("p a b -> p (a b)")[:, 0:S]
            w = a["od_w_in_2"][0]

            tx = transposed(pr.track("xt3"), lambda tb, k: x[:, tb, k * P:(k + 1) * P], KT, xh, xl, lambda g: ready[g // 2],
                            gain=vcol("od", KT))
            t_rms = []
            rms = rms_columns("rms3", ready, t_rms)
            t_gw = load("gw", gw, lambda: a["od_gate_w_2"][0].rearrange("n c d -> c n d"), ready)
            t_al = load("alog", alog, lambda: row(a["od_a_log_2"], H), ready)
            t_dt = load("dtb", dtb, lambda: row(a["od_dt_bias_2"], H), ready)
            t_on = load("onorm", onorm, lambda: row(a["od_onorm_2"], P), ready)
            tr = pr.track("const3")
            t = tr.do("pool", lambda: pool.memset(mincl, 0.0), ready)
            t_incl = causal(tr, mincl, P, 0, t)
            t = tr.do("pool", lambda: pool.memset(strict, 1.0), ready)
            t_strict = tr.do("pool", lambda: pool.affine_select(
                out=strict, in_=strict, compare_op=ALU.is_gt, fill=0.0, base=0,
                pattern=[[-1, P]], channel_multiplier=1), t)
            ia, ib = (X[:, n, 0:P].bitcast(I32) for n in (0, 1))
            t = tr.do("pool", lambda: pool.iota(ia, [[0, P]], base=0, channel_multiplier=1), ready)
            t = tr.do("pool", lambda: pool.iota(ib, [[1, P]], base=0, channel_multiplier=0), t)
            t = tr.do("dve", lambda: dve.tensor_tensor(ia, ia, ib, ALU.bitwise_xor), t)
            for l in range(7):
                t = tr.do("dve", lambda l=l: dve.tensor_scalar(ib, ia, l, None, ALU.logical_shift_right), t)
                t = tr.do("dve", lambda l=l: dve.tensor_scalar(lev[:, l], ib, 1.0, None, ALU.is_equal), t)
            t_lev = t
            t_cp = tr.do("pool", lambda: pool.memset(cp[:, :, 0:PAD], 0.0), ready)
            t_cpd = tr.do("pool", lambda: pool.memset(cpd[:, :, 0:PAD], 0.0), ready)
            t_sel = selector(tr, sel[0:H], H, ready)
            t_one = tr.do("pool", lambda: pool.memset(rone[0:H], 1.0), ready)
            t = ln_of_1_plus_exp(tr, sp, vcol("lam", H), tmp8, ready, -1.0)
            t_sp = tr.do("dve", lambda: dve.tensor_scalar(sp, sp, 4.0, None, ALU.mult), t)
            t_gb = tr.do("dve", lambda: dve.tensor_scalar(hgb, vcol("gb", 2 * H), 0.5, None, ALU.mult), ready)


            def taps(tr, jobs, after, name):
                t = [after] * len(jobs)
                for j in range(4):
                    for n, (out_, src, wc, bias) in enumerate(jobs):
                        s0 = src[:, PAD - 3 + j:PAD - 3 + j + S]
                        if j:
                            f = lambda out_=out_, s0=s0, wc=wc, j=j: dve.scalar_tensor_tensor(
                                out=out_, in0=s0, scalar=wc(j), in1=out_, op0=ALU.mult, op1=ALU.add)
                        elif bias is None:
                            f = lambda out_=out_, s0=s0, wc=wc: dve.tensor_scalar(out_, s0, wc(0), None, ALU.mult)
                        else:
                            f = lambda out_=out_, s0=s0, wc=wc, bias=bias: dve.tensor_scalar(
                                out_, s0, wc(0), bias, ALU.mult, ALU.add)
                        t[n] = tr.do("dve", f, t[n], name=name if j == 3 and n == len(jobs) - 1 else None)
                    if j % 2:
                        yield
                return t

            ev, rg_ = pr.track("ev3"), pr.track("lru")
            evd, dl = pr.track("evd"), pr.track("delta")
            done3 = {}

            def blocks_projection(pair, side, base):
                ev.begin(pair + 1)
                tm = project(w, [(pair * HALF + W, HALF), (pair * HALF, HALF)], 0,
                             [evd.at(pair + 1, "outq")], side, step=(pair * 3) + (base + 2), tx=tx)
                scaled_out(ev, lambda tb: hx[:, tb], lambda tb: ps[:, tb, HALF:N],
                           tm, t_rms, rg_.at(pair, "took"), name="out")
                gate_out(ev, "gate", ps[:, 0:2, 0:HALF], pair * HALF, HALF, tm, scratch,
                         evd.at(pair + 1, "gate"), hrstd)

            def blocks_lru(pair):
                tr = rg_
                tr.begin(pair + 1)
                prior = lambda n: tr.at(index(pair), n)
                here = [ev.at(pair + 1, "out"), ev.at(pair + 1, "gate")]

                def f():
                    for n in range(2):
                        for tb in range(TB):
                            m = pe.transpose(ps[:, Q, (n * TB + tb) * P:(n * TB + tb + 1) * P],
                                             hx[:, tb, n * P:(n + 1) * P], ident[:, :])
                    return m
                t = tr.do("pe", f, here, prior("cp"), dl.at(pair, "fin1"), done3["t"], name="took")
                t = tr.do("act", lambda: act.copy(cp[:, :, PAD:], ps[:, Q, :].rearrange("p (n t) -> p n t", n=2)),
                          t, t_cp, prior("conv"), name="cp")
                yield from turns(2)
                hc = small[:, 80:80 + 16]
                o = col["cw"]
                cwv = vec[:, o:o + 32].rearrange("p (j c) -> p c j", c=8)
                bk = lambda: (index(pair) * 2).v
                tcs = [tr.do("dve", lambda: dve.tensor_copy(
                    hc[:, 0:8].rearrange("p (c j) -> p c j", c=2), cwv[:, ds(bk(), 2), :]), prior("conv"), ready),
                    tr.do("dve", lambda: dve.tensor_copy(hc[:, 8:10], vec[:, ds(bk() + col["cb"], 2)]), prior("conv"), ready),
                    tr.do("dve", lambda: dve.tensor_copy(hc[:, 10:12], hgb[:, ds(bk(), 2)]), prior("i1"), t_gb),
                    tr.do("dve", lambda: dve.tensor_copy(hc[:, 12:14], hgb[:, ds(bk() + H, 2)]), prior("i1"), t_gb),
                    tr.do("dve", lambda: dve.tensor_copy(hc[:, 14:16], sp[:, ds(bk(), 2)]), prior("i1"), t_sp)]
                tgc = tr.do("dve", lambda: dve.tensor_copy(gwc, gw[:, ds(bk(), 2), :]), t_gw, prior("gates"))
                tconv = yield from taps(tr, [
                    (xc[:, n], cp[:, n], lambda j, n=n: hc[:, 4 * n + j:4 * n + j + 1], hc[:, 8 + n:9 + n])
                    for n in range(2)], [t, tcs, prior("gates"), prior("ix")], "conv")
                for n in range(2):
                    bank = Q + 1 + n

                    def g(n=n, bank=bank):
                        for s in range(2):
                            m = pe.matmul(ps[:, bank, s * S:(s + 1) * S], gwc[:, n, s * P:(s + 1) * P], xc[:, n],
                                          start=True, stop=True)
                        return m
                    t = tr.do("pe", g, tconv, tgc, prior("i1"), name="gates")
                    yield
                    t1 = tr.do("act", lambda n=n, bank=bank: act.activation(
                        gt[:, 0], ps[:, bank, 0:S], ACT.Tanh, scale=0.5, bias=hc[:, 10 + n:11 + n]), t,
                        gfree[0] if n else prior("tw"))
                    t2 = tr.do("act", lambda n=n, bank=bank: act.activation(
                        gt[:, 1], ps[:, bank, S:N], ACT.Tanh, scale=0.5, bias=hc[:, 12 + n:13 + n]), t,
                        gfree[0] if n else prior("tw"), name="i1")
                    yield
                    t3 = tr.do("dve", lambda n=n: dve.tensor_scalar(
                        L[:, n], gt[:, 0], 1.0, hc[:, 14 + n:15 + n], ALU.add, ALU.mult), t1, prior("turned"))
                    gfree[0] = tr.do("dve", lambda n=n: dve.scalar_tensor_tensor(
                        out=X[:, n], in0=gt[:, 1], scalar=1.0, in1=xc[:, n], op0=ALU.add, op1=ALU.mult),
                        t2, t_lev, prior("scan"), name="ix")
                    yield
                    t4 = tr.do("act", lambda n=n: act.activation(A[:, n], L[:, n], ACT.Exp, scale=-1.0), t3, prior("scan"))
                    th = tr.do("act", lambda n=n: act.activation(L[:, n], L[:, n], ACT.Tanh), t3, t4)
                    yield
                whole = lambda v: v.rearrange("p a b -> p (a b)")
                t = tr.do("dve", lambda: dve.tensor_scalar(whole(gt), whole(L), 1.0, None, ALU.add), th, gfree[0])
                for n in range(2):
                    t = tr.do("dve", lambda n=n: dve.reciprocal(gt[:, n], gt[:, n]), t)
                    yield from turns(3)
                t = tr.do("dve", lambda: dve.scalar_tensor_tensor(
                    out=whole(L), in0=whole(L), scalar=2.0, in1=whole(gt), op0=ALU.mult, op1=ALU.mult), t, name="tw")
                yield
                t = tr.do("act", lambda: act.activation(whole(L), whole(L), ACT.Sqrt), t)
                yield from turns(2)
                t = tr.do("dve", lambda: dve.scalar_tensor_tensor(
                    out=whole(X), in0=whole(X), scalar=0.5, in1=whole(L), op0=ALU.mult, op1=ALU.mult), t, gfree[0])
                for n in range(2):
                    ts = tr.do("dve", lambda n=n: dve.tensor_tensor_scan(
                        L[:, n], A[:, n], X[:, n], 0.0, ALU.mult, ALU.add), t, t4, name="scan")
                yield from turns(2)

                def states():
                    for n in range(2):
                        for tb in range(TB):
                            m = pe.transpose(ps[:, Q + 3, (tb * 2 + n) * P:(tb * 2 + n + 1) * P],
                                             L[:, n, tb * P:(tb + 1) * P], ident[:, :])
                    return m
                t = tr.do("pe", states, ts, prior("end"), name="turned")
                c = index(pair) * HALF
                yy = lambda: y[:, :, ds(c.v, HALF)]
                tr.do("dve", lambda: dve.tensor_tensor(
                    yy(), ps[:, Q + 3, :].rearrange("p (t c) -> p t c", t=TB), yy(), ALU.mult), t, here, name="end")
                yield
            gfree = [None]

            def delta_gates():
                tr = pr.track("dg")
                t = scaled_out(tr, lambda tb: ab[:, tb], lambda tb: ps[:, 2 + tb, 0:2 * H], tgm, t_rms, ready)
                done3["read"] = t
                tbt = tr.do("act", lambda: act.activation(beta, ab[:, :, H:], ACT.Tanh, scale=0.5), t)
                tbt = tr.do("dve", lambda: dve.tensor_scalar(beta, beta, 0.5, 0.5, ALU.mult, ALU.add), tbt)
                te = tr.do("act", lambda: act.activation(alog, alog, ACT.Exp), t_al)
                t = tr.do("dve", lambda: dve.tensor_tensor(ab[:, :, 0:H], ab[:, :, 0:H], bc(dtb, 1, TB), ALU.add), t, t_dt)
                yield
                t = ln_of_1_plus_exp(tr, gg, ab[:, :, 0:H], gtmp, t, 1.0)
                t = tr.do("dve", lambda: dve.tensor_tensor(gg, gg, bc(alog, 1, TB), ALU.mult), t, te)
                yield
                t = token_rows(tr, rg[0:H], lambda tb: gg[:, tb], H, Q + 2, t, None)
                for tb in range(TB):
                    o = slice(tb * P, (tb + 1) * P)
                    t = tr.do("dve", lambda o=o: dve.tensor_tensor_scan(
                        rdec[0:H, o], rone[0:H, o], rg[0:H, o], 0.0, ALU.mult, ALU.subtract), t, t_one)
                yield
                done3["t"] = [token_cols(tr, dcol, rdec, H, Q + 2, t, None), t, tbt]
                yield

            def delta_projection(pair, side, base):
                evd.begin(pair + 1)
                tm = project(w, [(pair * HALF + 2 * W, HALF), (pair * HALF + 3 * W, HALF)], 0,
                             [ev.at(pair, "gate"), evd.at(pair, "outq")], side, step=(pair * 3) + base, tx=tx)
                scaled_out(evd, lambda tb: hh4[:, 0:2, tb], lambda tb: ps[:, tb, :].rearrange("p (b c) -> p b c", b=2),
                           tm, t_rms, dl.at(pair, "took"), name="outq")
                tm = project(w, [(pair * HALF + 4 * W, HALF), (pair * HALF + 5 * W, HALF)], 2,
                             [evd.at(pair, "gate"), done3["read"]], side, step=(pair * 3) + (base + 1), tx=tx)
                scaled_out(evd, lambda tb: hh4[:, 2, tb], lambda tb: ps[:, 2 + tb, 0:HALF],
                           tm, t_rms, dl.at(pair, "took"), name="outv")
                gate_out(evd, "gate", ps[:, 2:4, HALF:N], pair * HALF + W, HALF, tm, scratch,
                         [evd.at(pair, "gate"), ev.at(pair, "gate")], hrstd)

            def delta_heads(pair):
                tr = dl
                tr.begin(pair + 1)
                prior = lambda n: tr.at(index(pair), n)
                here = [evd.at(pair + 1, "outq"), evd.at(pair + 1, "outv"), evd.at(pair + 1, "gate")]
                hidx = lambda: (index(pair) * 2).v
                cps = []
                for n in range(3):
                    bank = Q + n % 2

                    def f(n=n, bank=bank):
                        for hh in range(2):
                            for tb in range(TB):
                                m = pe.transpose(ps[:, bank, (hh * TB + tb) * P:(hh * TB + tb + 1) * P],
                                                 hh4[:, n, tb, hh * P:(hh + 1) * P], ident[:, :])
                        return m
                    t = tr.do("pe", f, here, rg_.at(pair + 1, "end"), cps[0] if n == 2 else [prior("od1"), prior("qk1"), prior("lvl")],
                              name="took")
                    cps.append(tr.do("act", lambda n=n, bank=bank: act.copy(
                        cpd[:, 2 * n:2 * n + 2, PAD:], ps[:, bank, :].rearrange("p (h t) -> p h t", h=2)),
                        t, t_cpd, prior("convv" if n == 2 else "conv")))
                yield from turns(2)
                hc = small[:, 100:140]
                cdv = vec[:, 0:96].rearrange("p (j c) -> p c j", c=24)
                tcs = [tr.do("dve", lambda n=n: dve.tensor_copy(
                    hc[:, 8 * n:8 * n + 8].rearrange("p (c j) -> p c j", c=2),
                    cdv[:, ds(hidx() + 8 * n, 2), :]), prior("conv"), prior("convv"), ready) for n in range(3)]
                tcs += [tr.do("dve", lambda o=o, src=src: dve.tensor_copy(
                    hc[:, o:o + 4].rearrange("p (t c) -> p t c", t=TB), src[:, :, ds(hidx(), 2)]),
                    prior("fin1"), prior("E1"), done3["t"]) for o, src in ((24, beta), (28, dcol))]
                tsel = tr.do("dve", lambda: dve.tensor_copy(selc[0:H], sel[0:H, ds(hidx(), 2), :]), t_sel, prior("R1"))
                dec = lambda hh, tb: hc[:, 28 + 2 * tb + hh:29 + 2 * tb + hh]
                dsts = (QT, KTt, VT)
                def jobs(n):
                    return [(dsts[n][:, hh], cpd[:, 2 * n + hh],
                             lambda j, c=2 * n + hh: hc[:, 4 * c + j:4 * c + j + 1], None) for hh in range(2)]
                flatE, flatT = (v_.rearrange("p a b -> p (a b)") for v_ in (E, TRN))
                scr = [flatE[:, 0:S], flatE[:, S:2 * S]] + [flatT[:, m * S:(m + 1) * S] for m in range(4)]
                outs_ = []

                def silus(n, after):
                    t1 = [tr.do("act", lambda hh=hh: act.activation(
                        scr[2 * n + hh], dsts[n][:, hh], ACT.Tanh, scale=0.5),
                        after[hh], prior("st"), prior("uu"), prior("od1")) for hh in range(2)]
                    yield
                    for hh in range(2):
                        outs_.append(tr.do("dve", lambda hh=hh: dve.scalar_tensor_tensor(
                            out=dsts[n][:, hh], in0=scr[2 * n + hh], scalar=1.0, in1=dsts[n][:, hh],
                            op0=ALU.add, op1=ALU.mult), t1[hh]))
                free = [prior("kk1"), prior("qk1"), prior("vt")]
                temps = [v_.rearrange("p a b -> p (a b)")[:, m * S:(m + 1) * S] for v_ in (Z, B, AD) for m in range(2)]
                ends = []
                for hh, (dst, src, wc, _) in enumerate(jobs(2)):
                    parts = [dst] + temps[3 * hh:3 * hh + 3]
                    for j in range(4):
                        tp = tr.do("act", lambda j=j, src=src, wc=wc, parts=parts: act.activation(
                            parts[j], src[:, PAD - 3 + j:PAD - 3 + j + S], ACT.Copy, scale=wc(j)),
                            cps, tcs, free, prior("fin1"), name="convv")
                    for j in range(1, 4):
                        tp = tr.do("pool", lambda j=j, parts=parts: pool.tensor_tensor(
                            parts[0], parts[0], parts[j], ALU.add), tp)
                    ends.append(tp)
                for n in range(2):
                    yield from silus(n, (yield from taps(tr, jobs(n), [cps, tcs, free], "conv" if n else None)))
                    yield
                yield from silus(2, ends)
                yield
                for n in range(2):
                    ts_ = tr.do("act", lambda n=n: act.activation(
                        (M if n == 0 else Mt).rearrange("p a b -> p (a b)"),
                        dsts[n].rearrange("p a b -> p (a b)"), ACT.Square, scale=0.5), outs_, prior("lvl"), prior("uu"))
                yield from turns(6)

                def ssq():
                    for n, m_ in enumerate((M, Mt)):
                        for k in range(4):
                            r = pe.matmul(ps[:, Q, 4 * n + k:4 * n + k + 1], m_[:, k, :], ones[:, 0:1],
                                          start=True, stop=True)
                    return r
                t = tr.do("pe", ssq, ts_, cps)
                def vturn():
                    for hh in range(2):
                        for tb in range(TB):
                            m = pe.transpose(ps[:, Q + 1, (hh * TB + tb) * P:(hh * TB + tb + 1) * P],
                                             VT[:, hh, tb * P:(tb + 1) * P], ident[:, :])
                    return m
                tvt = tr.do("pe", vturn, outs_, cps, name="vt")
                sc = small[:, 144:176]
                t = tr.do("dve", lambda: dve.tensor_scalar(sc[:, 0:8], ps[:, Q, 0:8], EPS, None, ALU.add), t, prior("fin1"))
                t = tr.do("pool", lambda: pool.tensor_tensor(sc[:, 0:8], sc[:, 0:8], nhalf[:, 0:8], ALU.pow), t)
                yield from turns(4)
                bh = hc[:, 24:28].rearrange("p (t h) -> p h t", t=TB)
                rk = sc[:, 4:8].rearrange("p (h t) -> p h t", h=2)
                rb_ = sc[:, 8:12].rearrange("p (h t) -> p h t", h=2)
                c2 = sc[:, 12:16].rearrange("p (h t) -> p h t", h=2)
                t1 = tr.do("dve", lambda: dve.scalar_tensor_tensor(
                    out=rb_, in0=rk, scalar=0.5, in1=bh, op0=ALU.mult, op1=ALU.mult), t, tcs)
                t2 = tr.do("dve", lambda: dve.scalar_tensor_tensor(
                    out=c2, in0=rk, scalar=0.5, in1=rb_, op0=ALU.mult, op1=ALU.mult), t1)
                rq = tr.do("dve", lambda: dve.tensor_scalar(
                    sc[:, 16:20], sc[:, 0:4], 0.25 * P ** -0.5, None, ALU.mult), t)
                tu = tr.do("dve", lambda: dve.tensor_tensor(
                    u.rearrange("p h t d -> p (h t) d"), ps[:, Q + 1, :].rearrange("p (k d) -> p k d", k=4),
                    bc(sc[:, 8:12], 2, P), ALU.mult), t1, tvt, prior("od1"), prior("uu"))
                yield
                for hh in range(2):
                    t = tr.do("pe", lambda hh=hh: pe.matmul(ps[:, Q, 0:S], selc[0:H, hh, :], rdec[0:H],
                                                            start=True, stop=True),
                              tsel, done3["t"], tu, prior("lvl"), dfree[0] if hh else None, name=f"R{hh}")
                    td = tr.do("dve", lambda hh=hh: dve.tensor_tensor(
                        sc[:, 20:21], ps[:, Q, P - 1:P], dec(hh, 1), ALU.add), t, tcs, dfree[0] if hh else None)
                    e0 = E[:, hh]
                    te = tr.do("dve", lambda hh=hh, e0=e0: dve.scalar_tensor_tensor(
                        out=e0[:, 0:P], in0=ps[:, Q, 0:P], scalar=-1.0, in1=mincl,
                        op0=ALU.mult, op1=ALU.add), t, t_incl, outs_)
                    te = tr.do("dve", lambda hh=hh, e0=e0: dve.tensor_scalar(
                        e0[:, P:S], ps[:, Q, 0:P], -1.0, None, ALU.mult), t, outs_)
                    te = tr.do("dve", lambda hh=hh, e0=e0: dve.scalar_tensor_tensor(
                        out=e0[:, S:], in0=ps[:, Q, P:S], scalar=-1.0, in1=mincl,
                        op0=ALU.mult, op1=ALU.add), t, t_incl, outs_)
                    yield
                    for n, bcol_ in enumerate((dec(hh, 0), sc[:, 20:21], dec(hh, 1))):
                        te2 = tr.do("act", lambda n=n, e0=e0, bcol_=bcol_: act.activation(
                            e0[:, n * P:(n + 1) * P], e0[:, n * P:(n + 1) * P], ACT.Exp, bias=bcol_), te, td, tcs,
                            name=f"E{hh}")

                    def kk(hh=hh, other=KTt, bank=Q + 1):
                        pe.matmul(ps[:, bank, 0:P], other[:, hh, 0:P], KTt[:, hh, 0:P], start=True, stop=True)
                        return pe.matmul(ps[:, bank, P:3 * P], other[:, hh, P:S], KTt[:, hh, :], start=True, stop=True)
                    tk = tr.do("pe", kk, outs_, tu, name=f"kk{hh}")
                    tq_ = tr.do("pe", lambda kk=kk: kk(other=QT, bank=Q + 2), outs_, prior("od1"), dfree[1] if hh else None,
                                name=f"qk{hh}")
                    yield from turns(2)
                    ta_ = []
                    T4 = TRN[:, hh]
                    for n, (s0, cc_) in enumerate(((0, 0), (1, 1), (2, 1))):
                        col_ = sc[:, 12 + 2 * hh + cc_:13 + 2 * hh + cc_]
                        dst = AD[:, 2 * hh] if n == 0 else (AD[:, 2 * hh + 1] if n == 2 else T4[:, 0:P])
                        ta_.append(tr.do("dve", lambda n=n, dst=dst, col_=col_, e0=e0: dve.scalar_tensor_tensor(
                            out=dst, in0=ps[:, Q + 1, n * P:(n + 1) * P], scalar=col_, in1=e0[:, n * P:(n + 1) * P],
                            op0=ALU.mult, op1=ALU.mult), tk, te2, t2, outs_))
                    for n in range(2):
                        ta_.append(tr.do("dve", lambda n=n, hh=hh: dve.tensor_tensor(
                            AD[:, 2 * hh + n], AD[:, 2 * hh + n], strict, ALU.mult), ta_[0], ta_[2], t_strict))
                    tqk = tr.do("dve", lambda hh=hh, T4=T4, e0=e0: dve.tensor_tensor(
                        T4[:, P:], ps[:, Q + 2, 0:3 * P], e0, ALU.mult), tq_, te2, outs_)
                    yield from turns(2)

                    def turn4(T4=T4):
                        for n in range(4):
                            m = pe.transpose(ps[:, Q + 3, n * P:(n + 1) * P], T4[:, n * P:(n + 1) * P], ident[:, :])
                        return m
                    tt = tr.do("pe", turn4, tqk, ta_, prior("fin1"), dfree[2] if hh else None)
                    tn_ = tr.do("act", lambda T4=T4: act.copy(T4, ps[:, Q + 3, :]), tt, name="st")
                    dfree[0:3] = [[te, ta_], tqk, tn_]
                    yield
                four = lambda b_: b_.rearrange("p a b -> p (a b)")
                tb0 = tr.do("pool", lambda: pool.tensor_tensor(B, AD, bc(lev[:, 0], 1, 4), ALU.mult), ta_, dfree[0],
                            t_lev, prior("lvl"))
                tm_ = tr.do("dve", lambda: dve.tensor_tensor(M, bc(ident[:, :], 1, 4), B, ALU.subtract), tb0, ts_, t)

                yield from turns(2)

                def mturn():
                    for n in range(4):
                        m = pe.transpose(ps[:, Q, n * P:(n + 1) * P], M[:, n, :], ident[:, :])
                    return m
                t = tr.do("pe", mturn, tm_, te)
                tmt = tr.do("act", lambda: act.copy(four(Mt), ps[:, Q, :]), t)
                for l in range(1, 7):
                    tb_ = tr.do("pool", lambda l=l: pool.tensor_tensor(B, AD, bc(lev[:, l], 1, 4), ALU.mult),
                                tb0, tm_ if l == 1 else None)

                    def z():
                        for n in range(4):
                            m = pe.matmul(ps[:, Q, n * P:(n + 1) * P], B[:, n, :], Mt[:, n, :], start=True, stop=True)
                        return m
                    tz = tr.do("pe", z, tb_, tmt)
                    tb0 = tz
                    tzc = tr.do("act", lambda: act.copy(four(Z), ps[:, Q, :]), tz)
                    yield from turns(2)

                    def dm(l=l):
                        for n in range(4):
                            m = pe.matmul(ps[:, Q + 1, n * P:(n + 1) * P], M[:, n, :], Z[:, n, :], start=True, stop=True)
                        if l < 6:
                            for n in range(4):
                                m = pe.matmul(ps[:, Q + 2, n * P:(n + 1) * P], Z[:, n, :], M[:, n, :], start=True, stop=True)
                        return m
                    t = tr.do("pe", dm, tzc, tm_, tqk if l == 1 else None, ta_ if l == 1 else None)
                    tmt = tr.do("dve", lambda: dve.tensor_tensor(four(Mt), four(Mt), ps[:, Q + 1, :], ALU.subtract), t,
                                name="lvl" if l == 6 else None)
                    if l < 6:
                        tm_ = tr.do("dve", lambda: dve.tensor_tensor(four(M), four(M), ps[:, Q + 2, :], ALU.subtract), t)
                    yield from turns(2)
                def u0():
                    for hh in range(2):
                        m = pe.matmul(ps[:, Q, hh * P:(hh + 1) * P], Mt[:, 2 * hh, :], u[:, hh, 0], start=True, stop=True)
                    return m
                t = tr.do("pe", u0, tmt, tu)
                t = tr.do("dve", lambda: dve.tensor_copy(u[:, :, 0], ps[:, Q, 0:S].rearrange("p (h d) -> p h d", h=2)), t)
                yield

                def a10():
                    for hh in range(2):
                        m = pe.matmul(ps[:, Q + 1, hh * P:(hh + 1) * P], TRN[:, hh, 0:P], u[:, hh, 0], start=True, stop=True)
                    return m
                t = tr.do("pe", a10, t, tn_, tmt)
                t = tr.do("dve", lambda: dve.tensor_tensor(
                    u[:, :, 1], u[:, :, 1], ps[:, Q + 1, 0:S].rearrange("p (h d) -> p h d", h=2), ALU.subtract), t)
                yield

                def u1():
                    for hh in range(2):
                        m = pe.matmul(ps[:, Q, hh * P:(hh + 1) * P], Mt[:, 2 * hh + 1, :], u[:, hh, 1], start=True, stop=True)
                    return m
                t = tr.do("pe", u1, t)
                t = tr.do("dve", lambda: dve.tensor_copy(u[:, :, 1], ps[:, Q, 0:S].rearrange("p (h d) -> p h d", h=2)), t,
                          name="uu")
                yield

                def o_():
                    for hh in range(2):
                        for tb in range(TB):
                            for kb in range(tb + 1):
                                m = pe.matmul(ps[:, Q + 2, (hh * TB + tb) * P:(hh * TB + tb + 1) * P],
                                              TRN[:, hh, (1 + tb + kb) * P:(2 + tb + kb) * P], u[:, hh, kb],
                                              start=kb == 0, stop=kb == tb)
                    return m
                t = tr.do("pe", o_, t, tn_, tmt, tm_)
                od = Z
                t = tr.do("dve", lambda: dve.tensor_tensor(od, ps[:, Q + 2, :].rearrange("p (k d) -> p k d", k=4),
                                                           bc(sc[:, 16:20], 2, P), ALU.mult), t, rq, name="od1")
                tsq = tr.do("act", lambda: act.activation(B, od, ACT.Square), t)
                yield
                t = tr.do("dve", lambda: dve.tensor_reduce(sc[:, 24:28], B, AX.X, ALU.add), tsq)
                t = root_inverse(tr, sc[:, 28:32], sc[:, 24:28], 4, EPS, 1.0 / P, t)
                yield
                t = tr.do("dve", lambda: dve.tensor_tensor(od, od, bc(sc[:, 28:32], 2, P), ALU.mult), t)
                t = tr.do("dve", lambda: dve.tensor_tensor(od, od, bc(onorm, 1, 4), ALU.mult), t, t_on)
                c = index(pair) * HALF + W
                yv = lambda: y[:, :, ds(c.v, HALF)].rearrange("p t (h d) -> p t h d", h=2)
                tr.do("dve", lambda: dve.tensor_tensor(yv(), yv(), od.rearrange("p (h t) d -> p t h d", h=2), ALU.mult),
                      t, here, name="fin1")
                yield
            dfree = [None, None, None]

            def recurrences(pair):
                yield from blocks_lru(pair)
                yield from delta_heads(pair)

            tgm = project(w, [(6 * W, 2 * H)], 2, [], rms, tx=tx)
            side = delta_gates()
            next(side)
            base = nstep[0]
            nstep[0] += 3 * HP
            delta_projection(index(0), side, base)
            blocks_projection(index(0), side, base)
            quiet(side)
            with pr.loop(1, HP) as i:
                side = recurrences(i + -1)
                delta_projection(i, side, base)
                blocks_projection(i, side, base)
                quiet(side)
            return last_product("out3", a["od_w_out_2"][0], recurrences(index(HP - 1)),
                                [dl.at(HP - 1, "fin1"), rg_.at(HP - 1, "end")], [dl.at(HP, "fin1"), rg_.at(HP, "end")],
                                [evd.at(HP, "outq"), evd.at(HP, "outv"), evd.at(HP, "gate"), ev.at(HP, "gate"), done3["read"]],
                                1.0, last, pairs=(0, 1, 2, 4, 5, 6, 3, 7))

        t = t_x
        if layers[0] != 0:
            quiet(tables)
            t = [[t_x, t_vec, t_rope]] * 4
        for n in layers:
            t = {0: layer0, 1: layer1, 2: layer2, 3: layer3}[n](t, n == layers[-1])
        fin = pr.track("store")
        stored = [fin.do("sp", lambda q=q: nc.sync.dma_start(
            out[0].rearrange("(t p) d -> p t d", p=P)[:, :, q * N:(q + 1) * N], x[:, :, q * N:(q + 1) * N]),
            t[q], sem=f"out{q}", inc=16) for q in range(4)]
        fin.do("sp", lambda: nc.sync.nop(), stored)
        block = ctx.enter_context(nc.Block())

        @block.tensor
        def _(eng):
            pr.emit("pe", eng)

        @block.scalar
        def _(eng):
            pr.emit("act", eng)

        @block.vector
        def _(eng):
            pr.emit("dve", eng)

        @block.gpsimd
        def _(eng):
            pr.emit("pool", eng)

        @block.sync
        def _(eng):
            pr.emit("sp", eng)


def frequencies():
    return np.concatenate([1.0 / (np.float32(THETA) ** (np.arange(0, n, 2, dtype=np.float32) / np.float32(n)))
                           for n in (128, 64)]).astype(np.float32)


def declare(nc, inputs, layers=(0, 1, 2, 3)):
    arrays = {f"in_{name}": np.ascontiguousarray(v) for name, v in inputs.items()}
    arrays["in_inv_freq"] = frequencies()
    args = {name[3:]: nc.dram_tensor(name, v.shape, mybir.dt.from_np(v.dtype), kind="ExternalInput").ap()
            for name, v in arrays.items()}
    out = nc.dram_tensor("out_x", (1, S, D), F32, kind="ExternalOutput").ap()
    build_program(nc, args, out, layers)
    return arrays


def kernel(**inputs):
    import concourse.bacc as bacc
    from concourse.bass_utils import run_bass_kernel_spmd

    nc = bacc.Bacc("TRN2", target_bir_lowering=False, num_devices=1)
    arrays = declare(nc, inputs)
    r = run_bass_kernel_spmd(nc, [arrays], core_ids=[0])
    return r.results[0]["out_x"]
```
